# Optimizing a Trainium2 kernel written in Bass

```python
import jax, jax.numpy as jnp
from jax import lax
import numpy as np

D_MODEL = 1024
BATCH = 1
SEQ = 512
DEPTH = 2

CONV_WIDTH = D_MODEL // 2
LRU_WIDTH = D_MODEL // 2
LRU_HEADS = 8
LRU_HEAD_DIM = LRU_WIDTH // LRU_HEADS
LRU_C = 8.0
SHORT_CONV_W = 3
REC_CONV_W = 4
IN_AB = 3 * CONV_WIDTH + 2 * LRU_WIDTH
MIX_AB = CONV_WIDTH + LRU_WIDTH
N_HEADS = 16
HEAD_DIM = D_MODEL // N_HEADS
ATTN_WIDTH = N_HEADS * HEAD_DIM
ROT_DIM = HEAD_DIM // 4
ROPE_THETA = 500000.0
DILATED_PATTERNS = ((128, 1), (512, 4), (2048, 16))
QUERY_BLOCK = 64
N_EXPERTS = 16
N_GROUPS = 4
EXPERTS_PER_GROUP = N_EXPERTS // N_GROUPS
TOP_K = 2
EXPERT_FF = D_MODEL // 2
DISPATCH_BLOCK = 128
N_EVEN = (DEPTH + 1) // 2
N_ODD = DEPTH // 2
EPS = 1e-6
NEG_INF = -1e30

kernel_name = "hybrid_conv_lru_dilated_attn_grouped_moe_encoder"

def rmsnorm(x, g):
    xf = x.astype(jnp.float32)
    y = xf * lax.rsqrt(jnp.mean(xf * xf, axis=-1, keepdims=True) + EPS)
    return (y * g.astype(jnp.float32)).astype(x.dtype)

def modulate(h, shift, scale):
    return h * (1 + scale[:, None, :]) + shift[:, None, :]

def depthwise_conv(u, w, left):
    K = w.shape[0]
    S = u.shape[1]
    up = jnp.pad(u, ((0, 0), (left, K - 1 - left), (0, 0)))
    out = up[:, 0:S] * w[0]
    for k in range(1, K):
        out = out + up[:, k:k + S] * w[k]
    return out

def _linear_recurrence_combine(e1, e2):
    a1, b1 = e1
    a2, b2 = e2
    return a1 * a2, a2 * b1 + b2

def rglru(xr, wa, ba, wx, bx, lam, reverse):
    Bz, S, C = xr.shape
    xh = xr.reshape(Bz, S, LRU_HEADS, LRU_HEAD_DIM)
    r = jax.nn.sigmoid(jnp.einsum('bshi,hij->bshj', xh, wa).reshape(Bz, S, C) + ba).astype(jnp.float32)
    i = jax.nn.sigmoid(jnp.einsum('bshi,hij->bshj', xh, wx).reshape(Bz, S, C) + bx).astype(jnp.float32)
    log_a = -LRU_C * r * jax.nn.softplus(-lam.astype(jnp.float32))
    a = jnp.exp(log_a)
    mult = jnp.sqrt(-jnp.expm1(2.0 * log_a))
    b = xr.astype(jnp.float32) * i * mult
    _, h = lax.associative_scan(_linear_recurrence_combine, (a, b), axis=1, reverse=reverse)
    return h

def conv_lru_mixer(h, w_in, conv_a_w, conv_b_w, conv_b_b, lru_wa, lru_ba, lru_wx, lru_bx, lru_lambda, w_out):
    z = h @ w_in
    cw, lw = CONV_WIDTH, LRU_WIDTH
    a_val = z[..., 0:cw]
    a_gb = z[..., cw:2 * cw]
    a_gc = z[..., 2 * cw:3 * cw]
    b_gate = z[..., 3 * cw:3 * cw + lw]
    b_in = z[..., 3 * cw + lw:3 * cw + 2 * lw]
    y_a = a_gb * depthwise_conv(a_gc * a_val, conv_a_w, 1)
    xr = depthwise_conv(b_in, conv_b_w, 1) + conv_b_b
    h_rec = (rglru(xr, lru_wa[0], lru_ba[0], lru_wx[0], lru_bx[0], lru_lambda[0], False)
             + rglru(xr, lru_wa[1], lru_ba[1], lru_wx[1], lru_bx[1], lru_lambda[1], True))
    y_b = jax.nn.gelu(b_gate) * h_rec.astype(h.dtype)
    return jnp.concatenate([y_a, y_b], axis=-1) @ w_out

def partial_rotary(t, positions):
    inv_freq = ROPE_THETA ** (-jnp.arange(0, ROT_DIM, 2, dtype=jnp.float32) / ROT_DIM)
    ang = positions.astype(jnp.float32)[..., None] * inv_freq
    cos = jnp.cos(ang)[:, :, None, :]
    sin = jnp.sin(ang)[:, :, None, :]
    tr = t[..., :ROT_DIM].astype(jnp.float32)
    t1, t2 = tr[..., :ROT_DIM // 2], tr[..., ROT_DIM // 2:]
    rot = jnp.concatenate([t1 * cos - t2 * sin, t2 * cos + t1 * sin], axis=-1)
    return jnp.concatenate([rot.astype(t.dtype), t[..., ROT_DIM:]], axis=-1)

def band_attention(q, k, v, radius):
    Bz, G, L, H, hd = q.shape
    qb = QUERY_BLOCK
    nb = -(-L // qb)
    Lp = nb * qb
    span = qb + 2 * radius
    qp = jnp.pad(q, ((0, 0), (0, 0), (0, Lp - L), (0, 0), (0, 0)))
    kp = jnp.pad(k, ((0, 0), (0, 0), (radius, radius + Lp - L), (0, 0), (0, 0)))
    vp = jnp.pad(v, ((0, 0), (0, 0), (radius, radius + Lp - L), (0, 0), (0, 0)))
    kidx = jnp.arange(nb)[:, None] * qb + jnp.arange(span)[None, :]
    kb = kp[:, :, kidx]
    vb = vp[:, :, kidx]
    qblk = qp.reshape(Bz, G, nb, qb, H, hd)
    qpos = jnp.arange(nb)[:, None] * qb + jnp.arange(qb)[None, :]
    kpos = kidx - radius
    valid = ((jnp.abs(qpos[:, :, None] - kpos[:, None, :]) <= radius)
             & (kpos[:, None, :] >= 0) & (kpos[:, None, :] < L))
    s = jnp.einsum('bgnqhd,bgnkhd->bgnhqk', qblk, kb).astype(jnp.float32) * (hd ** -0.5)
    s = jnp.where(valid[:, None], s, NEG_INF)
    m = jnp.max(s, axis=-1, keepdims=True)
    p = jnp.exp(s - m)
    den = jnp.sum(p, axis=-1, keepdims=True)
    o = jnp.einsum('bgnhqk,bgnkhd->bgnqhd', p, vb.astype(jnp.float32)) / jnp.swapaxes(den, 3, 4)
    lse = jnp.swapaxes((m + jnp.log(den))[..., 0], 3, 4)
    o = o.reshape(Bz, G, Lp, H, hd)[:, :, :L]
    lse = lse.reshape(Bz, G, Lp, H)[:, :, :L]
    return o, lse

def dilated_attention(q, k, v):
    Bz, S, H, hd = q.shape
    outs, lses = [], []
    for (w, d) in DILATED_PATTERNS:
        radius = w // (2 * d)
        def to_sub(t):
            return t.reshape(Bz, S // d, d, H, hd).transpose(0, 2, 1, 3, 4)
        o, lse = band_attention(to_sub(q), to_sub(k), to_sub(v), radius)
        outs.append(o.transpose(0, 2, 1, 3, 4).reshape(Bz, S, H, hd))
        lses.append(lse.transpose(0, 2, 1, 3).reshape(Bz, S, H))
    wts = jax.nn.softmax(jnp.stack(lses, axis=-1), axis=-1)
    return jnp.einsum('bshp,pbshd->bshd', wts, jnp.stack(outs, axis=0))

def dilated_attn_mixer(h, positions, w_qkv, w_o):
    Bz, S, _ = h.shape
    qkv = (h @ w_qkv).reshape(Bz, S, 3, N_HEADS, HEAD_DIM)
    q = partial_rotary(qkv[:, :, 0], positions)
    k = partial_rotary(qkv[:, :, 1], positions)
    v = qkv[:, :, 2]
    o = dilated_attention(q, k, v).astype(h.dtype)
    return o.reshape(Bz, S, ATTN_WIDTH) @ w_o

def grouped_moe(h, router_w, router_bias, w_gate, w_up, w_down):
    Bz, S, D = h.shape
    T = Bz * S
    hf = h.reshape(T, D)
    scores = jax.nn.sigmoid((hf @ router_w).astype(jnp.float32))
    biased = scores + router_bias.astype(jnp.float32)
    grouped = biased.reshape(T, N_GROUPS, EXPERTS_PER_GROUP)
    group_score = jnp.sum(lax.top_k(grouped, 2)[0], axis=-1)
    best_group = jnp.argmax(group_score, axis=-1)
    in_group = (jnp.arange(N_EXPERTS) // EXPERTS_PER_GROUP)[None, :] == best_group[:, None]
    _, top_idx = lax.top_k(jnp.where(in_group, biased, -jnp.inf), TOP_K)
    top_s = jnp.take_along_axis(scores, top_idx, axis=-1)
    top_w = top_s / jnp.sum(top_s, axis=-1, keepdims=True)
    n_assign = T * TOP_K
    e_flat = top_idx.reshape(-1)
    w_flat = top_w.reshape(-1)
    tok_flat = jnp.arange(n_assign, dtype=jnp.int32) // TOP_K
    order = jnp.argsort(e_flat)
    e_sorted = e_flat[order]
    counts = jnp.zeros((N_EXPERTS,), jnp.int32).at[e_flat].add(1)
    padded = ((counts + DISPATCH_BLOCK - 1) // DISPATCH_BLOCK) * DISPATCH_BLOCK
    start = jnp.cumsum(counts) - counts
    pend = jnp.cumsum(padded)
    pstart = pend - padded
    dest = pstart[e_sorted] + (jnp.arange(n_assign, dtype=jnp.int32) - start[e_sorted])
    cap = n_assign + N_EXPERTS * DISPATCH_BLOCK
    n_blocks = cap // DISPATCH_BLOCK
    slot_tok = jnp.full((cap,), T, jnp.int32).at[dest].set(tok_flat[order])
    slot_w = jnp.zeros((cap,), jnp.float32).at[dest].set(w_flat[order])
    block_start = jnp.arange(n_blocks, dtype=jnp.int32) * DISPATCH_BLOCK
    block_expert = jnp.minimum(jnp.searchsorted(pend, block_start, side='right'), N_EXPERTS - 1)
    hpad = jnp.concatenate([hf, jnp.zeros((1, D), hf.dtype)], axis=0)
    xs = hpad[slot_tok].reshape(n_blocks, DISPATCH_BLOCK, D)

    def expert_block(args):
        xb, e = args
        return (jax.nn.silu(xb @ w_gate[e]) * (xb @ w_up[e])) @ w_down[e]

    yb = lax.map(expert_block, (xs, block_expert)).reshape(cap, D)
    out = jnp.zeros((T + 1, D), jnp.float32).at[slot_tok].add(yb.astype(jnp.float32) * slot_w[:, None])
    return out[:T].reshape(Bz, S, D).astype(h.dtype)

def setup_inputs(seed: int = 0) -> dict:
    key = jax.random.key(seed)
    ks = iter(jax.random.split(key, 32))
    nrm = lambda shape, scale: jax.random.normal(next(ks), shape, jnp.float32) * scale
    x = nrm((BATCH, SEQ, D_MODEL), 1.0)
    c = nrm((BATCH, D_MODEL), 1.0)
    offset = jax.random.randint(next(ks), (BATCH, 1), 0, 1024, dtype=jnp.int32)
    positions = (jnp.arange(SEQ, dtype=jnp.int32)[None, :] + offset).astype(jnp.int32)
    mod_w = nrm((DEPTH, D_MODEL, 6 * D_MODEL), 0.5 * D_MODEL ** -0.5)
    mod_b = nrm((DEPTH, 6 * D_MODEL), 0.02)
    norm_mix_g = 1.0 + nrm((DEPTH, D_MODEL), 0.02)
    norm_ffn_g = 1.0 + nrm((DEPTH, D_MODEL), 0.02)
    final_norm_g = 1.0 + nrm((D_MODEL,), 0.02)
    w_in_ab = nrm((N_EVEN, D_MODEL, IN_AB), D_MODEL ** -0.5)
    conv_a_w = nrm((N_EVEN, SHORT_CONV_W, CONV_WIDTH), SHORT_CONV_W ** -0.5)
    conv_b_w = nrm((N_EVEN, REC_CONV_W, LRU_WIDTH), REC_CONV_W ** -0.5)
    conv_b_b = nrm((N_EVEN, LRU_WIDTH), 0.02)
    lru_wa = nrm((N_EVEN, 2, LRU_HEADS, LRU_HEAD_DIM, LRU_HEAD_DIM), LRU_HEAD_DIM ** -0.5)
    lru_ba = nrm((N_EVEN, 2, LRU_WIDTH), 0.02)
    lru_wx = nrm((N_EVEN, 2, LRU_HEADS, LRU_HEAD_DIM, LRU_HEAD_DIM), LRU_HEAD_DIM ** -0.5)
    lru_bx = nrm((N_EVEN, 2, LRU_WIDTH), 0.02)
    u = jax.random.uniform(next(ks), (N_EVEN, 2, LRU_WIDTH), jnp.float32, 0.9, 0.999)
    s_lam = u ** (1.0 / LRU_C)
    lru_lambda = jnp.log(s_lam) - jnp.log1p(-s_lam)
    w_out_ab = nrm((N_EVEN, MIX_AB, D_MODEL), MIX_AB ** -0.5)
    w_qkv = nrm((N_ODD, D_MODEL, 3 * ATTN_WIDTH), D_MODEL ** -0.5)
    w_o = nrm((N_ODD, ATTN_WIDTH, D_MODEL), ATTN_WIDTH ** -0.5)
    router_w = nrm((D_MODEL, N_EXPERTS), D_MODEL ** -0.5)
    router_bias = nrm((N_EXPERTS,), 0.01)
    expert_w_gate = nrm((DEPTH, N_EXPERTS, D_MODEL, EXPERT_FF), D_MODEL ** -0.5)
    expert_w_up = nrm((DEPTH, N_EXPERTS, D_MODEL, EXPERT_FF), D_MODEL ** -0.5)
    expert_w_down = nrm((DEPTH, N_EXPERTS, EXPERT_FF, D_MODEL), EXPERT_FF ** -0.5)
    return {"x": x, "c": c, "positions": positions, "mod_w": mod_w, "mod_b": mod_b,
            "norm_mix_g": norm_mix_g, "norm_ffn_g": norm_ffn_g, "final_norm_g": final_norm_g,
            "w_in_ab": w_in_ab, "conv_a_w": conv_a_w, "conv_b_w": conv_b_w, "conv_b_b": conv_b_b,
            "lru_wa": lru_wa, "lru_ba": lru_ba, "lru_wx": lru_wx, "lru_bx": lru_bx,
            "lru_lambda": lru_lambda, "w_out_ab": w_out_ab, "w_qkv": w_qkv, "w_o": w_o,
            "router_w": router_w, "router_bias": router_bias, "expert_w_gate": expert_w_gate,
            "expert_w_up": expert_w_up, "expert_w_down": expert_w_down}

def reference(x, c, positions, mod_w, mod_b, norm_mix_g, norm_ffn_g, final_norm_g,
              w_in_ab, conv_a_w, conv_b_w, conv_b_b, lru_wa, lru_ba, lru_wx, lru_bx,
              lru_lambda, w_out_ab, w_qkv, w_o, router_w, router_bias,
              expert_w_gate, expert_w_up, expert_w_down):
    cs = jax.nn.silu(c)
    for l in range(DEPTH):
        mod = cs @ mod_w[l] + mod_b[l]
        sh1, sc1, g1, sh2, sc2, g2 = jnp.split(mod, 6, axis=-1)
        h = modulate(rmsnorm(x, norm_mix_g[l]), sh1, sc1)
        if l % 2 == 0:
            j = l // 2
            y = conv_lru_mixer(h, w_in_ab[j], conv_a_w[j], conv_b_w[j], conv_b_b[j], lru_wa[j], lru_ba[j],
                               lru_wx[j], lru_bx[j], lru_lambda[j], w_out_ab[j])
        else:
            j = l // 2
            y = dilated_attn_mixer(h, positions, w_qkv[j], w_o[j])
        x = x + g1[:, None, :] * y
        h = modulate(rmsnorm(x, norm_ffn_g[l]), sh2, sc2)
        x = x + g2[:, None, :] * grouped_moe(h, router_w, router_bias,
                                             expert_w_gate[l], expert_w_up[l], expert_w_down[l])
    return rmsnorm(x, final_norm_g)


_drawn_inputs = setup_inputs


def setup_inputs(seed=0):
    import zlib

    import numpy as np

    out = dict(_drawn_inputs(seed))
    spreads = {}
    factors = {'final_norm_g': 2.895, 'lru_ba': 8.0, 'lru_bx': 4.738}
    for name, (base, spread) in spreads.items():
        noise = np.random.default_rng([zlib.crc32(name.encode()), seed]).standard_normal(out[name].shape)
        drawn = base * np.exp(spread * noise) if base else spread * noise
        out[name] = __import__('jax').numpy.asarray(drawn.astype(out[name].dtype))
    for name, factor in factors.items():
        out[name] = (out[name] * factor).astype(out[name].dtype)
    return out
```

```python
from contextlib import ExitStack

import numpy as np

import concourse.bass as bass
from concourse import mybir

ALU = mybir.AluOpType
ACT = mybir.ActivationFunctionType
AX_X = mybir.AxisListType.X
F32 = mybir.dt.float32
BF16 = mybir.dt.bfloat16
I32 = mybir.dt.int32
U32 = mybir.dt.uint32

P = 128
D = 1024
S = 512
TT = S // P
KT = D // P
HALF = 512
LRU_TILES = 4
HEADS, HD = 16, 64
ROT = 8
NE, NG, EPG = 16, 4, 4
FF = 512
FT = FF // P
MAX_OVER = 2 * S // P - 1
NBLK = NE + MAX_OVER
RING = 6
MOD_RING = 4
MOD_QUARTERS = 8
LAYERS = 2
PARTS = 6
EPS = 1e-6
NEG = -1.0e30
NO_TOKEN = 1 << 20
ROPE_THETA = 500000.0
MAGIC = 12582912.0
LSPAN = (TT - 1) * P + S


class Link:

    def __init__(self, eng, sem):
        self.eng, self.sem, self.n, self.turn, self.per = eng, sem, 0, None, 0

    def __call__(self, ins):
        self.n += 1
        ins.then_inc(self.sem, 1)
        value = self.n if self.turn is None else self.turn * self.per + self.n
        self.eng.wait_ge(self.sem, value)

    def enter_loop(self, turn, first, per):
        self.turn, self.per, self.entry = turn, per, self.n
        self.n -= first * per

    def leave_loop(self, first, end):
        assert self.n + first * self.per == self.entry + self.per, (self.n + first * self.per - self.entry, self.per)
        self.turn = None
        self.n = self.entry + (end - first) * self.per


def part_of(n):
    return n // PARTS, n % PARTS


def trunk(nc, a, out):
    with ExitStack() as ctx:
        build(nc, ctx, a, out)


def build(nc, ctx, a, out):
    def small(name, shape, dt=F32):
        return ctx.enter_context(nc.sbuf_tensor(name, shape, dt))

    sems = {}

    def sem(name):
        sems[name] = ctx.enter_context(nc.semaphore(name))
        return sems[name]

    UNIT = 512
    X = small("x_res", [P, TT, D])
    ring = small("slab_ring", [P, RING, KT, HALF])
    modr = small("mod_ring", [P, 8, UNIT])
    G = small("gate_rows", [P, 4, D])
    LC = small("log_count", [P, LSPAN])
    HT = small("h_t", [P, KT, S])
    XN = small("x_norm", [P, TT, D])
    R = small("scratch", [P, 16, UNIT])

    ps = ctx.enter_context(nc.psum_tensor("ps", [P, 8, HALF], F32))

    mod_slot = [modr[:, 2 * i:2 * i + 2, :] for i in range(MOD_RING)]
    u_in = R[:, 0, :]
    xr = [R[:, 1 + j, :] for j in range(LRU_TILES)]
    th = [R[:, 5, :], R[:, 8, :]]
    ti = [R[:, 6, :], R[:, 9, :]]
    av = [R[:, 7, :], R[:, 10, :]]
    tmp0 = R[:, 11, :]
    acc = [R[:, 12:14, :].rearrange("p a n -> p (a n)"), R[:, 14:16, :].rearrange("p a n -> p (a n)")]
    mixT = XN[:, :, :].rearrange("p t (h n) -> p (t h) n", h=2)
    BD = G[:, 2:4, :].rearrange("p g (x o) -> p (g x) o", o=P)
    mflt = R[:, 11, :].rearrange("p (i n) -> p i n", n=P)
    mlow = R[:, 10, 0:P].bitcast(I32)
    xs = [R[:, 0:2, :].rearrange("p a n -> p (a n)"), R[:, 2:4, :].rearrange("p a n -> p (a n)")]
    xsT = R[:, 4:6, :].rearrange("p a (b n) -> p (a b) n", n=P)
    sg = R[:, 6, :]
    hid = R[:, 7, :]
    hidT = R[:, 8, :].rearrange("p (f n) -> p f n", n=P)
    ybuf = [R[:, 9:11, :].rearrange("p a n -> p (a n)"), R[:, 11:13, :].rearrange("p a n -> p (a n)")]
    rt = R[:, 13:16, :].rearrange("p a n -> p (a n)")
    comb = [[XN[:, t, :] for t in range(TT)],
            [HT[:, 2 * t:2 * t + 2, :].rearrange("p a n -> p (a n)") for t in range(TT)]]
    Q = R[:, 0:8, :].rearrange("p (t h) n -> p t (h n)", h=2)
    O = Q
    QT = R[:, 8:16, :]
    K = modr[:, :, :].rearrange("p (t h) n -> p t (h n)", h=2)
    KTR = HT
    V = XN
    OT = HT
    prob = [modr[:, i, :] for i in range(4)]
    rots = [G[:, i // 2, (i % 2) * HALF:(i % 2) * HALF + HALF] for i in range(4)]
    probT = rots

    ident = small("ident", [P, P])
    ones = small("ones", [P, P])
    before = small("before", [P, P], BF16)
    ones_b = small("ones_b", [P, P], BF16)
    rows = small("param_rows", [56, P])
    cols = small("param_cols", [P, 56])
    cT = small("c_t", [P, KT])
    cs = small("c_silu", [P, KT])
    gcols = small("norm_gains", [P, LAYERS, 2, KT])
    mbc = small("mod_b_cols", [P, LAYERS * PARTS, KT])
    AB = small("mod_ab", [P, LAYERS * 2, 2, KT])
    rw = small("router_w", [P, KT, NE])
    rb = small("router_b", [P, NE])
    lru = small("lru_consts", [P, 6, 8])
    hbias = small("half_bias", [P, 16])
    dec = small("decay", [P, 2, 8])
    stats = small("stats", [P, 4, TT])
    posi = small("pos_i", [P, TT], I32)
    posf = small("pos_f", [P, TT])
    invf = small("inv_freq", [P, ROT])
    rope = small("rope", [P, 6, TT * ROT])
    mx = small("row_max", [P, 64])
    nmx = small("neg_max", [P, 64])
    ssum = small("row_sum", [P, 64])
    rsum = small("row_rcp", [P, 64])
    e_id = small("expert_id", [P, NE])
    g_id = small("group_id", [P, NE])
    em15 = small("over_base", [P, NE])
    k_id = small("over_id", [P, MAX_OVER])
    tok = small("token_id", [P, TT], I32)
    empty = small("no_token", [P, NBLK], I32)
    slot_tok = small("slot_token", [P, NBLK], I32)
    gpad = small("group_pad", [P, TT, 8])
    mx8 = small("max8", [P, TT, 8])
    ix8 = small("index8", [P, TT, 8], U32)
    comb_w = small("combine_w", [P, 2, TT])
    yrow = small("y_row", [P, 2, TT], I32)
    trow = small("table_row", [P, 2, TT], I32)
    ytmp = small("y_tmp", [P, 2, 8], I32)
    dst = small("dest", [P, 2, TT])
    info = small("over_info", [P, 8], I32)
    hot = small("hot_b", [P, TT, NE], BF16)
    idx = [small(f"gather_idx{i}", [P, 1], I32) for i in range(2)]

    xn_dram = nc.dram_tensor("xn_rows", [S, D], F32, kind="Internal").ap()
    y_dram = nc.dram_tensor("y_rows", [NBLK * P, D], F32, kind="Internal").ap()
    tables = [nc.dram_tensor(f"slot_table{l}", [P * NBLK, 1], I32, kind="Internal").ap() for l in range(LAYERS)]

    x_loaded = sem("x_loaded")
    params_loaded = sem("params_loaded")
    bd_loaded = sem("bd_loaded")
    g_bias_loaded = [sem(f"g_bias_loaded{i}") for i in range(4)]
    slab_filled = [sem(f"slab_filled{i}") for i in range(RING)]
    mod_filled = [sem(f"mod_filled{i}") for i in range(MOD_RING)]
    mod_used = sem("mod_used")
    dve_step, act_step, pool_step = sem("dve_step"), sem("act_step"), sem("pool_step")
    consts_ready = sem("consts_ready")
    bd_zeroed = sem("bd_zeroed")
    mask_base = sem("mask_base")
    mask_ready = sem("mask_ready")
    cs_ready = sem("cs_ready")
    cols_turned = sem("cols_turned")
    cols_ready = sem("cols_ready")
    lam_abs, lam_exp = sem("lam_abs"), sem("lam_exp")
    angle_ready, rope_ready = sem("angle_ready"), sem("rope_ready")
    dec_ready = sem("dec_ready")
    x_ready = sem("x_ready")
    ssq_ready, ms_ready, rms_ready = sem("ssq_ready"), sem("ms_ready"), sem("rms_ready")
    xn_ready = sem("xn_ready")
    xn_turned = sem("xn_turned")
    ht_act, ht_dve = sem("ht_act"), sem("ht_dve")
    acc_ready, mod_reduced, mod_done = sem("acc_ready"), sem("mod_reduced"), sem("mod_done")
    z_ready, z_act, z_dve = sem("z_ready"), sem("z_act"), sem("z_dve")
    xr_ready, gate_ready, gate_read = sem("xr_ready"), sem("gate_ready"), sem("gate_read")
    m_ready, mult_ready, scan_done = sem("m_ready"), sem("mult_ready"), sem("scan_done")
    mix_ready = sem("mix_ready")
    y_ready = sem("y_ready")
    logit_ready, score_ready = sem("logit_ready"), sem("score_ready")
    hot_ready, rank_ready, route_ready = sem("hot_ready"), sem("rank_ready"), sem("route_ready")
    xn_stored, table_filled, table_set, table_back = sem("xn_stored"), sem("table_filled"), sem("table_set"), sem("table_back")
    xs_filled = [sem("xs_filled0"), sem("xs_filled1")]
    xs_turned, xst_act, xst_dve = sem("xs_turned"), sem("xst_act"), sem("xst_dve")
    gate_done, up_done, silu_done = sem("gate_done"), sem("up_done"), sem("silu_done")
    hid_ready, hid_turned, hidt_ready = sem("hid_ready"), sem("hid_turned"), sem("hidt_ready")
    down_done, yb_ready = sem("down_done"), sem("yb_ready")
    yb_stored = [sem("yb_stored0"), sem("yb_stored1")]
    over_done = sem("over_done")
    turn_seen = sem("turn_seen")
    y_zeroed = sem("y_zeroed")
    comb_filled = [sem(f"comb_filled{t}") for t in range(TT)]
    over = [{n: sem(f"over{l}_{n}") for n in ("wg", "wu", "wd", "xs", "turned", "xst", "gu", "silu", "hid", "hidt_in", "hidt", "down", "yb", "stored", "step", "over", "seen")}
            for l in range(LAYERS)]
    qkv_ready, qkv_act, qkv_dve = sem("qkv_ready"), sem("qkv_act"), sem("qkv_dve")
    rot_ready, qt_turned, kt_turned, qt_ready, kt_ready = (sem(n) for n in ("rot_ready", "qt_turned", "kt_turned", "qt_ready", "kt_ready"))
    s_ready, max_ready, p_ready, p_turned = sem("s_ready"), sem("max_ready"), sem("p_ready"), sem("p_turned")
    pt_act, pt_dve, av_ready, o_ready = sem("pt_act"), sem("pt_dve"), sem("av_ready"), sem("o_ready")
    o_turned, ot_act, ot_dve = sem("o_turned"), sem("ot_act"), sem("ot_dve")
    fg_loaded = sem("fg_loaded")
    final_ready, out_stored = sem("final_ready"), sem("out_stored")

    N_IN, N_OUT, N_EXP0 = 0, 5, 7
    N_QKV = N_EXP0 + 3 * NE
    N_WO = N_QKV + 6
    N_EXP1 = N_WO + 2
    exp_base = [N_EXP0, N_EXP1]
    IN_ORDER = [4, 3, 2, 0, 1]

    def slab(n):
        return ring[:, n % RING, :, :]

    def wait_slab(eng, n, turn=None, first=0):
        if turn is None:
            eng.wait_ge(slab_filled[n % RING], 16 * (n // RING + 1))
        else:
            eng.wait_ge(slab_filled[n % RING], turn * 16 + 16 * (n // RING + 1))

    def pk(w):
        return w.rearrange("(p k) n -> p k n", p=P)

    def kp(w):
        return w.rearrange("(k p) n -> p k n", p=P)

    w_in, w_out = pk(a["w_in_ab"][0]), kp(a["w_out_ab"][0])
    w_qkv, w_o = pk(a["w_qkv"][0]), kp(a["w_o"][0])

    N_PARAMS = 15
    block = ctx.enter_context(nc.Block())

    @block.sync
    def _(sp):
        def load_slab(n, src):
            sp.dma_start(slab(n), src).then_inc(slab_filled[n % RING], 16)

        def load_mod(n, quarters=range(MOD_QUARTERS)):
            l, q = part_of(n)
            for m in quarters:
                half, kt = m // 4, 2 * (m % 4)
                g = n * MOD_QUARTERS + m
                if g >= MOD_RING:
                    sp.wait_ge(mod_used, g - MOD_RING + 1)
                src = pk(a["mod_w"][l])[:, kt:kt + 2, q * D + half * HALF:q * D + half * HALF + HALF]
                sp.dma_start(mod_slot[g % MOD_RING], src).then_inc(mod_filled[g % MOD_RING], 16)

        def load_expert_part(l, e, c, slot_n):
            if c < 2:
                src = a[("expert_w_gate", "expert_w_up")[c]][l, bass.ds(e, 1)].rearrange("e (p k) n -> p (e k) n", p=P)
                dst_ap = slab(slot_n)
            else:
                src = a["expert_w_down"][l, bass.ds(e, 1)].rearrange("e (k p) n -> p (e k) n", p=P)
                dst_ap = slab(slot_n).rearrange("p (f h) n -> p f (h n)", h=2)
            sp.dma_start(dst_ap, src).then_inc(slab_filled[slot_n % RING], 16)

        sp.dma_start(X[:, :, :], a["x"][0].rearrange("(t p) d -> p t d", p=P)).then_inc(x_loaded, 16)
        load_mod(0)
        load_mod(1)
        for n in range(5):
            load_slab(N_IN + n, w_in[:, :, IN_ORDER[n] * HALF:IN_ORDER[n] * HALF + HALF])
        load_slab(N_OUT, w_out[:, :, 0:HALF])
        g_slot = {2: 0, 5: 1, 8: 2, 11: 3}
        for n in range(2, LAYERS * PARTS):
            if n in g_slot:
                if n == 8:
                    sp.wait_ge(gate_read, LRU_TILES)
                l, q = part_of(n)
                sp.dma_start(G[:, g_slot[n], :], a["mod_b"][l, q * D:(q + 1) * D].unsqueeze(0).to_broadcast([P, D])).then_inc(g_bias_loaded[g_slot[n]], 16)
            load_mod(n)
            if n == 6:
                sp.wait_ge(z_ready, 4)
                load_slab(N_OUT + 1, w_out[:, :, HALF:D])

        def stream_experts(l):
            base = exp_base[l]
            e0 = l * NE

            free = [(z_ready, 8), (z_ready, 12), (z_ready, 16), (z_ready, 20), (y_ready, 4), (y_ready, 8)] if l == 0 else \
                   [(qkv_ready, 12), (qkv_ready, 16), (qkv_ready, 20), (qkv_ready, 24), (y_ready, 12), (y_ready, 16)]
            for e in range(2):
                for c in range(3):
                    sp.wait_ge(*free[3 * e + c])
                    load_expert_part(l, e, c, base + 3 * e + c)

            def step(pair, par, turn):
                e = 2 * pair + par
                for c, used in enumerate((gate_done, up_done, down_done)):
                    sp.wait_ge(used, e + (e0 + 1))
                    if turn is not None or e + 2 < NE:
                        load_expert_part(l, e + 2, c, base + 3 * par + c)
                    elif l == 0:
                        load_slab(N_QKV + 3 * par + c, w_qkv[:, :, (3 * par + c) * HALF:(3 * par + c + 1) * HALF])
                sp.wait_ge(yb_ready, e + (e0 + 1))
                row = e * P
                sp.dma_start(y_dram[bass.ds(row, P), :], ybuf[par]).then_inc(yb_stored[par], 16)

            with sp.Fori(0, NE // 2 - 1) as i:
                step(i, 0, i)
                step(i, 1, i)
            for par in range(2):
                step(NE // 2 - 1, par, None)

            o = over[l]
            wbuf = [HT[:, :, :], XN[:, :, :].rearrange("p t (h n) -> p (t h) n", h=2)]
            sp.wait_ge(route_ready, l + 1)
            sp.wait_ge(xn_stored, 16 * (l + 1))
            n_over = sp.value_load(info[0:1, 7:8], min_val=0, max_val=MAX_OVER)
            with sp.Fori(0, MAX_OVER) as k:
                with sp.If(k < n_over):
                    ex = sp.value_load(info[0:1, bass.ds(k, 1)], min_val=0, max_val=NE - 1)
                    for c, name in ((0, "wg"), (1, "wu")):
                        src = a[("expert_w_gate", "expert_w_up")[c]][l, bass.ds(ex, 1)].rearrange("e (p k) n -> p (e k) n", p=P)
                        sp.dma_start(wbuf[c], src).then_inc(o[name], 16)
                    sp.wait_ge(o["gu"], k + 1)
                    src = a["expert_w_down"][l, bass.ds(ex, 1)].rearrange("e (k p) n -> p (e k) n", p=P)
                    sp.dma_start(wbuf[0].rearrange("p (f h) n -> p f (h n)", h=2), src).then_inc(o["wd"], 16)
                    sp.wait_ge(o["yb"], k + 1)
                    sp.dma_start(y_dram[bass.ds((k + NE) * P, P), :], ybuf[0]).then_inc(o["stored"], 16)
                    sp.wait_ge(o["stored"], (k + 1) * 16)
                    sp.sem_inc(o["over"], 1)
            for par in range(2):
                sp.wait_ge(yb_stored[par], 16 * (NE // 2) * (l + 1))
            sp.sem_inc(over_done, 1)

        stream_experts(0)
        sp.wait_ge(qkv_ready, 4)
        load_slab(N_WO, w_o[:, :, 0:HALF])
        sp.wait_ge(qkv_ready, 8)
        load_slab(N_WO + 1, w_o[:, :, HALF:D])
        stream_experts(1)
        for t in range(TT):
            sp.wait_ge(final_ready, t + 1)
            sp.dma_start(out[0, t * P:(t + 1) * P, :], XN[:, t, :]).then_inc(out_stored, 16)
        sp.wait_ge(out_stored, 16 * TT)

    @block.gpsimd
    def _(gp):
        link = Link(gp, pool_step)
        link(gp.memset(ident[:, :], 0.0))
        link(gp.affine_select(out=ident[:, :], in_=ident[:, :], compare_op=ALU.not_equal, fill=1.0, base=0, pattern=[[-1, P]], channel_multiplier=1))
        link(gp.memset(ones[:, :], 1.0))
        link(gp.memset(BD, 0.0))
        gp.sem_inc(bd_zeroed, 1)
        link(gp.memset(ones_b[:, :], 1.0))
        link(gp.affine_select(out=before[:, :], in_=ones_b[:, :], compare_op=ALU.is_gt, fill=0.0, base=0, pattern=[[1, P]], channel_multiplier=-1))
        for i in range(ROT):
            f = float(np.float32(ROPE_THETA) ** np.float32(-2.0 * i / (2 * ROT)))
            link(gp.memset(invf[:, i:i + 1], f))
        link(gp.iota(mlow, [[1, P]], base=P, channel_multiplier=-1))
        link(gp.iota(e_id[:, :], [[1, NE]], base=0, channel_multiplier=0, allow_small_or_imprecise_dtypes=True))
        link(gp.iota(g_id[:, :], [[1, NG], [0, EPG]], base=0, channel_multiplier=0, allow_small_or_imprecise_dtypes=True))
        link(gp.iota(em15[:, :], [[-1, NE]], base=NE - 1, channel_multiplier=0, allow_small_or_imprecise_dtypes=True))
        link(gp.iota(k_id[:, :], [[1, MAX_OVER]], base=0, channel_multiplier=0, allow_small_or_imprecise_dtypes=True))
        link(gp.iota(tok[:, :], [[P, TT]], base=0, channel_multiplier=1))
        link(gp.iota(empty[:, :], [[0, NBLK]], base=NO_TOKEN, channel_multiplier=0))
        link(gp.memset(gpad[:, :, :], NEG))
        gp.sem_inc(consts_ready, 1)
        for l in range(LAYERS):
            gp.dma_start(tables[l].rearrange("(p b) o -> p (b o)", p=P), empty[:, :]).then_inc(table_filled, 16)

        gp.wait_ge(mask_base, 1)
        rep = LSPAN // P
        wide = lambda i: mflt[:, i, :].unsqueeze(1).to_broadcast([P, rep, P])
        part = R[:, 8:10, :].rearrange("p a n -> p (a n)")[:, 0:LSPAN]
        lcv = LC[:, :].rearrange("p (r n) -> p r n", n=P)
        link(gp.tensor_copy(lcv, wide(0)))
        for i, radius in ((1, 256), (2, 64)):
            link(gp.tensor_copy(part.rearrange("p (r n) -> p r n", n=P), wide(i)))
            link(gp.affine_select(out=part, in_=part, compare_op=ALU.is_ge, fill=0.0, base=radius + (TT - 1) * P, pattern=[[-1, LSPAN]], channel_multiplier=1))
            link(gp.affine_select(out=part, in_=part, compare_op=ALU.is_ge, fill=0.0, base=radius - (TT - 1) * P, pattern=[[1, LSPAN]], channel_multiplier=-1))
            link(gp.tensor_tensor(LC[:, :], LC[:, :], part, ALU.add))
        gp.sem_inc(mask_ready, 1)

        zeros = R[:, 8:10, :].rearrange("p a n -> p (a n)")
        gp.wait_ge(scan_done, LRU_TILES)
        link(gp.memset(zeros, 0.0))
        gp.wait_ge(y_ready, 1)
        for b in range(NE, NBLK):
            gp.dma_start(y_dram[b * P:(b + 1) * P, :], zeros).then_inc(y_zeroed, 16)
        gp.wait_ge(y_zeroed, 16 * MAX_OVER)

        def gathers(l):
            e0 = l * NE
            gp.wait_ge(xn_ready, 4 * (2 * l + 2))
            link(gp.memset(R[:, 0:4, :], 0.0))
            gp.wait_ge(route_ready, l + 1)
            gp.wait_ge(table_filled, 16 * LAYERS)
            for j in range(2):
                for t in range(TT):
                    gp.indirect_dma_start(out=tables[l], out_offset=bass.IndirectOffsetOnAxis(ap=trow[:, j, t:t + 1], axis=0),
                                          in_=tok[:, t:t + 1], in_offset=None, bounds_check=P * NBLK - 1,
                                          oob_is_err=False).then_inc(table_set, 16)
            gp.wait_ge(table_back, 16 * (l + 1))
            gp.wait_ge(xn_stored, 16 * (l + 1))

            def gather(col, buf, done):
                link(gp.tensor_copy(idx[buf][:, :], slot_tok[:, bass.ds(col, 1)]))
                gp.sem_inc(turn_seen, 1)
                gp.indirect_dma_start(out=xs[buf], out_offset=None, in_=xn_dram,
                                      in_offset=bass.IndirectOffsetOnAxis(ap=idx[buf][:, 0:1], axis=0),
                                      bounds_check=S - 1, oob_is_err=False).then_inc(done, 16)

            gather(0, 0, xs_filled[0])
            gather(1, 1, xs_filled[1])
            with gp.Fori(0, NE // 2 - 1) as i:
                link.enter_loop(i, 0, 2)
                for par in range(2):
                    gp.wait_ge(xs_turned, 2 * i + (par + e0 + 1))
                    gp.sem_inc(turn_seen, 1)
                    gather(2 * i + (par + 2), par, xs_filled[par])
                link.leave_loop(0, NE // 2 - 1)

            o = over[l]
            n_over = gp.value_load(info[0:1, 7:8], min_val=0, max_val=MAX_OVER)
            gp.wait_ge(xs_turned, e0 + NE)
            with gp.Fori(0, MAX_OVER) as k:
                with gp.If(k < n_over):
                    gp.wait_ge(o["wg"], (k + 1) * 16)
                    gp.sem_inc(o["seen"], 1)
                    gp.tensor_copy(idx[0][:, :], slot_tok[:, bass.ds(k + NE, 1)]).then_inc(o["step"], 1)
                    gp.wait_ge(o["step"], k + 1)
                    gp.sem_inc(o["seen"], 1)
                    gp.indirect_dma_start(out=xs[0], out_offset=None, in_=xn_dram,
                                          in_offset=bass.IndirectOffsetOnAxis(ap=idx[0][:, 0:1], axis=0),
                                          bounds_check=S - 1, oob_is_err=False).then_inc(o["xs"], 16)
            gp.wait_ge(over_done, l + 1)
            for t in range(TT):
                for j in range(2):
                    gp.indirect_dma_start(out=comb[j][t], out_offset=None, in_=y_dram,
                                          in_offset=bass.IndirectOffsetOnAxis(ap=yrow[:, j, t:t + 1], axis=0),
                                          bounds_check=NBLK * P - 1, oob_is_err=False).then_inc(comb_filled[t], 16)

        gathers(0)
        gathers(1)

    @block.scalar
    def _(act):
        link = Link(act, act_step)
        def load(dst_ap, src):
            act.dma_start(dst_ap, src).then_inc(params_loaded, 16)

        with nc.allow_non_contiguous_dma(reason="512 positions, once"):
            load(cT[:, :], a["c"][0].rearrange("(p k) -> p k", k=KT))
            load(mbc[:, :, :], a["mod_b"].rearrange("l (q p k) -> p (l q) k", p=P, k=KT))
            load(gcols[:, :, 0, :], a["norm_mix_g"].rearrange("l (p k) -> p l k", k=KT))
            load(gcols[:, :, 1, :], a["norm_ffn_g"].rearrange("l (p k) -> p l k", k=KT))
            load(rows[0:12, :], a["conv_a_w"][0].rearrange("k (j n) -> (k j) n", n=P))
            load(rows[12:28, :], a["conv_b_w"][0].rearrange("k (j n) -> (k j) n", n=P))
            load(rows[28:32, :], a["conv_b_b"][0].rearrange("(j n) -> j n", n=P))
            load(rows[32:40, :], a["lru_ba"][0].rearrange("d (j n) -> (d j) n", n=P))
            load(rows[40:48, :], a["lru_bx"][0].rearrange("d (j n) -> (d j) n", n=P))
            load(rows[48:56, :], a["lru_lambda"][0].rearrange("d (j n) -> (d j) n", n=P))
            load(posi[:, :], a["positions"][0].rearrange("(t p) -> p t", p=P))
            load(rw[:, :, :], a["router_w"].rearrange("(p k) e -> p k e", k=KT))
            load(rb[:, :], a["router_bias"].unsqueeze(0).to_broadcast([P, NE]))
            act.wait_ge(bd_zeroed, 1)
            for d in range(2):
                for w, name in enumerate(("lru_wa", "lru_wx")):
                    src = a[name][0, d].rearrange("(j two) i o -> two i j o", two=2)
                    b0 = (d * 2 + w) * LRU_TILES
                    for two in range(2):
                        act.dma_start(BD[two * 64:(two + 1) * 64, b0:b0 + LRU_TILES, two * 64:(two + 1) * 64], src[two]).then_inc(bd_loaded, 16)
        act.wait_ge(params_loaded, 16 * 13)
        act.activation(cs[:, :], cT[:, :], ACT.Silu).then_inc(cs_ready, 1)
        act.wait_ge(angle_ready, 1)
        act.activation(rope[:, 4, :], rope[:, 2, :], ACT.Sin).then_inc(rope_ready, 1)
        act.activation(rope[:, 5, :], rope[:, 3, :], ACT.Sin).then_inc(rope_ready, 1)

        def norm(s):
            if s == 0:
                act.wait_ge(x_loaded, 16)
            else:
                act.wait_ge(x_ready, s)
            for t in (2, 3):
                act.activation(XN[:, t, :], X[:, t, :], ACT.Square, accum_out=stats[:, 0, t:t + 1]).then_inc(ssq_ready, 1)
            act.wait_ge(ms_ready, s + 1)
            act.activation(stats[:, 2, :], stats[:, 1, :], ACT.Sqrt).then_inc(rms_ready, 1)
            if s == 4:
                return
            for kt in range(0, KT, 2):
                act.wait_ge(xn_turned, KT * s + kt + 1)
                if kt == 0:
                    act.wait_ge(xn_ready, 4 * (s + 1))
                act.activation(HT[:, kt, :], ps[:, kt, :], ACT.Identity, bias=AB[:, s, 1, kt:kt + 1], scale=AB[:, s, 0, kt:kt + 1]).then_inc(ht_act, 1)

        norm(0)
        act.wait_ge(lam_abs, 1)
        act.activation(lru[:, 1, :], lru[:, 0, :], ACT.Exp, scale=-1.0).then_inc(lam_exp, 1)
        for j in range(LRU_TILES):
            act.wait_ge(z_ready, j + 1)
            if j:
                act.wait_ge(xr_ready, j)
            act.activation(u_in, ps[:, j, :], ACT.Copy).then_inc(z_act, 1)
        act.wait_ge(mask_ready, 1)
        act.wait_ge(dec_ready, 1)
        for j in range(LRU_TILES):
            act.wait_ge(z_ready, LRU_TILES + j + 1)
            act.activation(mixT[:, LRU_TILES + j, :], ps[:, 4 + j % 2, :], ACT.Gelu_apprx_tanh).then_inc(z_act, 1)
            act.wait_ge(gate_ready, j + 1)
            if j:
                act.wait_ge(scan_done, j)
            for d in range(2):
                c = d * LRU_TILES + j
                link(act.activation(th[d], ps[:, 2 * d, :], ACT.Tanh, bias=hbias[:, c:c + 1], scale=0.5))
                link(act.activation(ti[d], ps[:, 2 * d + 1, :], ACT.Tanh, bias=hbias[:, 8 + c:9 + c], scale=0.5))
                if d == 1:
                    act.sem_inc(gate_read, 1)
                link(act.activation(av[d], th[d], ACT.Exp, bias=dec[:, 0, c:c + 1], scale=dec[:, 0, c:c + 1]))
                act.activation(th[d], th[d], ACT.Tanh, bias=dec[:, 1, c:c + 1], scale=dec[:, 1, c:c + 1]).then_inc(m_ready, 1)
            for d in range(2):
                act.wait_ge(mult_ready, 4 * j + d + 1)
                act.activation(th[d], th[d], ACT.Sqrt, scale=0.25).then_inc(m_ready, 1)
        for j in range(LRU_TILES):
            t = 2 * LRU_TILES + j
            act.wait_ge(z_ready, t + 1)
            act.activation(mixT[:, j, :], ps[:, (4, 5, 0, 1, 2, 3)[(t - 8) % 6], :], ACT.Copy).then_inc(z_act, 1)

        def experts(l):
            s = 2 * l + 1
            norm(s)
            e0 = l * NE
            act.wait_ge(logit_ready, l + 1)
            act.activation(rt[:, 0:TT * NE], ps[:, 0, 0:TT * NE], ACT.Sigmoid).then_inc(score_ready, 1)
            act.dma_start(xn_dram.rearrange("(t p) d -> p t d", p=P), XN[:, :, :]).then_inc(xn_stored, 16)
            if l == 1:
                act.dma_start(G[:, 0, :], a["final_norm_g"].unsqueeze(0).to_broadcast([P, D])).then_inc(fg_loaded, 16)
            act.wait_ge(table_set, 16 * 8 * (l + 1))
            act.dma_start(slot_tok[:, :], tables[l].rearrange("(p b) o -> p (b o)", p=P)).then_inc(table_back, 16)

            def xst(n):
                act.wait_ge(xs_turned, n)
                for kt in range(4):
                    ins = act.activation(xsT[:, kt, :], ps[:, 0, kt * P:(kt + 1) * P], ACT.Identity, bias=AB[:, s, 1, kt:kt + 1], scale=AB[:, s, 0, kt:kt + 1])
                ins.then_inc(xst_act, 1)

            def step(e, first, last):
                act.wait_ge(gate_done, e + (e0 + 1))
                if not first:
                    act.wait_ge(hid_ready, e + e0)
                act.activation(sg, ps[:, 2, :], ACT.Silu).then_inc(silu_done, 1)
                if not last:
                    xst(e + (e0 + 2))
                act.wait_ge(hid_turned, e + (e0 + 1))
                if not first:
                    act.wait_ge(down_done, e + e0)
                act.activation(hidT, ps[:, 4, :].rearrange("p (f n) -> p f n", n=P), ACT.Copy).then_inc(hidt_ready, 1)

            xst(e0 + 1)
            for par in range(2):
                step(par, par == 0, False)
            with act.Fori(1, NE // 2 - 1) as i:
                for par in range(2):
                    step(2 * i + par, False, False)
            for par in range(2):
                step(NE - 2 + par, False, par == 1)

            o = over[l]
            act.wait_ge(route_ready, l + 1)
            n_over = act.value_load(info[0:1, 7:8], min_val=0, max_val=MAX_OVER)
            with act.Fori(0, MAX_OVER) as k:
                with act.If(k < n_over):
                    act.wait_ge(o["turned"], k + 1)
                    for kt in range(4):
                        ins = act.activation(xsT[:, kt, :], ps[:, 0, kt * P:(kt + 1) * P], ACT.Identity, bias=AB[:, s, 1, kt:kt + 1], scale=AB[:, s, 0, kt:kt + 1])
                    ins.then_inc(o["xst"], 1)
                    act.wait_ge(o["gu"], k + 1)
                    act.activation(sg, ps[:, 2, :], ACT.Silu).then_inc(o["silu"], 1)
                    act.wait_ge(o["hidt_in"], k + 1)
                    act.activation(hidT, ps[:, 4, :].rearrange("p (f n) -> p f n", n=P), ACT.Copy).then_inc(o["hidt"], 1)

        experts(0)
        norm(2)
        for w in range(6):
            dest = (Q, K, V)[w // 2]
            for t in (0, 2):
                act.wait_ge(qkv_ready, 4 * w + t + 1)
                act.activation(dest[:, t, (w % 2) * HALF:(w % 2) * HALF + HALF], ps[:, 4 * (w % 2) + t, :], ACT.Copy).then_inc(qkv_act, 1)
        for hp in range(8):
            act.wait_ge(qt_turned, hp + 1)
            act.activation(QT[:, hp, :], ps[:, (2 * hp) % 8, :], ACT.Copy).then_inc(qt_ready, 1)

        def exp_step(v):
            act.wait_ge(max_ready, v + 1)
            act.activation(prob[v % 4], prob[v % 4], ACT.Exp, bias=nmx[:, v:v + 1], accum_out=ssum[:, v:v + 1]).then_inc(p_ready, 1)

        exp_step(0)
        exp_step(1)
        for u in range(64):
            if u + 2 < 64:
                exp_step(u + 2)
            if u % 2 == 0:
                act.wait_ge(p_turned, u + 1)
                if u >= 4:
                    act.wait_ge(av_ready, u - 3)
                act.activation(probT[u % 4], ps[:, 3 + u % 2, :], ACT.Copy).then_inc(pt_act, 1)
        for kt in range(0, KT, 2):
            act.wait_ge(o_turned, kt + 1)
            act.activation(OT[:, kt, :], ps[:, kt, :], ACT.Copy).then_inc(ot_act, 1)
        experts(1)
        norm(4)

    @block.vector
    def _(v):
        link = Link(v, dve_step)
        ts, tt_, stt = v.tensor_scalar, v.tensor_tensor, v.scalar_tensor_tensor

        v.wait_ge(consts_ready, 1)
        mi = mlow
        mtmp = mflt[:, 3, :].bitcast(I32)
        m16, m4 = mflt[:, 0, :], mflt[:, 1, :]
        link(ts(mtmp, mi, 15, None, ALU.bitwise_and))
        link(ts(m16, mtmp, 0, None, ALU.is_equal))
        link(ts(mtmp, mi, 3, None, ALU.bitwise_and))
        link(ts(m4, mtmp, 0, None, ALU.is_equal))
        L2, L3 = 8.0 * float(np.log(2.0)), 8.0 * float(np.log(3.0))
        f2 = mflt[:, 2, :]
        t3 = mflt[:, 3, :]
        link(ts(f2, m16, L3 - L2, None, ALU.mult))
        link(stt(f2, m4, L2, f2, ALU.mult, ALU.add))
        link(ts(t3, m4, -NEG, NEG, ALU.mult, ALU.add))
        link(stt(t3, m16, L2, t3, ALU.mult, ALU.add))
        link(tt_(f2, f2, t3, ALU.subtract))
        link(ts(m16, m16, -NEG, NEG, ALU.mult, ALU.add))
        link(tt_(m4, t3, m16, ALU.subtract))
        v.sem_inc(mask_base, 1)

        v.wait_ge(params_loaded, 16 * 13)
        link(v.tensor_copy(posf[:, :], posi[:, :]))
        ang, nn, red, co = (rope[:, i, :] for i in range(4))
        as3 = lambda x: x.rearrange("p (t r) -> p t r", r=ROT)
        link(tt_(as3(ang), posf[:, :].unsqueeze(2).to_broadcast([P, TT, ROT]), invf[:, :].unsqueeze(1).to_broadcast([P, TT, ROT]), ALU.mult))
        link(ts(nn, ang, float(1.0 / (2.0 * np.pi)), MAGIC, ALU.mult, ALU.add))
        link(ts(nn, nn, -MAGIC, None, ALU.add))
        two_pi = 2.0 * np.pi
        c1 = 6.28125
        c2 = float(np.float32(int((two_pi - c1) * 2 ** 20) / 2 ** 20))
        c3 = float(two_pi - c1 - c2)
        link(stt(red, nn, -c1, ang, ALU.mult, ALU.add))
        link(stt(red, nn, -c2, red, ALU.mult, ALU.add))
        link(stt(red, nn, -c3, red, ALU.mult, ALU.add))
        link(ts(red, red, 3.1415925, -3.1415925, ALU.min, ALU.max))
        link(ts(co, red, -1.0, None, ALU.mult))
        link(tt_(co, co, red, ALU.max))
        link(ts(co, co, -1.0, float(np.pi / 2), ALU.mult, ALU.add))
        v.sem_inc(angle_ready, 1)

        mod_state = {"g": 0}

        def mod_acc(n):
            for half in range(2):
                dest = acc[n % 2][:, half * HALF:half * HALF + HALF]
                for kt in range(0, KT, 2):
                    g = mod_state["g"]
                    v.wait_ge(mod_filled[g % MOD_RING], 16 * (g // MOD_RING + 1))
                    w = mod_slot[g % MOD_RING]
                    if kt == 0:
                        link(ts(dest, w[:, 0, :], cs[:, 0:1], None, ALU.mult))
                    else:
                        link(stt(dest, w[:, 0, :], cs[:, kt:kt + 1], dest, ALU.mult, ALU.add))
                    ins = stt(dest, w[:, 1, :], cs[:, kt + 1:kt + 2], dest, ALU.mult, ALU.add)
                    ins.then_inc(mod_used, 1)
                    v.wait_ge(mod_used, g + 1)
                    mod_state["g"] += 1
            v.sem_inc(acc_ready, 1)

        def mod_take(n):
            l, q = part_of(n)
            v.wait_ge(mod_reduced, n + 1)
            if q in (2, 5):
                g = 2 * l + q // 5
                v.wait_ge(g_bias_loaded[g], 16)
                link(tt_(G[:, g, 0:HALF], ps[:, 6, :], G[:, g, 0:HALF], ALU.add))
                tt_(G[:, g, HALF:D], ps[:, 7, :], G[:, g, HALF:D], ALU.add).then_inc(mod_done, 1)
            else:
                w = 2 * l + q // 3
                if q % 3 == 0:
                    tt_(AB[:, w, 1, :], ps[:, 7, 0:KT], mbc[:, n, :], ALU.add).then_inc(mod_done, 1)
                else:
                    link(tt_(AB[:, w, 0, :], ps[:, 7, 0:KT], mbc[:, n, :], ALU.add))
                    stt(AB[:, w, 0, :], AB[:, w, 0, :], 1.0, gcols[:, l, q // 3, :], ALU.add, ALU.mult).then_inc(mod_done, 1)
            v.wait_ge(mod_done, n + 1)

        def norm(s):
            for t in (0, 1):
                link(v.tensor_tensor_reduce(XN[:, t, :], X[:, t, :], X[:, t, :], 1.0, 0.0, ALU.mult, ALU.add, stats[:, 0, t:t + 1]))
            v.wait_ge(ssq_ready, 2 * (s + 1))
            ts(stats[:, 1, :], stats[:, 0, :], 1.0 / D, EPS, ALU.mult, ALU.add).then_inc(ms_ready, 1)
            v.wait_ge(rms_ready, s + 1)
            link(v.reciprocal(stats[:, 3, :], stats[:, 2, :]))
            for t in range(TT):
                if s < 4:
                    ts(XN[:, t, :], X[:, t, :], stats[:, 3, t:t + 1], None, ALU.mult).then_inc(xn_ready, 1)
                else:
                    if t == 0:
                        v.wait_ge(fg_loaded, 16)
                    stt(XN[:, t, :], X[:, t, :], stats[:, 3, t:t + 1], G[:, 0, :], ALU.mult, ALU.mult).then_inc(final_ready, 1)
            if s == 4:
                return

        def norm_take(s):
            for kt in range(1, KT, 2):
                v.wait_ge(xn_turned, KT * s + kt + 1)
                ts(HT[:, kt, :], ps[:, kt, :], AB[:, s, 0, kt:kt + 1], AB[:, s, 1, kt:kt + 1], ALU.mult, ALU.add).then_inc(ht_dve, 1)

        v.wait_ge(cs_ready, 1)
        mod_acc(0)
        mod_acc(1)
        v.wait_ge(x_loaded, 16)
        mod_take(0)
        mod_take(1)
        norm(0)
        norm_take(0)

        v.wait_ge(cols_turned, 1)
        link(v.tensor_copy(cols[:, :], ps[:, 7, 64:120]))
        v.sem_inc(cols_ready, 1)
        link(ts(hbias[:, :], cols[:, 32:48], 0.5, None, ALU.mult))
        lam = cols[:, 48:56]
        link(ts(lru[:, 0, :], lam, -1.0, None, ALU.mult))
        link(tt_(lru[:, 0, :], lru[:, 0, :], lam, ALU.max))
        v.sem_inc(lam_abs, 1)
        v.wait_ge(lam_exp, 1)
        e_, s_, t_, y_ = lru[:, 1, :], lru[:, 2, :], lru[:, 3, :], lru[:, 4, :]
        link(ts(s_, e_, 2.0, None, ALU.add))
        link(v.reciprocal(s_, s_))
        link(tt_(s_, s_, e_, ALU.mult))
        link(tt_(t_, s_, s_, ALU.mult))
        link(ts(y_, t_, 1.0 / 17.0, None, ALU.mult))
        for k in range(15, 1, -2):
            link(stt(y_, y_, 1.0 / k, t_, ALU.add, ALU.mult))
        link(stt(y_, y_, 1.0, s_, ALU.add, ALU.mult))
        link(ts(t_, lam, -1.0, 0.0, ALU.mult, ALU.max))
        link(stt(t_, y_, 2.0, t_, ALU.mult, ALU.add))
        link(ts(dec[:, 0, :], t_, -4.0, None, ALU.mult))
        ts(dec[:, 1, :], t_, 4.0, None, ALU.mult).then_inc(dec_ready, 1)

        def col(i):
            return cols[:, i:i + 1]

        def conv_b(j):
            v.wait_ge(z_act, j + 1)
            u, x = u_in, xr[j]
            w = lambda k: col(12 + 4 * k + j)
            link(ts(x, u, w(1), col(28 + j), ALU.mult, ALU.add))
            link(stt(x[:, 1:S], u[:, 0:S - 1], w(0), x[:, 1:S], ALU.mult, ALU.add))
            link(stt(x[:, 0:S - 1], u[:, 1:S], w(2), x[:, 0:S - 1], ALU.mult, ALU.add))
            stt(x[:, 0:S - 2], u[:, 2:S], w(3), x[:, 0:S - 2], ALU.mult, ALU.add).then_inc(xr_ready, 1)
            v.wait_ge(xr_ready, j + 1)

        def gates(j):
            for d in range(2):
                v.wait_ge(m_ready, 4 * j + d + 1)
                link(tt_(tmp0, av[d], av[d], ALU.mult))
                stt(th[d], tmp0, 1.0, th[d], ALU.add, ALU.mult).then_inc(mult_ready, 1)
                v.wait_ge(mult_ready, 4 * j + d + 1)
                link(stt(ti[d], ti[d], 1.0, xr[j], ALU.add, ALU.mult))
            for d in range(2):
                v.wait_ge(m_ready, 4 * j + 2 + d + 1)
                link(tt_(ti[d], ti[d], th[d], ALU.mult))
                if d == 0:
                    x0, x1, o_ = av[0], ti[0], th[0]
                else:
                    x0, x1, o_ = av[1][:, ::-1], ti[1][:, ::-1], th[1][:, ::-1]
                v.tensor_tensor_scan(o_, x0, x1, 0.0, ALU.mult, ALU.add).then_inc(mult_ready, 1)
                v.wait_ge(mult_ready, 4 * j + 2 + d + 1)
            link(tt_(tmp0, th[0], th[1], ALU.add))
            v.sem_inc(scan_done, 1)
            tt_(mixT[:, LRU_TILES + j, :], mixT[:, LRU_TILES + j, :], tmp0, ALU.mult).then_inc(mix_ready, 1)
            v.wait_ge(mix_ready, j + 1)

        bank_of = lambda t: (4, 5, 0, 1, 2, 3)[(t - 8) % 6]

        def val(j):
            t = 12 + j
            v.wait_ge(z_ready, t + 1)
            v.wait_ge(z_act, 8 + j + 1)
            m = mixT[:, j, :]
            tt_(m, ps[:, bank_of(t), :], m, ALU.mult).then_inc(z_dve, 1)
            v.wait_ge(z_dve, j + 1)
            c_ = xr[j]
            w = lambda k: col(4 * k + j)
            link(ts(c_, m, w(1), None, ALU.mult))
            link(stt(c_[:, 1:S], m[:, 0:S - 1], w(0), c_[:, 1:S], ALU.mult, ALU.add))
            link(stt(c_[:, 0:S - 1], m[:, 1:S], w(2), c_[:, 0:S - 1], ALU.mult, ALU.add))

        def gb(j):
            t = 16 + j
            v.wait_ge(z_ready, t + 1)
            tt_(mixT[:, j, :], ps[:, bank_of(t), :], xr[j], ALU.mult).then_inc(z_dve, 1)

        for j in range(4):
            conv_b(j)
        mod_acc(2)
        gates(0)
        mod_acc(3)
        mod_take(2)
        gates(1)
        mod_acc(4)
        mod_take(3)
        gates(2)
        mod_acc(5)
        mod_take(4)
        gates(3)
        mod_acc(6)
        mod_take(5)
        val(0)
        mod_acc(7)
        mod_take(6)
        val(1)
        val(2)
        mod_acc(8)
        mod_take(7)
        val(3)
        mod_acc(9)
        mod_take(8)
        gb(0)
        gb(1)
        mod_acc(10)
        mod_take(9)
        gb(2)
        mod_acc(11)
        mod_take(10)
        gb(3)
        mod_take(11)

        def residual(l):
            for b in range(8):
                half, t = b // 4, b % 4
                v.wait_ge(y_ready, 8 * l + b + 1)
                bank = ps[:, b, :]
                cut = slice(half * HALF, half * HALF + HALF)
                link(tt_(bank, bank, G[:, 2 * l, cut], ALU.mult))
                link(tt_(X[:, t, cut], bank, X[:, t, cut], ALU.add))
            v.sem_inc(x_ready, 1)

        def take(base, size, shape=None):
            x = rt[:, base:base + size]
            return x

        def route(l):
            n = TT * NE
            v.wait_ge(score_ready, l + 1)
            sc, bia, o1, o2 = (rt[:, i * n:(i + 1) * n] for i in range(4))
            t0, t1, t2 = (rt[:, i * n:(i + 1) * n] for i in range(4, 7))
            q64 = rt[:, 7 * n:8 * n]
            b0 = 8 * n
            hi, lo = rt[:, b0:b0 + 32], rt[:, b0 + 32:b0 + 64]
            hm, lm, h1 = (rt[:, b0 + 64 + 16 * i:b0 + 80 + 16 * i] for i in range(3))
            gi = rt[:, b0 + 112:b0 + 116]
            ef = rt[:, b0 + 120:b0 + 152]
            cnt, inc, exc, cmp_ = (rt[:, b0 + 160 + 16 * i:b0 + 176 + 16 * i] for i in range(4))
            cond = rt[:, b0 + 224:b0 + 224 + MAX_OVER * NE]
            sel = rt[:, b0 + 344:b0 + 352]
            s12 = rt[:, b0 + 352:b0 + 368]
            v3 = lambda x: x.rearrange("p (t e) -> p t e", t=TT)
            bc_e = lambda x: x.unsqueeze(1).to_broadcast([P, TT, NE])
            bc_t = lambda x: x.unsqueeze(2).to_broadcast([P, TT, NE])
            link(tt_(v3(bia), v3(sc), bc_e(rb[:, :]), ALU.add))
            link(tt_(hi, bia[:, 0:n:2], bia[:, 1:n:2], ALU.max))
            link(tt_(lo, bia[:, 0:n:2], bia[:, 1:n:2], ALU.min))
            link(tt_(hm, hi[:, 0:32:2], hi[:, 1:32:2], ALU.min))
            link(tt_(lm, lo[:, 0:32:2], lo[:, 1:32:2], ALU.max))
            link(tt_(h1, hi[:, 0:32:2], hi[:, 1:32:2], ALU.max))
            link(tt_(hm, hm, lm, ALU.max))
            link(tt_(gpad[:, :, 0:NG], h1.rearrange("p (t g) -> p t g", g=NG), hm.rearrange("p (t g) -> p t g", g=NG), ALU.add))
            for t in range(TT):
                link(v.max(mx8[:, t, :], gpad[:, t, :]))
                link(v.max_index(ix8[:, t, :], mx8[:, t, :], gpad[:, t, :]))
            link(v.tensor_copy(gi, ix8[:, :, 0]))
            link(tt_(v3(t0), bc_e(g_id[:, :]), bc_t(gi), ALU.is_equal))
            link(tt_(t1, bia, t0, ALU.mult))
            link(ts(t0, t0, -NEG, NEG, ALU.mult, ALU.add))
            link(tt_(t1, t1, t0, ALU.add))
            for t in range(TT):
                link(v.max(mx8[:, t, :], t1[:, t * NE:(t + 1) * NE]))
                link(v.max_index(ix8[:, t, :], mx8[:, t, :], t1[:, t * NE:(t + 1) * NE]))
            efv = ef.rearrange("p (t k) -> p t k", k=8)
            link(v.tensor_copy(efv, ix8[:, :, :]))
            link(tt_(v3(o1), bc_e(e_id[:, :]), bc_t(efv[:, :, 0]), ALU.is_equal))
            link(tt_(v3(o2), bc_e(e_id[:, :]), bc_t(efv[:, :, 1]), ALU.is_equal))
            tt_(hot[:, :, :], v3(o1), v3(o2), ALU.add).then_inc(hot_ready, 1)
            link(tt_(t0, o1, sc, ALU.mult))
            link(v.tensor_reduce(s12[:, 0:4], v3(t0), AX_X, ALU.add))
            link(tt_(t0, o2, sc, ALU.mult))
            link(v.tensor_reduce(s12[:, 4:8], v3(t0), AX_X, ALU.add))
            link(tt_(s12[:, 8:12], s12[:, 0:4], s12[:, 4:8], ALU.add))
            link(v.reciprocal(s12[:, 12:16], s12[:, 8:12]))
            link(tt_(comb_w[:, 0, :], s12[:, 0:4], s12[:, 12:16], ALU.mult))
            link(tt_(comb_w[:, 1, :], s12[:, 4:8], s12[:, 12:16], ALU.mult))
            v.wait_ge(rank_ready, l + 1)
            link(v.tensor_copy(t0, ps[:, 1, 0:n]))
            link(v.tensor_copy(cnt, ps[:, 1, n:n + NE]))
            link(ts(q64, t0, float(P), None, ALU.is_ge))
            link(ts(cmp_, cnt, float(P), None, ALU.is_gt))
            for i in range(2, TT):
                link(stt(q64, t0, float(i * P), q64, ALU.is_ge, ALU.add))
                link(stt(cmp_, cnt, float(i * P), cmp_, ALU.is_gt, ALU.add))
            link(v.tensor_tensor_scan(inc, ones[:, 0:NE], cmp_, 0.0, ALU.mult, ALU.add))
            link(tt_(exc, inc, cmp_, ALU.subtract))
            link(tt_(exc, exc, em15[:, :], ALU.add))
            link(tt_(v3(t1), v3(q64), bc_e(exc), ALU.add))
            link(ts(t2, q64, 1.0, None, ALU.min))
            link(tt_(t1, t1, t2, ALU.mult))
            link(tt_(v3(t1), v3(t1), bc_e(e_id[:, :]), ALU.add))
            link(stt(t0, q64, -float(P), t0, ALU.mult, ALU.add))
            link(stt(t0, t1, float(P), t0, ALU.mult, ALU.add))
            for j, oh in enumerate((o1, o2)):
                link(tt_(t2, oh, t0, ALU.mult))
                link(v.tensor_reduce(dst[:, j, :], v3(t2), AX_X, ALU.add))
            link(v.tensor_copy(yrow[:, :, :], dst[:, :, :]))
            yr = yrow[:, :, :].rearrange("p a b -> p (a b)")
            link(ts(ytmp[:, 0, :], yr, 7, None, ALU.arith_shift_right))
            link(ts(ytmp[:, 1, :], yr, P - 1, None, ALU.bitwise_and))
            link(stt(trow[:, :, :].rearrange("p a b -> p (a b)"), ytmp[:, 1, :], float(NBLK), ytmp[:, 0, :], ALU.mult, ALU.add))
            cv = cond.rearrange("p (k e) -> p k e", e=NE)
            link(tt_(cv, inc.unsqueeze(1).to_broadcast([P, MAX_OVER, NE]), k_id[:, :].unsqueeze(2).to_broadcast([P, MAX_OVER, NE]), ALU.is_le))
            link(v.tensor_reduce(sel[:, 0:MAX_OVER], cv, AX_X, ALU.add))
            link(ts(sel[:, 0:MAX_OVER], sel[:, 0:MAX_OVER], float(NE - 1), None, ALU.min))
            link(v.tensor_copy(sel[:, MAX_OVER:8], inc[:, NE - 1:NE]))
            v.tensor_copy(info[:, :], sel).then_inc(route_ready, 1)
            v.wait_ge(route_ready, l + 1)

        def experts(l):
            s = 2 * l + 1
            e0 = l * NE
            norm(s)
            norm_take(s)
            route(l)

            def xst(n):
                v.wait_ge(xs_turned, n)
                for kt in range(4, KT):
                    ins = ts(xsT[:, kt, :], ps[:, 1, (kt - 4) * P:(kt - 3) * P], AB[:, s, 0, kt:kt + 1], AB[:, s, 1, kt:kt + 1], ALU.mult, ALU.add)
                ins.then_inc(xst_dve, 1)

            def step(e, par, first, second, last):
                v.wait_ge(silu_done, e + (e0 + 1))
                v.wait_ge(up_done, e + (e0 + 1))
                if not first:
                    v.wait_ge(hid_turned, e + e0)
                tt_(hid, ps[:, 3, :], sg, ALU.mult).then_inc(hid_ready, 1)
                if not last:
                    xst(e + (e0 + 2))
                v.wait_ge(down_done, e + (e0 + 1))
                if not second:
                    n_before = (NE // 2) * l * 16
                    v.wait_ge(yb_stored[par], (e - par) * 8 + n_before)
                for h in range(2):
                    ins = tt_(ybuf[par][:, h * HALF:h * HALF + HALF], ps[:, 5 + h, :], G[:, 2 * l + 1, h * HALF:h * HALF + HALF], ALU.mult)
                ins.then_inc(yb_ready, 1)

            xst(e0 + 1)
            for par in range(2):
                step(par, par, par == 0, True, False)
            with v.Fori(1, NE // 2 - 1) as i:
                for par in range(2):
                    step(2 * i + par, par, False, False, False)
            for par in range(2):
                step(NE - 2 + par, par, False, False, par == 1)

            o = over[l]
            n_over = v.value_load(info[0:1, 7:8], min_val=0, max_val=MAX_OVER)
            with v.Fori(0, MAX_OVER) as k:
                with v.If(k < n_over):
                    v.wait_ge(o["turned"], k + 1)
                    for kt in range(4, KT):
                        ins = ts(xsT[:, kt, :], ps[:, 1, (kt - 4) * P:(kt - 3) * P], AB[:, s, 0, kt:kt + 1], AB[:, s, 1, kt:kt + 1], ALU.mult, ALU.add)
                    ins.then_inc(o["xst"], 1)
                    v.wait_ge(o["silu"], k + 1)
                    tt_(hid, ps[:, 3, :], sg, ALU.mult).then_inc(o["hid"], 1)
                    v.wait_ge(o["down"], k + 1)
                    for h in range(2):
                        ins = tt_(ybuf[0][:, h * HALF:h * HALF + HALF], ps[:, 5 + h, :], G[:, 2 * l + 1, h * HALF:h * HALF + HALF], ALU.mult)
                    ins.then_inc(o["yb"], 1)
            for t in range(TT):
                v.wait_ge(comb_filled[t], 32 * (l + 1))
                for j in range(2):
                    link(stt(X[:, t, :], comb[j][t], comb_w[:, j, t:t + 1], X[:, t, :], ALU.mult, ALU.add))
            v.sem_inc(x_ready, 1)

        residual(0)
        experts(0)
        norm(2)
        norm_take(2)

        def rotate(z, n):
            v.wait_ge(qkv_act, 4 * n)
            zv = z.rearrange("p t (h d) -> p t h d", d=HD)
            z1, z2 = zv[:, :, :, 0:ROT], zv[:, :, :, ROT:2 * ROT]
            bc = lambda x: x.rearrange("p (t r) -> p t r", r=ROT).unsqueeze(2).to_broadcast([P, TT, HEADS, ROT])
            sin, cos = bc(rope[:, 4, :]), bc(rope[:, 5, :])
            r4 = [x.rearrange("p (t h r) -> p t h r", h=HEADS, r=ROT) for x in rots]
            link(tt_(r4[0], z1, cos, ALU.mult))
            link(tt_(r4[1], z2, sin, ALU.mult))
            link(tt_(r4[2], z2, cos, ALU.mult))
            link(tt_(r4[3], z1, sin, ALU.mult))
            link(tt_(z1, r4[0], r4[1], ALU.subtract))
            link(tt_(z2, r4[2], r4[3], ALU.add))
            v.sem_inc(rot_ready, 1)

        v.wait_ge(rope_ready, 2)
        for w in range(6):
            dest = (Q, K, V)[w // 2]
            for t in (1, 3):
                v.wait_ge(qkv_ready, 4 * w + t + 1)
                v.tensor_copy(dest[:, t, (w % 2) * HALF:(w % 2) * HALF + HALF], ps[:, 4 * (w % 2) + t, :]).then_inc(qkv_dve, 1)
            if w in (1, 3):
                v.wait_ge(qkv_dve, 2 * (w + 1))
                rotate(dest, (w + 1) // 2)
        for hp in range(8):
            v.wait_ge(kt_turned, hp + 1)
            v.tensor_copy(KTR[:, hp, :], ps[:, (2 * hp + 1) % 8, :]).then_inc(kt_ready, 1)

        def score_step(n):
            it = (n // 2) % TT
            v.wait_ge(s_ready, n + 1)
            if n >= 4:
                v.wait_ge(p_turned, n - 3)
            lc = LC[:, (TT - 1 - it) * P:(TT - 1 - it) * P + S]
            link(v.tensor_tensor_reduce(prob[n % 4], ps[:, n % 3, :], lc, HD ** -0.5, -3.0e38, ALU.add, ALU.max, mx[:, n:n + 1]))
            ts(nmx[:, n:n + 1], mx[:, n:n + 1], -1.0, None, ALU.mult).then_inc(max_ready, 1)

        def head_out(hp):
            v.wait_ge(av_ready, 8 * hp + 8)
            link(v.reciprocal(rsum[:, 8 * hp:8 * hp + 8], ssum[:, 8 * hp:8 * hp + 8]))
            o4 = O[:, :, hp * P:(hp + 1) * P].rearrange("p t (h d) -> p t h d", d=HD)
            p4 = ps[:, 5 + hp % 2, :].rearrange("p (t h d) -> p t h d", h=2, d=HD)
            r4 = rsum[:, 8 * hp:8 * hp + 8].rearrange("p (t h) -> p t h", h=2).unsqueeze(3).to_broadcast([P, TT, 2, HD])
            tt_(o4, p4, r4, ALU.mult).then_inc(o_ready, 1)

        v.wait_ge(mask_ready, 1)
        v.wait_ge(kt_turned, 8)
        score_step(0)
        score_step(1)
        for u in range(64):
            if u + 2 < 64:
                score_step(u + 2)
            if u % 2 == 1:
                v.wait_ge(p_turned, u + 1)
                if u >= 4:
                    v.wait_ge(av_ready, u - 3)
                v.tensor_copy(probT[u % 4], ps[:, 3 + u % 2, :]).then_inc(pt_dve, 1)
            if u % 8 == 2 and u > 8:
                head_out(u // 8 - 1)
        head_out(7)
        for kt in range(1, KT, 2):
            v.wait_ge(o_turned, kt + 1)
            v.tensor_copy(OT[:, kt, :], ps[:, kt, :]).then_inc(ot_dve, 1)
        residual(1)
        experts(1)
        norm(4)

    @block.tensor
    def _(pe):
        def norm(s):
            pe.wait_ge(xn_ready, 4 * (s + 1))
            for kt in range(KT):
                for t in range(TT):
                    ins = pe.transpose(ps[:, kt, t * P:(t + 1) * P], XN[:, t, kt:D:KT], ident[:, :])
                ins.then_inc(xn_turned, 1)

        def wait_ht(s):
            pe.wait_ge(ht_act, 4 * (s + 1))
            pe.wait_ge(ht_dve, 4 * (s + 1))

        def mod_reduce(n):
            l, q = part_of(n)
            if n:
                pe.wait_ge(mod_done, n)
            pe.wait_ge(acc_ready, n + 1)
            if q in (2, 5):
                for h in range(2):
                    ins = pe.matmul(ps[:, 6 + h, :], ones[:, :], acc[n % 2][:, h * HALF:h * HALF + HALF], start=True, stop=True)
            else:
                for kt in range(KT):
                    ins = pe.matmul(ps[:, 7, kt:kt + 1], acc[n % 2][:, kt:D:KT], ones[:, 0:1], start=True, stop=True)
            ins.then_inc(mod_reduced, 1)

        pe.wait_ge(consts_ready, 1)
        pe.wait_ge(params_loaded, 16 * 13)
        mod_reduce(0)
        mod_reduce(1)
        pe.wait_ge(mod_done, 2)
        norm(0)
        wait_ht(0)
        pe.transpose(ps[:, 7, 64:120], rows[0:56, :], ident[0:56, 0:56]).then_inc(cols_turned, 1)

        bank_of = lambda t: (4, 5, 0, 1, 2, 3)[(t - 8) % 6]

        def z_tile(t, bank):
            g, j = t // 4, t % 4
            if j == 0:
                wait_slab(pe, N_IN + g)
            for kt in range(KT):
                ins = pe.matmul(ps[:, bank, :], slab(N_IN + g)[:, kt, j * P:(j + 1) * P], HT[:, kt, :], start=(kt == 0), stop=(kt == KT - 1))
            ins.then_inc(z_ready, 1)

        for t in range(4):
            z_tile(t, t)
        pe.wait_ge(bd_loaded, 16 * 8)
        for j in range(LRU_TILES):
            if j >= 2:
                pe.wait_ge(z_act, LRU_TILES + j - 1)
            z_tile(LRU_TILES + j, 4 + j % 2)
            pe.wait_ge(z_act, LRU_TILES)
            pe.wait_ge(xr_ready, j + 1)
            if j:
                pe.wait_ge(gate_read, j)
            for d in range(2):
                for w in range(2):
                    ins = pe.matmul(ps[:, 2 * d + w, :], BD[:, (d * 2 + w) * LRU_TILES + j, :], xr[j], start=True, stop=True)
            ins.then_inc(gate_ready, 1)
            if j:
                mod_reduce(j + 1)
        reduce_after = {8: 5, 10: 6, 12: 7, 14: 8, 16: 9, 17: 10, 19: 11}
        for t in range(8, 20):
            if t < 10:
                pe.wait_ge(z_act, 8)
            elif t < 14:
                pe.wait_ge(gate_read, LRU_TILES)
            elif t < 18:
                pe.wait_ge(z_act, t - 5)
            else:
                pe.wait_ge(z_dve, t - 17)
            z_tile(t, bank_of(t))
            if t in reduce_after:
                mod_reduce(reduce_after[t])

        def project(l, lhs, n, order):
            for half in range(2):
                wait_slab(pe, n + half)
                for t in range(TT):
                    for i, kt in enumerate(order):
                        ins = pe.matmul(ps[:, half * 4 + t, :], lhs[:, kt, t * P:(t + 1) * P], slab(n + half)[:, kt, :], start=(i == 0), stop=(i == KT - 1))
                    ins.then_inc(y_ready, 1)

        pe.wait_ge(mix_ready, LRU_TILES)
        pe.wait_ge(z_dve, 8)
        pe.wait_ge(mod_done, LAYERS * PARTS)
        project(0, mixT, N_OUT, (4, 5, 6, 7, 0, 1, 2, 3))

        def experts(l):
            s = 2 * l + 1
            e0 = l * NE
            base = exp_base[l]
            norm(s)
            wait_ht(s)
            for t in range(TT):
                for kt in range(KT):
                    ins = pe.matmul(ps[:, 0, t * NE:(t + 1) * NE], HT[:, kt, t * P:(t + 1) * P], rw[:, kt, :], start=(kt == 0), stop=(kt == KT - 1))
            ins.then_inc(logit_ready, 1)
            pe.wait_ge(hot_ready, l + 1)
            for t in range(TT):
                for t0 in range(t + 1):
                    pe.matmul(ps[:, 1, t * NE:(t + 1) * NE], before[:, :] if t0 == t else ones_b[:, :], hot[:, t0, :], start=(t0 == 0), stop=(t0 == t))
            for t in range(TT):
                ins = pe.matmul(ps[:, 1, TT * NE:(TT + 1) * NE], ones_b[:, :], hot[:, t, :], start=(t == 0), stop=(t == TT - 1))
            ins.then_inc(rank_ready, 1)
            pe.wait_ge(route_ready, l + 1)

            def turn_xs(buf, done):
                for kt in range(KT):
                    ins = pe.transpose(ps[:, kt // 4, (kt % 4) * P:(kt % 4 + 1) * P], xs[buf][:, kt:D:KT], ident[:, :])
                ins.then_inc(done, 1)

            def product(w, bank, done):
                for kt in range(KT):
                    ins = pe.matmul(ps[:, bank, :], xsT[:, kt, :], w[:, kt, :], start=(kt == 0), stop=(kt == KT - 1))
                ins.then_inc(done, 1)

            def turn_hid(done):
                for f in range(FT):
                    ins = pe.transpose(ps[:, 4, f * P:(f + 1) * P], hid[:, f * P:(f + 1) * P], ident[:, :])
                ins.then_inc(done, 1)

            def down(w, done):
                for h in range(2):
                    for f in range(FT):
                        ins = pe.matmul(ps[:, 5 + h, :], hidT[:, f, :], w[:, 2 * f + h, :], start=(f == 0), stop=(f == FT - 1))
                ins.then_inc(done, 1)

            def step(e, par, turn, first, last):
                n = base + 3 * par if turn is not None else base + 3 * e
                pe.wait_ge(xst_act, e + (e0 + 1))
                pe.wait_ge(xst_dve, e + (e0 + 1))
                if not first:
                    pe.wait_ge(hid_ready, e + e0)
                wait_slab(pe, n, turn)
                product(slab(n), 2, gate_done)
                wait_slab(pe, n + 1, turn)
                product(slab(n + 1), 3, up_done)
                if not last:
                    k = 8 * l * 16
                    nxt = 1 - par
                    pe.wait_ge(xs_filled[nxt], (e + (1 + par - 1)) * 8 + (k + 16) if par == 0 else (e + 1) * 8 + (k + 16))
                    turn_xs(nxt, xs_turned)
                pe.wait_ge(hid_ready, e + (e0 + 1))
                turn_hid(hid_turned)
                pe.wait_ge(hidt_ready, e + (e0 + 1))
                if not first:
                    pe.wait_ge(yb_ready, e + e0)
                wait_slab(pe, n + 2, turn)
                down(slab(n + 2), down_done)

            pe.wait_ge(xs_filled[0], 8 * l * 16 + 16)
            turn_xs(0, xs_turned)
            for par in range(2):
                step(par, par, None, par == 0, False)
            with pe.Fori(1, NE // 2 - 1) as i:
                for par in range(2):
                    step(2 * i + par, par, i, False, False)
            for par in range(2):
                step(NE - 2 + par, par, None, False, par == 1)

            o = over[l]
            wbuf = [HT[:, :, :], XN[:, :, :].rearrange("p t (h n) -> p (t h) n", h=2)]
            n_over = pe.value_load(info[0:1, 7:8], min_val=0, max_val=MAX_OVER)
            with pe.Fori(0, MAX_OVER) as k:
                with pe.If(k < n_over):
                    pe.wait_ge(o["xs"], (k + 1) * 16)
                    pe.wait_ge(yb_ready, e0 + NE)
                    turn_xs(0, o["turned"])
                    pe.wait_ge(o["xst"], (k + 1) * 2)
                    pe.wait_ge(o["wg"], (k + 1) * 16)
                    pe.wait_ge(o["wu"], (k + 1) * 16)
                    for c in range(2):
                        for kt in range(KT):
                            ins = pe.matmul(ps[:, 2 + c, :], xsT[:, kt, :], wbuf[c][:, kt, :], start=(kt == 0), stop=(kt == KT - 1))
                    ins.then_inc(o["gu"], 1)
                    pe.wait_ge(o["hid"], k + 1)
                    turn_hid(o["hidt_in"])
                    pe.wait_ge(o["hidt"], k + 1)
                    pe.wait_ge(o["wd"], (k + 1) * 16)
                    down(wbuf[0], o["down"])

        experts(0)
        norm(2)
        wait_ht(2)
        for w in range(6):
            wait_slab(pe, N_QKV + w)
            if w >= 2:
                pe.wait_ge(qkv_act, 2 * (w - 1))
                pe.wait_ge(qkv_dve, 2 * (w - 1))
            for t in range(TT):
                for kt in range(KT):
                    ins = pe.matmul(ps[:, 4 * (w % 2) + t, :], HT[:, kt, t * P:(t + 1) * P], slab(N_QKV + w)[:, kt, :], start=(kt == 0), stop=(kt == KT - 1))
                ins.then_inc(qkv_ready, 1)
        pe.wait_ge(qkv_act, 12)
        pe.wait_ge(qkv_dve, 12)
        pe.wait_ge(rot_ready, 2)
        for hp in range(8):
            if hp >= 4:
                pe.wait_ge(qt_ready, hp - 3)
            for t in range(TT):
                ins = pe.transpose(ps[:, (2 * hp) % 8, t * P:(t + 1) * P], Q[:, t, hp * P:(hp + 1) * P], ident[:, :])
            ins.then_inc(qt_turned, 1)
            if hp >= 4:
                pe.wait_ge(kt_ready, hp - 3)
            for t in range(TT):
                ins = pe.transpose(ps[:, (2 * hp + 1) % 8, t * P:(t + 1) * P], K[:, t, hp * P:(hp + 1) * P], ident[:, :])
            ins.then_inc(kt_turned, 1)

        def scores(n):
            hp, it, par = n // 8, (n // 2) % TT, n % 2
            if n >= 3:
                pe.wait_ge(max_ready, n - 2)
            r0 = HD * par
            pe.matmul(ps[:, n % 3, :], QT[r0:r0 + HD, hp, it * P:(it + 1) * P], KTR[r0:r0 + HD, hp, :], start=True, stop=True).then_inc(s_ready, 1)

        def weigh(n):
            hp, it, par = n // 8, (n // 2) % TT, n % 2
            pe.wait_ge(pt_act if n % 2 == 0 else pt_dve, n // 2 + 1)
            if n % 8 == 0 and hp >= 2:
                pe.wait_ge(o_ready, hp - 1)
            dest = ps[:, 5 + hp % 2, (n % 8) * HD:(n % 8 + 1) * HD]
            h = 2 * hp + par
            for jt in range(TT):
                ins = pe.matmul(dest, probT[n % 4][:, jt * P:(jt + 1) * P], V[:, jt, h * HD:(h + 1) * HD], start=(jt == 0), stop=(jt == TT - 1))
            ins.then_inc(av_ready, 1)

        pe.wait_ge(qt_ready, 8)
        pe.wait_ge(kt_ready, 8)
        scores(0)
        scores(1)
        for u in range(64):
            if u + 2 < 64:
                scores(u + 2)
            pe.wait_ge(p_ready, u + 1)
            if u >= 2:
                pe.wait_ge(pt_act if u % 2 == 0 else pt_dve, u // 2)
            for jt in range(TT):
                ins = pe.transpose(ps[:, 3 + u % 2, jt * P:(jt + 1) * P], prob[u % 4][:, jt * P:(jt + 1) * P], ident[:, :])
            ins.then_inc(p_turned, 1)
            if u >= 1:
                weigh(u - 1)
        weigh(63)
        pe.wait_ge(o_ready, 8)
        for kt in range(KT):
            for t in range(TT):
                ins = pe.transpose(ps[:, kt, t * P:(t + 1) * P], O[:, t, kt * P:(kt + 1) * P], ident[:, :])
            ins.then_inc(o_turned, 1)
        pe.wait_ge(ot_act, 4)
        pe.wait_ge(ot_dve, 4)
        project(1, OT, N_WO, range(KT))
        experts(1)


_INS = ["x", "c", "positions", "mod_w", "mod_b", "norm_mix_g", "norm_ffn_g", "final_norm_g", "w_in_ab", "conv_a_w",
        "conv_b_w", "conv_b_b", "lru_wa", "lru_ba", "lru_wx", "lru_bx", "lru_lambda", "w_out_ab", "w_qkv", "w_o",
        "router_w", "router_bias", "expert_w_gate", "expert_w_up", "expert_w_down"]


def kernel(**inputs):
    import concourse.bacc as _bacc
    from concourse.bass_utils import run_bass_kernel_spmd as _run

    nc = _bacc.Bacc("TRN2", target_bir_lowering=False, num_devices=1, dynamic_dma_scratch_size=4096)
    arrays, args = {}, {}
    for name in _INS:
        arr = np.ascontiguousarray(inputs[name])
        arrays[f"in_{name}_dram"] = arr
        args[name] = nc.dram_tensor(f"in_{name}_dram", arr.shape, mybir.dt.from_np(arr.dtype), kind="ExternalInput").ap()
    out = nc.dram_tensor("out_dram", (1, S, D), F32, kind="ExternalOutput").ap()
    trunk(nc, args, out)
    r = _run(nc, [arrays], core_ids=[0])
    return r.results[0]["out_dram"]
```

```python
from contextlib import ExitStack

import numpy as np

import concourse.bass as bass
from concourse import mybir

ALU = mybir.AluOpType
ACT = mybir.ActivationFunctionType
AX_X = mybir.AxisListType.X
F32 = mybir.dt.float32
BF16 = mybir.dt.bfloat16
I32 = mybir.dt.int32
U32 = mybir.dt.uint32

P = 128
D = 1024
S = 512
TT = S // P
KT = D // P
HALF = 512
LRU_TILES = 4
HEADS, HD = 16, 64
ROT = 8
NE, NG, EPG = 16, 4, 4
FF = 512
FT = FF // P
MAX_OVER = 2 * S // P - 1
NBLK = NE + MAX_OVER
RING = 6
MOD_RING = 4
MOD_QUARTERS = 8
LAYERS = 2
PARTS = 6
EPS = 1e-6
NEG = -1.0e30
NO_TOKEN = 1 << 20
ROPE_THETA = 500000.0
MAGIC = 12582912.0
LSPAN = (TT - 1) * P + S


class Link:

    def __init__(self, eng, sem):
        self.eng, self.sem, self.n, self.turn, self.per = eng, sem, 0, None, 0

    def __call__(self, ins):
        self.n += 1
        ins.then_inc(self.sem, 1)
        value = self.n if self.turn is None else self.turn * self.per + self.n
        self.eng.wait_ge(self.sem, value)

    def enter_loop(self, turn, first, per):
        self.turn, self.per, self.entry = turn, per, self.n
        self.n -= first * per

    def leave_loop(self, first, end):
        assert self.n + first * self.per == self.entry + self.per, (self.n + first * self.per - self.entry, self.per)
        self.turn = None
        self.n = self.entry + (end - first) * self.per


def part_of(n):
    return n // PARTS, n % PARTS


def trunk(nc, a, out):
    with ExitStack() as ctx:
        build(nc, ctx, a, out)


def build(nc, ctx, a, out):
    def small(name, shape, dt=F32):
        return ctx.enter_context(nc.sbuf_tensor(name, shape, dt))

    sems = {}

    def sem(name):
        sems[name] = ctx.enter_context(nc.semaphore(name))
        return sems[name]

    UNIT = 512
    X = small("x_res", [P, TT, D])
    ring = small("slab_ring", [P, RING, KT, HALF])
    modr = small("mod_ring", [P, 8, UNIT])
    G = small("gate_rows", [P, 4, D])
    LC = small("log_count", [P, LSPAN])
    HT = small("h_t", [P, KT, S])
    XN = small("x_norm", [P, TT, D])
    R = small("scratch", [P, 16, UNIT])

    ps = ctx.enter_context(nc.psum_tensor("ps", [P, 8, HALF], F32))

    mod_slot = [modr[:, 2 * i:2 * i + 2, :] for i in range(MOD_RING)]
    u_in = R[:, 0, :]
    xr = [R[:, 1 + j, :] for j in range(LRU_TILES)]
    th = [R[:, 5, :], R[:, 8, :]]
    ti = [R[:, 6, :], R[:, 9, :]]
    av = [R[:, 7, :], R[:, 10, :]]
    tmp0 = R[:, 11, :]
    acc = [R[:, 12:14, :].rearrange("p a n -> p (a n)"), R[:, 14:16, :].rearrange("p a n -> p (a n)")]
    mixT = XN[:, :, :].rearrange("p t (h n) -> p (t h) n", h=2)
    BD = G[:, 2:4, :].rearrange("p g (x o) -> p (g x) o", o=P)
    mflt = R[:, 11, :].rearrange("p (i n) -> p i n", n=P)
    mlow = R[:, 10, 0:P].bitcast(I32)
    xs = [R[:, 0:2, :].rearrange("p a n -> p (a n)"), R[:, 2:4, :].rearrange("p a n -> p (a n)")]
    xsT = [R[:, i:i + 2, :].rearrange("p a (b n) -> p (a b) n", n=P) for i in (4, 13)]
    sg = R[:, 6, :]
    hid = R[:, 7, :]
    hidT = R[:, 8, :].rearrange("p (f n) -> p f n", n=P)
    ybuf = [R[:, 9:11, :].rearrange("p a n -> p (a n)"), R[:, 11:13, :].rearrange("p a n -> p (a n)")]
    rt = R[:, 13:16, :].rearrange("p a n -> p (a n)")
    comb = [[XN[:, t, :] for t in range(TT)],
            [HT[:, 2 * t:2 * t + 2, :].rearrange("p a n -> p (a n)") for t in range(TT)]]
    Q = R[:, 0:8, :].rearrange("p (t h) n -> p t (h n)", h=2)
    O = Q
    QT = R[:, 8:16, :]
    K = modr[:, :, :].rearrange("p (t h) n -> p t (h n)", h=2)
    KTR = HT
    V = XN
    OT = modr
    xnorm = [modr[:, :, :].rearrange("p (t h) n -> p t (h n)", h=2) if s == 1 else XN for s in range(2 * LAYERS + 1)]
    prob = [modr[:, i, :] for i in range(4)]
    rots = [G[:, i // 2, (i % 2) * HALF:(i % 2) * HALF + HALF] for i in range(4)]
    probT = rots

    ident = small("ident", [P, P])
    ones = small("ones", [P, P])
    before = small("before", [P, P], BF16)
    ones_b = small("ones_b", [P, P], BF16)
    rows = small("param_rows", [56, P])
    cols = small("param_cols", [P, 56])
    cT = small("c_t", [P, KT])
    cs = small("c_silu", [P, KT])
    gcols = small("norm_gains", [P, LAYERS, 2, KT])
    mbc = small("mod_b_cols", [P, LAYERS * PARTS, KT])
    AB = small("mod_ab", [P, LAYERS * 2, 2, KT])
    rw = small("router_w", [P, KT, NE])
    rb = small("router_b", [P, NE])
    lru = small("lru_consts", [P, 6, 8])
    hbias = small("half_bias", [P, 16])
    dec = small("decay", [P, 2, 8])
    stats = small("stats", [P, 4, TT])
    eps = small("eps", [P, 1])
    posi = small("pos_i", [P, TT], I32)
    posf = small("pos_f", [P, TT])
    invf = small("inv_freq", [P, ROT])
    rope = small("rope", [P, 6, TT * ROT])
    mx = small("row_max", [P, 64])
    nmx = small("neg_max", [P, 64])
    ssum = small("row_sum", [P, 64])
    rsum = small("row_rcp", [P, 64])
    e_id = small("expert_id", [P, NE])
    g_id = small("group_id", [P, NE])
    em15 = small("over_base", [P, NE])
    k_id = small("over_id", [P, MAX_OVER])
    tok = small("token_id", [P, TT], I32)
    empty = small("no_token", [P, NBLK], I32)
    slot_tok = small("slot_token", [P, NBLK], I32)
    gpad = small("group_pad", [P, TT, 8])
    mx8 = small("max8", [P, TT, 8])
    ix8 = small("index8", [P, TT, 8], U32)
    comb_w = small("combine_w", [P, 2, TT])
    yrow = small("y_row", [P, 2, TT], I32)
    trow = small("table_row", [P, 2, TT], I32)
    ytmp = small("y_tmp", [P, 2, 8], I32)
    dst = small("dest", [P, 2, TT])
    info = small("over_info", [P, 8], I32)
    hot = small("hot_b", [P, TT, NE], BF16)
    idx = [small(f"gather_idx{i}", [P, 1], I32) for i in range(2)]

    xn_dram = nc.dram_tensor("xn_rows", [S, D], F32, kind="Internal").ap()
    y_dram = nc.dram_tensor("y_rows", [NBLK * P, D], F32, kind="Internal").ap()
    tables = [nc.dram_tensor(f"slot_table{l}", [P * NBLK, 1], I32, kind="Internal").ap() for l in range(LAYERS)]

    x_loaded = sem("x_loaded")
    params_loaded = sem("params_loaded")
    bd_loaded = sem("bd_loaded")
    g_bias_loaded = [sem(f"g_bias_loaded{i}") for i in range(4)]
    slab_filled = [sem(f"slab_filled{i}") for i in range(RING)]
    mod_filled = [sem(f"mod_filled{i}") for i in range(MOD_RING)]
    mod_used = sem("mod_used")
    dve_step, act_step, pool_step = sem("dve_step"), sem("act_step"), sem("pool_step")
    consts_ready = sem("consts_ready")
    bd_zeroed = sem("bd_zeroed")
    mask_base = sem("mask_base")
    mask_ready = sem("mask_ready")
    cs_ready = sem("cs_ready")
    cols_turned = sem("cols_turned")
    cols_ready = sem("cols_ready")
    lam_abs, lam_exp = sem("lam_abs"), sem("lam_exp")
    angle_ready, rope_ready = sem("angle_ready"), sem("rope_ready")
    dec_ready = sem("dec_ready")
    x_ready = sem("x_ready")
    rms_ready = sem("rms_ready")
    xn_ready = sem("xn_ready")
    xn_turned = sem("xn_turned")
    ht_act, ht_dve = sem("ht_act"), sem("ht_dve")
    acc_ready, mod_reduced, mod_done = sem("acc_ready"), sem("mod_reduced"), sem("mod_done")
    z_ready, z_act, z_dve = sem("z_ready"), sem("z_act"), sem("z_dve")
    xr_ready, gate_ready, gate_read = sem("xr_ready"), sem("gate_ready"), sem("gate_read")
    m_ready, mult_ready, scan_done = sem("m_ready"), sem("mult_ready"), sem("scan_done")
    mix_ready = sem("mix_ready")
    y_ready = sem("y_ready")
    logit_ready, score_ready = sem("logit_ready"), sem("score_ready")
    hot_ready, rank_ready, route_ready = sem("hot_ready"), sem("rank_ready"), sem("route_ready")
    xn_stored, table_filled, table_set, table_back = sem("xn_stored"), sem("table_filled"), sem("table_set"), sem("table_back")
    xs_filled = [sem("xs_filled0"), sem("xs_filled1")]
    xs_turned, xst_act, xst_dve = sem("xs_turned"), sem("xst_act"), sem("xst_dve")
    gate_done, up_done, silu_done = sem("gate_done"), sem("up_done"), sem("silu_done")
    hid_ready, hid_turned, hidt_ready = sem("hid_ready"), sem("hid_turned"), sem("hidt_ready")
    down_done, yb_ready = sem("down_done"), sem("yb_ready")
    yb_stored = [sem("yb_stored0"), sem("yb_stored1")]
    over_done = sem("over_done")
    turn_seen = sem("turn_seen")
    y_zeroed = sem("y_zeroed")
    comb_filled = [sem(f"comb_filled{t}") for t in range(TT)]
    over = [{n: sem(f"over{l}_{n}") for n in ("wg", "wu", "wd", "xs", "turned", "xst", "gu", "silu", "hid", "hidt_in", "hidt", "down", "yb", "stored", "step", "over", "seen", "gate")}
            for l in range(LAYERS)]
    qkv_ready, qkv_act, qkv_dve = sem("qkv_ready"), sem("qkv_act"), sem("qkv_dve")
    rot_ready, qt_turned, kt_turned, qt_ready, kt_ready = (sem(n) for n in ("rot_ready", "qt_turned", "kt_turned", "qt_ready", "kt_ready"))
    s_ready, max_ready, p_ready, p_turned = sem("s_ready"), sem("max_ready"), sem("p_ready"), sem("p_turned")
    pt_act, pt_dve, av_ready, o_ready = sem("pt_act"), sem("pt_dve"), sem("av_ready"), sem("o_ready")
    o_turned, ot_act, ot_dve = sem("o_turned"), sem("ot_act"), sem("ot_dve")
    fg_loaded = sem("fg_loaded")
    final_ready, out_stored = sem("final_ready"), sem("out_stored")

    fills = [0] * RING
    place = {}

    def plan(name, slot, times=1):
        fills[slot] += 1
        place[name] = (slot, fills[slot])
        fills[slot] += times - 1

    for g in range(5):
        plan(("in", g), g)
    plan(("out", 0), 5)
    plan(("out", 1), 0)
    EXP_SLOT = {(c, par): (1 + 3 * par + c) % RING for c in range(3) for par in range(2)}
    for l in range(LAYERS):
        if l == 1:
            for w in range(6):
                plan(("qkv", w), (4, 5, 0, 1, 2, 3)[w])
            plan(("o", 0), 5)
            plan(("o", 1), 0)
        for (c, par), slot in EXP_SLOT.items():
            plan(("exp", l, c, par), slot, NE // 2)
    MOD1_SLOT = 4

    def slab(name):
        return ring[:, place[name][0], :, :]

    def wait_slab(eng, name, turn=0):
        slot, times = place[name]
        eng.wait_ge(slab_filled[slot], turn * 16 + 16 * times)

    IN_ORDER = [4, 3, 2, 0, 1]
    MOD_SPLIT = 8
    mod1_slot = [ring[:, MOD1_SLOT, 2 * i:2 * i + 2, :] for i in range(MOD_RING)]

    def mod_place(g):
        return (mod_slot if g < MOD_SPLIT * MOD_QUARTERS else mod1_slot)[g % MOD_RING]

    def z_bank(t):
        return t if t < 4 else t - 14 if 14 <= t < 18 else 4 + t % 2

    def pair(bank):
        return ps[:, bank:bank + 2, :].rearrange("p a n -> p (a n)")

    def pk(w):
        return w.rearrange("(p k) n -> p k n", p=P)

    def kp(w):
        return w.rearrange("(k p) n -> p k n", p=P)

    w_in, w_out = pk(a["w_in_ab"][0]), kp(a["w_out_ab"][0])
    w_qkv, w_o = pk(a["w_qkv"][0]), kp(a["w_o"][0])

    block = ctx.enter_context(nc.Block())

    @block.sync
    def _(sp):
        def load_slab(name, src):
            sp.dma_start(slab(name), src).then_inc(slab_filled[place[name][0]], 16)

        def load_mod(n):
            l, q = part_of(n)
            for m in range(MOD_QUARTERS):
                half, kt = m // 4, 2 * (m % 4)
                g = n * MOD_QUARTERS + m
                if g >= MOD_RING:
                    sp.wait_ge(mod_used, g - MOD_RING + 1)
                src = pk(a["mod_w"][l])[:, kt:kt + 2, q * D + half * HALF:q * D + half * HALF + HALF]
                sp.dma_start(mod_place(g), src).then_inc(mod_filled[g % MOD_RING], 16)

        def load_gate_bias(n):
            l, q = part_of(n)
            g = 2 * l + q // 5
            sp.dma_start(G[:, g, :], a["mod_b"][l, q * D:(q + 1) * D].unsqueeze(0).to_broadcast([P, D])).then_inc(g_bias_loaded[g], 16)

        def part_src(l, c, e):
            if c < 2:
                return a[("expert_w_gate", "expert_w_up")[c]][l, bass.ds(e, 1)].rearrange("e (p k) n -> p (e k) n", p=P)
            return a["expert_w_down"][l, bass.ds(e, 1)].rearrange("e (k p) n -> p (e k) n", p=P)

        def part_dst(c, par):
            dst_ap = ring[:, EXP_SLOT[c, par], :, :]
            return dst_ap if c < 2 else dst_ap.rearrange("p (f h) n -> p f (h n)", h=2)

        def load_part(l, c, e, par):
            sp.dma_start(part_dst(c, par), part_src(l, c, e)).then_inc(slab_filled[EXP_SLOT[c, par]], 16)

        load_mod(0)
        sp.dma_start(X[:, :, :], a["x"][0].rearrange("(t p) d -> p t d", p=P)).then_inc(x_loaded, 16)
        load_mod(1)
        for g in range(5):
            load_slab(("in", g), w_in[:, :, IN_ORDER[g] * HALF:IN_ORDER[g] * HALF + HALF])
        load_slab(("out", 0), w_out[:, :, 0:HALF])
        load_gate_bias(2)
        load_gate_bias(5)
        for n in range(2, MOD_SPLIT):
            load_mod(n)
            if n == 4:
                sp.wait_ge(z_ready, 4)
                load_slab(("out", 1), w_out[:, :, HALF:D])

        def stream_experts(l):
            e0 = l * NE
            free = {0: [(z_ready, 8), (z_ready, 12), (z_ready, 16), (z_ready, 20), (y_ready, 8), (y_ready, 8)],
                    1: [(qkv_ready, 16), (qkv_ready, 20), (qkv_ready, 24), (mod_used, LAYERS * PARTS * MOD_QUARTERS), (y_ready, 16), (y_ready, 16)]}[l]
            for e in range(2):
                for c in range(3):
                    sp.wait_ge(*free[3 * e + c])
                    load_part(l, c, e, e)

            def refill(pair, par, more, first=False):
                e = 2 * pair + par
                if more:
                    sp.wait_ge(gate_done, e + (e0 + 1))
                    load_part(l, 0, e + 2, par)
                if not first:
                    sp.wait_ge(down_done, e + e0)
                    load_part(l, 2, e + 1, 1 - par)
                if more:
                    sp.wait_ge(up_done, e + (e0 + 1))
                    load_part(l, 1, e + 2, par)
                if not first:
                    store(e - 1, 1 - par)

            def store(e, par):
                sp.wait_ge(yb_ready, e + (e0 + 1))
                sp.dma_start(y_dram[bass.ds(e * P, P), :], ybuf[par]).then_inc(yb_stored[par], 16)

            refill(0, 0, True, first=True)
            refill(0, 1, True)
            with sp.Fori(1, NE // 2 - 1) as i:
                refill(i, 0, True)
                refill(i, 1, True)
            refill(NE // 2 - 1, 0, False)
            o = over[l]
            n_over = sp.value_load(info[0:1, 7:8], min_val=0, max_val=MAX_OVER)

            def load_over(k, name, c):
                ex = sp.value_load(info[0:1, bass.ds(k, 1)], min_val=0, max_val=NE - 1)
                sp.dma_start(part_dst(c, 0), part_src(l, c, ex)).then_inc(o[name], 16)

            sp.wait_ge(gate_done, e0 + NE - 1)
            sp.wait_ge(up_done, e0 + NE - 1)
            with sp.If(n_over > 0):
                load_over(0, "wg", 0)
                load_over(0, "wu", 1)
            sp.wait_ge(down_done, e0 + NE - 1)
            with sp.If(n_over > 0):
                load_over(0, "wd", 2)
                sp.sem_inc(o["stored"], 16)
            store(NE - 2, 0)
            if l == 0:
                for w, used in enumerate((gate_done, up_done, down_done)):
                    sp.wait_ge(used, e0 + NE)
                    load_slab(("qkv", w), w_qkv[:, :, w * HALF:(w + 1) * HALF])
            store(NE - 1, 1)
            with sp.Fori(0, MAX_OVER) as k:
                with sp.If(k + 1 < n_over):
                    ex = sp.value_load(info[0:1, bass.ds(k + 1, 1)], min_val=0, max_val=NE - 1)
                    for c, name, used in ((0, "wg", "gate"), (1, "wu", "gu"), (2, "wd", "down")):
                        sp.wait_ge(o[used], k + 1)
                        sp.dma_start(part_dst(c, 0), part_src(l, c, ex)).then_inc(o[name], 16)
                with sp.If(k < n_over):
                    sp.wait_ge(o["yb"], k + 1)
                    sp.dma_start(y_dram[bass.ds((k + NE) * P, P), :], ybuf[0]).then_inc(o["stored"], 16)
                    sp.wait_ge(o["stored"], (k + 2) * 16)
                    sp.sem_inc(o["over"], 1)
            for par in range(2):
                sp.wait_ge(yb_stored[par], 16 * (NE // 2) * (l + 1))
            sp.sem_inc(over_done, 1)
            if l == 0:
                for w in range(3, 6):
                    load_slab(("qkv", w), w_qkv[:, :, w * HALF:(w + 1) * HALF])

        stream_experts(0)
        load_gate_bias(8)
        load_gate_bias(11)
        sp.wait_ge(qkv_ready, 4)
        load_mod(8)
        load_mod(9)
        sp.wait_ge(qkv_ready, 8)
        load_slab(("o", 0), w_o[:, :, 0:HALF])
        load_mod(10)
        load_mod(11)
        sp.wait_ge(qkv_ready, 12)
        load_slab(("o", 1), w_o[:, :, HALF:D])
        stream_experts(1)
        for t in range(TT):
            sp.wait_ge(final_ready, t + 1)
            sp.dma_start(out[0, t * P:(t + 1) * P, :], XN[:, t, :]).then_inc(out_stored, 16)
        sp.wait_ge(out_stored, 16 * TT)

    @block.gpsimd
    def _(gp):
        link = Link(gp, pool_step)
        link(gp.memset(ident[:, :], 0.0))
        link(gp.affine_select(out=ident[:, :], in_=ident[:, :], compare_op=ALU.not_equal, fill=1.0, base=0, pattern=[[-1, P]], channel_multiplier=1))
        link(gp.memset(ones[:, :], 1.0))
        link(gp.memset(BD, 0.0))
        gp.sem_inc(bd_zeroed, 1)
        link(gp.memset(ones_b[:, :], 1.0))
        link(gp.memset(eps[:, :], EPS))
        link(gp.affine_select(out=before[:, :], in_=ones_b[:, :], compare_op=ALU.is_gt, fill=0.0, base=0, pattern=[[1, P]], channel_multiplier=-1))
        for i in range(ROT):
            f = float(np.float32(ROPE_THETA) ** np.float32(-2.0 * i / (2 * ROT)))
            link(gp.memset(invf[:, i:i + 1], f))
        link(gp.iota(mlow, [[1, P]], base=P, channel_multiplier=-1))
        link(gp.iota(e_id[:, :], [[1, NE]], base=0, channel_multiplier=0, allow_small_or_imprecise_dtypes=True))
        link(gp.iota(g_id[:, :], [[1, NG], [0, EPG]], base=0, channel_multiplier=0, allow_small_or_imprecise_dtypes=True))
        link(gp.iota(em15[:, :], [[-1, NE]], base=NE - 1, channel_multiplier=0, allow_small_or_imprecise_dtypes=True))
        link(gp.iota(k_id[:, :], [[1, MAX_OVER]], base=0, channel_multiplier=0, allow_small_or_imprecise_dtypes=True))
        link(gp.iota(tok[:, :], [[P, TT]], base=0, channel_multiplier=1))
        link(gp.iota(empty[:, :], [[0, NBLK]], base=NO_TOKEN, channel_multiplier=0))
        link(gp.memset(gpad[:, :, :], NEG))
        gp.sem_inc(consts_ready, 1)
        for l in range(LAYERS):
            gp.dma_start(tables[l].rearrange("(p b) o -> p (b o)", p=P), empty[:, :]).then_inc(table_filled, 16)

        gp.wait_ge(mask_base, 1)
        rep = LSPAN // P
        wide = lambda i: mflt[:, i, :].unsqueeze(1).to_broadcast([P, rep, P])
        part = R[:, 8:10, :].rearrange("p a n -> p (a n)")[:, 0:LSPAN]
        lcv = LC[:, :].rearrange("p (r n) -> p r n", n=P)
        link(gp.tensor_copy(lcv, wide(0)))
        for i, radius in ((1, 256), (2, 64)):
            link(gp.tensor_copy(part.rearrange("p (r n) -> p r n", n=P), wide(i)))
            link(gp.affine_select(out=part, in_=part, compare_op=ALU.is_ge, fill=0.0, base=radius + (TT - 1) * P, pattern=[[-1, LSPAN]], channel_multiplier=1))
            link(gp.affine_select(out=part, in_=part, compare_op=ALU.is_ge, fill=0.0, base=radius - (TT - 1) * P, pattern=[[1, LSPAN]], channel_multiplier=-1))
            link(gp.tensor_tensor(LC[:, :], LC[:, :], part, ALU.add))
        gp.sem_inc(mask_ready, 1)

        zeros = R[:, 8:10, :].rearrange("p a n -> p (a n)")
        gp.wait_ge(scan_done, LRU_TILES)
        link(gp.memset(zeros, 0.0))
        gp.wait_ge(y_ready, 1)
        for b in range(NE, NBLK):
            gp.dma_start(y_dram[b * P:(b + 1) * P, :], zeros).then_inc(y_zeroed, 16)
        gp.wait_ge(y_zeroed, 16 * MAX_OVER)

        def gathers(l):
            e0 = l * NE
            gp.wait_ge(xn_ready, 4 * (2 * l + 2))
            link(gp.memset(R[:, 0:4, :], 0.0))
            gp.wait_ge(route_ready, l + 1)
            gp.wait_ge(table_filled, 16 * LAYERS)
            for j in range(2):
                for t in range(TT):
                    gp.indirect_dma_start(out=tables[l], out_offset=bass.IndirectOffsetOnAxis(ap=trow[:, j, t:t + 1], axis=0),
                                          in_=tok[:, t:t + 1], in_offset=None, bounds_check=P * NBLK - 1,
                                          oob_is_err=False).then_inc(table_set, 16)
            gp.wait_ge(table_back, 16 * (l + 1))
            gp.wait_ge(xn_stored, 16 * TT * (l + 1))

            def gather(col, buf, done):
                link(gp.tensor_copy(idx[buf][:, :], slot_tok[:, bass.ds(col, 1)]))
                gp.sem_inc(turn_seen, 1)
                gp.indirect_dma_start(out=xs[buf], out_offset=None, in_=xn_dram,
                                      in_offset=bass.IndirectOffsetOnAxis(ap=idx[buf][:, 0:1], axis=0),
                                      bounds_check=S - 1, oob_is_err=False).then_inc(done, 16)

            gather(0, 0, xs_filled[0])
            gather(1, 1, xs_filled[1])
            with gp.Fori(0, NE // 2 - 1) as i:
                link.enter_loop(i, 0, 2)
                for par in range(2):
                    gp.wait_ge(xs_turned, 2 * i + (par + e0 + 1))
                    gp.sem_inc(turn_seen, 1)
                    gather(2 * i + (par + 2), par, xs_filled[par])
                link.leave_loop(0, NE // 2 - 1)

            o = over[l]
            n_over = gp.value_load(info[0:1, 7:8], min_val=0, max_val=MAX_OVER)
            gp.wait_ge(xs_turned, e0 + NE - 1)

            def gather_over(k):
                gp.tensor_copy(idx[0][:, :], slot_tok[:, bass.ds(k + NE, 1)]).then_inc(o["step"], 1)
                gp.wait_ge(o["step"], k + 1)
                gp.sem_inc(o["seen"], 1)
                gp.indirect_dma_start(out=xs[0], out_offset=None, in_=xn_dram,
                                      in_offset=bass.IndirectOffsetOnAxis(ap=idx[0][:, 0:1], axis=0),
                                      bounds_check=S - 1, oob_is_err=False).then_inc(o["xs"], 16)

            with gp.If(n_over > 0):
                gather_over(0)
            with gp.Fori(0, MAX_OVER - 1) as k:
                with gp.If(k + 1 < n_over):
                    gp.wait_ge(o["turned"], k + 1)
                    gp.sem_inc(o["seen"], 1)
                    gather_over(k + 1)
            gp.wait_ge(over_done, l + 1)
            for t in range(TT):
                for j in range(2):
                    gp.indirect_dma_start(out=comb[j][t], out_offset=None, in_=y_dram,
                                          in_offset=bass.IndirectOffsetOnAxis(ap=yrow[:, j, t:t + 1], axis=0),
                                          bounds_check=NBLK * P - 1, oob_is_err=False).then_inc(comb_filled[t], 16)

        gathers(0)
        gathers(1)

    @block.scalar
    def _(act):
        link = Link(act, act_step)
        def load(dst_ap, src):
            act.dma_start(dst_ap, src).then_inc(params_loaded, 16)

        with nc.allow_non_contiguous_dma(reason="512 positions, once"):
            load(cT[:, :], a["c"][0].rearrange("(p k) -> p k", k=KT))
            load(mbc[:, :, :], a["mod_b"].rearrange("l (q p k) -> p (l q) k", p=P, k=KT))
            load(gcols[:, :, 0, :], a["norm_mix_g"].rearrange("l (p k) -> p l k", k=KT))
            load(gcols[:, :, 1, :], a["norm_ffn_g"].rearrange("l (p k) -> p l k", k=KT))
            load(rows[0:12, :], a["conv_a_w"][0].rearrange("k (j n) -> (k j) n", n=P))
            load(rows[12:28, :], a["conv_b_w"][0].rearrange("k (j n) -> (k j) n", n=P))
            load(rows[28:32, :], a["conv_b_b"][0].rearrange("(j n) -> j n", n=P))
            load(rows[32:40, :], a["lru_ba"][0].rearrange("d (j n) -> (d j) n", n=P))
            load(rows[40:48, :], a["lru_bx"][0].rearrange("d (j n) -> (d j) n", n=P))
            load(rows[48:56, :], a["lru_lambda"][0].rearrange("d (j n) -> (d j) n", n=P))
            load(posi[:, :], a["positions"][0].rearrange("(t p) -> p t", p=P))
            load(rw[:, :, :], a["router_w"].rearrange("(p k) e -> p k e", k=KT))
            load(rb[:, :], a["router_bias"].unsqueeze(0).to_broadcast([P, NE]))
            act.wait_ge(bd_zeroed, 1)
            for d in range(2):
                for w, name in enumerate(("lru_wa", "lru_wx")):
                    src = a[name][0, d].rearrange("(j two) i o -> two i j o", two=2)
                    b0 = (d * 2 + w) * LRU_TILES
                    for two in range(2):
                        act.dma_start(BD[two * 64:(two + 1) * 64, b0:b0 + LRU_TILES, two * 64:(two + 1) * 64], src[two]).then_inc(bd_loaded, 16)
        act.wait_ge(params_loaded, 16 * 13)
        act.activation(cs[:, :], cT[:, :], ACT.Silu).then_inc(cs_ready, 1)
        act.wait_ge(angle_ready, 1)
        act.activation(rope[:, 4, :], rope[:, 2, :], ACT.Sin).then_inc(rope_ready, 1)
        act.activation(rope[:, 5, :], rope[:, 3, :], ACT.Sin).then_inc(rope_ready, 1)

        def rms(s, t):
            if s == 0:
                act.wait_ge(x_loaded, 16)
            else:
                act.wait_ge(x_ready, TT * (s - 1) + t + 1)
            if s == 1 and t == 0:
                act.wait_ge(mod_used, MOD_SPLIT * MOD_QUARTERS)
            link(act.activation(xnorm[s][:, t, :], X[:, t, :], ACT.Square, accum_out=stats[:, 0, t:t + 1]))
            act.activation(stats[:, 1, t:t + 1], stats[:, 0, t:t + 1], ACT.Sqrt, scale=1.0 / D, bias=eps[:, 0:1]).then_inc(rms_ready, 1)

        def take_ht(s, t):
            if s == 0:
                act.wait_ge(mod_done, 2)
            act.wait_ge(xn_turned, TT * s + t + 1)
            for kt in range(4):
                ins = act.activation(HT[:, kt, t * P:(t + 1) * P], ps[:, 2 * t, kt * P:(kt + 1) * P], ACT.Identity, bias=AB[:, s, 1, kt:kt + 1], scale=AB[:, s, 0, kt:kt + 1])
            ins.then_inc(ht_act, 1)

        act.wait_ge(consts_ready, 1)
        for t in range(TT):
            rms(0, t)
        for t in range(TT):
            take_ht(0, t)
        act.wait_ge(lam_abs, 1)
        act.activation(lru[:, 1, :], lru[:, 0, :], ACT.Exp, scale=-1.0).then_inc(lam_exp, 1)
        for j in range(LRU_TILES):
            act.wait_ge(z_ready, j + 1)
            if j:
                act.wait_ge(xr_ready, j)
            act.activation(u_in, ps[:, j, :], ACT.Copy).then_inc(z_act, 1)
        act.wait_ge(mask_ready, 1)
        act.wait_ge(dec_ready, 1)

        def take_z(t):
            j = t % 4
            act.wait_ge(z_ready, t + 1)
            act.activation(mixT[:, LRU_TILES + j if t < 8 else j, :], ps[:, z_bank(t), :], ACT.Gelu_apprx_tanh if t < 8 else ACT.Copy).then_inc(z_act, 1)

        for j in range(LRU_TILES):
            take_z(4 + 2 * j)
            act.wait_ge(gate_ready, j + 1)
            if j:
                act.wait_ge(scan_done, j)
            for d in range(2):
                c = d * LRU_TILES + j
                link(act.activation(th[d], ps[:, 2 * d, :], ACT.Tanh, bias=hbias[:, c:c + 1], scale=0.5))
                link(act.activation(ti[d], ps[:, 2 * d + 1, :], ACT.Tanh, bias=hbias[:, 8 + c:9 + c], scale=0.5))
                if d == 1:
                    act.sem_inc(gate_read, 1)
                link(act.activation(av[d], th[d], ACT.Exp, bias=dec[:, 0, c:c + 1], scale=dec[:, 0, c:c + 1]))
                act.activation(th[d], th[d], ACT.Tanh, bias=dec[:, 1, c:c + 1], scale=dec[:, 1, c:c + 1]).then_inc(m_ready, 1)
            take_z(5 + 2 * j)
            for d in range(2):
                act.wait_ge(mult_ready, 4 * j + d + 1)
                act.activation(th[d], th[d], ACT.Sqrt, scale=0.25).then_inc(m_ready, 1)

        def experts(l):
            s = 2 * l + 1
            e0 = l * NE
            for t in range(TT + 1):
                if t < TT:
                    rms(s, t)
                if t:
                    take_ht(s, t - 1)
                    act.dma_start(xn_dram[(t - 1) * P:t * P, :], xnorm[s][:, t - 1, :]).then_inc(xn_stored, 16)
            act.wait_ge(logit_ready, l + 1)
            act.activation(rt[:, 0:TT * NE], ps[:, 0, 0:TT * NE], ACT.Sigmoid).then_inc(score_ready, 1)
            if l == 1:
                act.dma_start(G[:, 0, :], a["final_norm_g"].unsqueeze(0).to_broadcast([P, D])).then_inc(fg_loaded, 16)
            act.wait_ge(table_set, 16 * 8 * (l + 1))
            act.dma_start(slot_tok[:, :], tables[l].rearrange("(p b) o -> p (b o)", p=P)).then_inc(table_back, 16)

            def xst(e, par, first=False):
                if not first:
                    act.wait_ge(up_done, e + (e0 - 1))
                act.wait_ge(xs_turned, e + (e0 + 1))
                for kt in range(4):
                    ins = act.activation(xsT[par][:, kt, :], ps[:, 0, kt * P:(kt + 1) * P], ACT.Identity, bias=AB[:, s, 1, kt:kt + 1], scale=AB[:, s, 0, kt:kt + 1])
                ins.then_inc(xst_act, 1)

            def take_hid(e, first=False):
                act.wait_ge(hid_turned, e + (e0 + 1))
                if not first:
                    act.wait_ge(down_done, e + e0)
                act.activation(hidT, ps[:, 4, :].rearrange("p (f n) -> p f n", n=P), ACT.Copy).then_inc(hidt_ready, 1)

            def step(e, par, first=0, last=False):
                if first != 1:
                    take_hid(e - 1, first == 2)
                act.wait_ge(gate_done, e + (e0 + 1))
                if first != 1:
                    act.wait_ge(hid_ready, e + e0)
                act.activation(sg, ps[:, 2, :], ACT.Silu).then_inc(silu_done, 1)
                if not last:
                    xst(e + 1, 1 - par, first == 1)

            xst(0, 0, True)
            step(0, 0, first=1)
            step(1, 1, first=2)
            with act.Fori(1, NE // 2 - 1) as i:
                for par in range(2):
                    step(2 * i + par, par)
            step(NE - 2, 0)
            step(NE - 1, 1, last=True)
            take_hid(NE - 1)

            o = over[l]
            act.wait_ge(route_ready, l + 1)
            n_over = act.value_load(info[0:1, 7:8], min_val=0, max_val=MAX_OVER)
            with act.Fori(0, MAX_OVER) as k:
                with act.If(k < n_over):
                    act.wait_ge(o["turned"], k + 1)
                    for kt in range(4):
                        ins = act.activation(xsT[0][:, kt, :], ps[:, 0, kt * P:(kt + 1) * P], ACT.Identity, bias=AB[:, s, 1, kt:kt + 1], scale=AB[:, s, 0, kt:kt + 1])
                    ins.then_inc(o["xst"], 1)
                    act.wait_ge(o["gate"], k + 1)
                    act.activation(sg, ps[:, 2, :], ACT.Silu).then_inc(o["silu"], 1)
                    act.wait_ge(o["hidt_in"], k + 1)
                    act.activation(hidT, ps[:, 4, :].rearrange("p (f n) -> p f n", n=P), ACT.Copy).then_inc(o["hidt"], 1)

        experts(0)
        for t in range(TT):
            rms(2, t)
        for t in range(TT):
            take_ht(2, t)
        for w in range(6):
            dest = (Q, K, V)[w // 2]
            for t in (0, 2):
                act.wait_ge(qkv_ready, 4 * w + t + 1)
                act.activation(dest[:, t, (w % 2) * HALF:(w % 2) * HALF + HALF], ps[:, (4 * w + t) % 6, :], ACT.Copy).then_inc(qkv_act, 1)
        for hp in range(8):
            act.wait_ge(qt_turned, hp + 1)
            act.activation(QT[:, hp, :], ps[:, (2 * hp) % 8, :], ACT.Copy).then_inc(qt_ready, 1)

        def exp_step(v):
            act.wait_ge(max_ready, v + 1)
            act.activation(prob[v % 4], prob[v % 4], ACT.Exp, bias=nmx[:, v:v + 1], accum_out=ssum[:, v:v + 1]).then_inc(p_ready, 1)

        exp_step(0)
        exp_step(1)
        for u in range(64):
            if u + 2 < 64:
                exp_step(u + 2)
            if u % 2 == 0:
                act.wait_ge(p_turned, u + 1)
                if u >= 4:
                    act.wait_ge(av_ready, u - 3)
                act.activation(probT[u % 4], ps[:, 3 + u % 2, :], ACT.Copy).then_inc(pt_act, 1)
        for kt in range(0, KT, 2):
            act.wait_ge(o_turned, kt + 1)
            act.activation(OT[:, kt, :], ps[:, kt, :], ACT.Copy).then_inc(ot_act, 1)
        experts(1)
        for t in range(TT):
            rms(4, t)

    @block.vector
    def _(v):
        link = Link(v, dve_step)
        ts, tt_, stt = v.tensor_scalar, v.tensor_tensor, v.scalar_tensor_tensor

        v.wait_ge(consts_ready, 1)
        mi = mlow
        mtmp = mflt[:, 3, :].bitcast(I32)
        m16, m4 = mflt[:, 0, :], mflt[:, 1, :]
        link(ts(mtmp, mi, 15, None, ALU.bitwise_and))
        link(ts(m16, mtmp, 0, None, ALU.is_equal))
        link(ts(mtmp, mi, 3, None, ALU.bitwise_and))
        link(ts(m4, mtmp, 0, None, ALU.is_equal))
        L2, L3 = 8.0 * float(np.log(2.0)), 8.0 * float(np.log(3.0))
        f2 = mflt[:, 2, :]
        t3 = mflt[:, 3, :]
        link(ts(f2, m16, L3 - L2, None, ALU.mult))
        link(stt(f2, m4, L2, f2, ALU.mult, ALU.add))
        link(ts(t3, m4, -NEG, NEG, ALU.mult, ALU.add))
        link(stt(t3, m16, L2, t3, ALU.mult, ALU.add))
        link(tt_(f2, f2, t3, ALU.subtract))
        link(ts(m16, m16, -NEG, NEG, ALU.mult, ALU.add))
        link(tt_(m4, t3, m16, ALU.subtract))
        v.sem_inc(mask_base, 1)

        v.wait_ge(params_loaded, 16 * 13)
        link(v.tensor_copy(posf[:, :], posi[:, :]))
        ang, nn, red, co = (rope[:, i, :] for i in range(4))
        as3 = lambda x: x.rearrange("p (t r) -> p t r", r=ROT)
        link(tt_(as3(ang), posf[:, :].unsqueeze(2).to_broadcast([P, TT, ROT]), invf[:, :].unsqueeze(1).to_broadcast([P, TT, ROT]), ALU.mult))
        link(ts(nn, ang, float(1.0 / (2.0 * np.pi)), MAGIC, ALU.mult, ALU.add))
        link(ts(nn, nn, -MAGIC, None, ALU.add))
        two_pi = 2.0 * np.pi
        c1 = 6.28125
        c2 = float(np.float32(int((two_pi - c1) * 2 ** 20) / 2 ** 20))
        c3 = float(two_pi - c1 - c2)
        link(stt(red, nn, -c1, ang, ALU.mult, ALU.add))
        link(stt(red, nn, -c2, red, ALU.mult, ALU.add))
        link(stt(red, nn, -c3, red, ALU.mult, ALU.add))
        link(ts(red, red, 3.1415925, -3.1415925, ALU.min, ALU.max))
        link(ts(co, red, -1.0, None, ALU.mult))
        link(tt_(co, co, red, ALU.max))
        link(ts(co, co, -1.0, float(np.pi / 2), ALU.mult, ALU.add))
        v.sem_inc(angle_ready, 1)

        def mod_acc(n, m0, count):
            for m in range(m0, m0 + count):
                g = n * MOD_QUARTERS + m
                half, kt = m // 4, 2 * (m % 4)
                dest = acc[n % 2][:, half * HALF:half * HALF + HALF]
                w = mod_place(g)
                v.wait_ge(mod_filled[g % MOD_RING], 16 * (g // MOD_RING + 1))
                if kt == 0:
                    link(ts(dest, w[:, 0, :], cs[:, 0:1], None, ALU.mult))
                else:
                    link(stt(dest, w[:, 0, :], cs[:, kt:kt + 1], dest, ALU.mult, ALU.add))
                stt(dest, w[:, 1, :], cs[:, kt + 1:kt + 2], dest, ALU.mult, ALU.add).then_inc(mod_used, 1)
                v.wait_ge(mod_used, g + 1)
            if m0 + count == MOD_QUARTERS:
                v.sem_inc(acc_ready, 1)

        def mod_take(n):
            l, q = part_of(n)
            v.wait_ge(mod_reduced, n + 1)
            if q in (2, 5):
                g = 2 * l + q // 5
                v.wait_ge(g_bias_loaded[g], 16)
                link(tt_(G[:, g, 0:HALF], ps[:, 6, :], G[:, g, 0:HALF], ALU.add))
                tt_(G[:, g, HALF:D], ps[:, 7, :], G[:, g, HALF:D], ALU.add).then_inc(mod_done, 1)
            else:
                w = 2 * l + q // 3
                if q % 3 == 0:
                    tt_(AB[:, w, 1, :], ps[:, 7, 0:KT], mbc[:, n, :], ALU.add).then_inc(mod_done, 1)
                else:
                    link(tt_(AB[:, w, 0, :], ps[:, 7, 0:KT], mbc[:, n, :], ALU.add))
                    stt(AB[:, w, 0, :], AB[:, w, 0, :], 1.0, gcols[:, l, q // 3, :], ALU.add, ALU.mult).then_inc(mod_done, 1)
            v.wait_ge(mod_done, n + 1)

        def scale_x(s, t):
            v.wait_ge(rms_ready, TT * s + t + 1)
            r = stats[:, 2, t:t + 1]
            link(v.reciprocal(r, stats[:, 1, t:t + 1]))
            if s < 4:
                ts(xnorm[s][:, t, :], X[:, t, :], r, None, ALU.mult).then_inc(xn_ready, 1)
            else:
                if t == 0:
                    v.wait_ge(fg_loaded, 16)
                stt(XN[:, t, :], X[:, t, :], r, G[:, 0, :], ALU.mult, ALU.mult).then_inc(final_ready, 1)

        def take_ht(s, t):
            v.wait_ge(xn_turned, TT * s + t + 1)
            for kt in range(4, KT):
                ins = ts(HT[:, kt, t * P:(t + 1) * P], ps[:, 2 * t + 1, (kt - 4) * P:(kt - 3) * P], AB[:, s, 0, kt:kt + 1], AB[:, s, 1, kt:kt + 1], ALU.mult, ALU.add)
            ins.then_inc(ht_dve, 1)

        v.wait_ge(cs_ready, 1)
        mod_acc(0, 0, 8)
        for t in range(TT):
            scale_x(0, t)
        mod_take(0)
        mod_acc(1, 0, 8)
        mod_take(1)
        for t in range(TT):
            take_ht(0, t)

        v.wait_ge(cols_turned, 1)
        link(v.tensor_copy(cols[:, :], ps[:, 7, 64:120]))
        v.sem_inc(cols_ready, 1)
        link(ts(hbias[:, :], cols[:, 32:48], 0.5, None, ALU.mult))
        lam = cols[:, 48:56]
        link(ts(lru[:, 0, :], lam, -1.0, None, ALU.mult))
        link(tt_(lru[:, 0, :], lru[:, 0, :], lam, ALU.max))
        v.sem_inc(lam_abs, 1)
        v.wait_ge(lam_exp, 1)
        e_, s_, t_, y_ = lru[:, 1, :], lru[:, 2, :], lru[:, 3, :], lru[:, 4, :]
        link(ts(s_, e_, 2.0, None, ALU.add))
        link(v.reciprocal(s_, s_))
        link(tt_(s_, s_, e_, ALU.mult))
        link(tt_(t_, s_, s_, ALU.mult))
        link(ts(y_, t_, 1.0 / 17.0, None, ALU.mult))
        for k in range(15, 1, -2):
            link(stt(y_, y_, 1.0 / k, t_, ALU.add, ALU.mult))
        link(stt(y_, y_, 1.0, s_, ALU.add, ALU.mult))
        link(ts(t_, lam, -1.0, 0.0, ALU.mult, ALU.max))
        link(stt(t_, y_, 2.0, t_, ALU.mult, ALU.add))
        link(ts(dec[:, 0, :], t_, -4.0, None, ALU.mult))
        ts(dec[:, 1, :], t_, 4.0, None, ALU.mult).then_inc(dec_ready, 1)

        def col(i):
            return cols[:, i:i + 1]

        def conv_b(j):
            v.wait_ge(z_act, j + 1)
            u, x = u_in, xr[j]
            w = lambda k: col(12 + 4 * k + j)
            link(ts(x, u, w(1), col(28 + j), ALU.mult, ALU.add))
            link(stt(x[:, 1:S], u[:, 0:S - 1], w(0), x[:, 1:S], ALU.mult, ALU.add))
            link(stt(x[:, 0:S - 1], u[:, 1:S], w(2), x[:, 0:S - 1], ALU.mult, ALU.add))
            stt(x[:, 0:S - 2], u[:, 2:S], w(3), x[:, 0:S - 2], ALU.mult, ALU.add).then_inc(xr_ready, 1)
            v.wait_ge(xr_ready, j + 1)

        def gates_in(j):
            for d in range(2):
                v.wait_ge(m_ready, 4 * j + d + 1)
                link(tt_(tmp0, av[d], av[d], ALU.mult))
                stt(th[d], tmp0, 1.0, th[d], ALU.add, ALU.mult).then_inc(mult_ready, 1)
                v.wait_ge(mult_ready, 4 * j + d + 1)
                link(stt(ti[d], ti[d], 1.0, xr[j], ALU.add, ALU.mult))

        def gates_out(j):
            for d in range(2):
                v.wait_ge(m_ready, 4 * j + 2 + d + 1)
                link(tt_(ti[d], ti[d], th[d], ALU.mult))
                if d == 0:
                    x0, x1, o_ = av[0], ti[0], th[0]
                else:
                    x0, x1, o_ = av[1][:, ::-1], ti[1][:, ::-1], th[1][:, ::-1]
                v.tensor_tensor_scan(o_, x0, x1, 0.0, ALU.mult, ALU.add).then_inc(mult_ready, 1)
                v.wait_ge(mult_ready, 4 * j + 2 + d + 1)
            link(tt_(tmp0, th[0], th[1], ALU.add))
            v.sem_inc(scan_done, 1)
            tt_(mixT[:, LRU_TILES + j, :], mixT[:, LRU_TILES + j, :], tmp0, ALU.mult).then_inc(mix_ready, 1)
            v.wait_ge(mix_ready, j + 1)

        def val(j):
            t = 12 + j
            v.wait_ge(z_ready, t + 1)
            v.wait_ge(z_act, 8 + j + 1)
            m = mixT[:, j, :]
            tt_(m, ps[:, z_bank(t), :], m, ALU.mult).then_inc(z_dve, 1)
            v.wait_ge(z_dve, j + 1)
            c_ = xr[j]
            w = lambda k: col(4 * k + j)
            link(ts(c_, m, w(1), None, ALU.mult))
            link(stt(c_[:, 1:S], m[:, 0:S - 1], w(0), c_[:, 1:S], ALU.mult, ALU.add))
            link(stt(c_[:, 0:S - 1], m[:, 1:S], w(2), c_[:, 0:S - 1], ALU.mult, ALU.add))

        def gb(j):
            t = 16 + j
            v.wait_ge(z_ready, t + 1)
            tt_(mixT[:, j, :], ps[:, z_bank(t), :], xr[j], ALU.mult).then_inc(z_dve, 1)

        conv_b(0)
        conv_b(1)
        conv_b(2)
        mod_acc(2, 0, 2)
        conv_b(3)
        mod_acc(2, 2, 6)
        gates_in(0)
        mod_acc(3, 0, 3)
        gates_out(0)
        mod_acc(3, 3, 2)
        mod_take(2)
        gates_in(1)
        mod_acc(3, 5, 3)
        gates_out(1)
        mod_acc(4, 0, 2)
        gates_in(2)
        mod_acc(4, 2, 4)
        gates_out(2)
        mod_acc(4, 6, 2)
        mod_take(3)
        gates_in(3)
        mod_acc(5, 0, 3)
        gates_out(3)
        mod_acc(5, 3, 2)
        mod_take(4)
        val(0)
        mod_acc(5, 5, 3)
        val(1)
        mod_acc(6, 0, 2)
        mod_take(5)
        val(2)
        mod_acc(6, 2, 3)
        val(3)
        mod_acc(6, 5, 3)
        gb(0)
        mod_acc(7, 0, 2)
        gb(1)
        mod_acc(7, 2, 2)
        mod_take(6)
        gb(2)
        mod_acc(7, 4, 2)
        gb(3)
        mod_acc(7, 6, 2)

        def residual(l, t):
            v.wait_ge(y_ready, 8 * l + 2 * t + 2)
            link(tt_(pair(2 * t), pair(2 * t), G[:, 2 * l, :], ALU.mult))
            tt_(X[:, t, :], pair(2 * t), X[:, t, :], ALU.add).then_inc(x_ready, 1)
            v.wait_ge(x_ready, TT * 2 * l + t + 1)

        def route(l):
            n = TT * NE
            v.wait_ge(score_ready, l + 1)
            sc, bia, o1, o2 = (rt[:, i * n:(i + 1) * n] for i in range(4))
            t0, t1, t2 = (rt[:, i * n:(i + 1) * n] for i in range(4, 7))
            q64 = rt[:, 7 * n:8 * n]
            b0 = 8 * n
            hi, lo = rt[:, b0:b0 + 32], rt[:, b0 + 32:b0 + 64]
            hm, lm, h1 = (rt[:, b0 + 64 + 16 * i:b0 + 80 + 16 * i] for i in range(3))
            gi = rt[:, b0 + 112:b0 + 116]
            ef = rt[:, b0 + 120:b0 + 152]
            cnt, inc, exc, cmp_ = (rt[:, b0 + 160 + 16 * i:b0 + 176 + 16 * i] for i in range(4))
            cond = rt[:, b0 + 224:b0 + 224 + MAX_OVER * NE]
            sel = rt[:, b0 + 344:b0 + 352]
            s12 = rt[:, b0 + 352:b0 + 368]
            v3 = lambda x: x.rearrange("p (t e) -> p t e", t=TT)
            bc_e = lambda x: x.unsqueeze(1).to_broadcast([P, TT, NE])
            bc_t = lambda x: x.unsqueeze(2).to_broadcast([P, TT, NE])
            link(tt_(v3(bia), v3(sc), bc_e(rb[:, :]), ALU.add))
            link(tt_(hi, bia[:, 0:n:2], bia[:, 1:n:2], ALU.max))
            link(tt_(lo, bia[:, 0:n:2], bia[:, 1:n:2], ALU.min))
            link(tt_(hm, hi[:, 0:32:2], hi[:, 1:32:2], ALU.min))
            link(tt_(lm, lo[:, 0:32:2], lo[:, 1:32:2], ALU.max))
            link(tt_(h1, hi[:, 0:32:2], hi[:, 1:32:2], ALU.max))
            link(tt_(hm, hm, lm, ALU.max))
            link(tt_(gpad[:, :, 0:NG], h1.rearrange("p (t g) -> p t g", g=NG), hm.rearrange("p (t g) -> p t g", g=NG), ALU.add))
            for t in range(TT):
                link(v.max(mx8[:, t, :], gpad[:, t, :]))
                link(v.max_index(ix8[:, t, :], mx8[:, t, :], gpad[:, t, :]))
            link(v.tensor_copy(gi, ix8[:, :, 0]))
            link(tt_(v3(t0), bc_e(g_id[:, :]), bc_t(gi), ALU.is_equal))
            link(tt_(t1, bia, t0, ALU.mult))
            link(ts(t0, t0, -NEG, NEG, ALU.mult, ALU.add))
            link(tt_(t1, t1, t0, ALU.add))
            for t in range(TT):
                link(v.max(mx8[:, t, :], t1[:, t * NE:(t + 1) * NE]))
                link(v.max_index(ix8[:, t, :], mx8[:, t, :], t1[:, t * NE:(t + 1) * NE]))
            efv = ef.rearrange("p (t k) -> p t k", k=8)
            link(v.tensor_copy(efv, ix8[:, :, :]))
            link(tt_(v3(o1), bc_e(e_id[:, :]), bc_t(efv[:, :, 0]), ALU.is_equal))
            link(tt_(v3(o2), bc_e(e_id[:, :]), bc_t(efv[:, :, 1]), ALU.is_equal))
            tt_(hot[:, :, :], v3(o1), v3(o2), ALU.add).then_inc(hot_ready, 1)
            link(tt_(t0, o1, sc, ALU.mult))
            link(v.tensor_reduce(s12[:, 0:4], v3(t0), AX_X, ALU.add))
            link(tt_(t0, o2, sc, ALU.mult))
            link(v.tensor_reduce(s12[:, 4:8], v3(t0), AX_X, ALU.add))
            link(tt_(s12[:, 8:12], s12[:, 0:4], s12[:, 4:8], ALU.add))
            link(v.reciprocal(s12[:, 12:16], s12[:, 8:12]))
            link(tt_(comb_w[:, 0, :], s12[:, 0:4], s12[:, 12:16], ALU.mult))
            link(tt_(comb_w[:, 1, :], s12[:, 4:8], s12[:, 12:16], ALU.mult))
            v.wait_ge(rank_ready, l + 1)
            link(v.tensor_copy(t0, ps[:, 1, 0:n]))
            link(v.tensor_copy(cnt, ps[:, 1, n:n + NE]))
            link(ts(q64, t0, float(P), None, ALU.is_ge))
            link(ts(cmp_, cnt, float(P), None, ALU.is_gt))
            for i in range(2, TT):
                link(stt(q64, t0, float(i * P), q64, ALU.is_ge, ALU.add))
                link(stt(cmp_, cnt, float(i * P), cmp_, ALU.is_gt, ALU.add))
            link(v.tensor_tensor_scan(inc, ones[:, 0:NE], cmp_, 0.0, ALU.mult, ALU.add))
            link(tt_(exc, inc, cmp_, ALU.subtract))
            link(tt_(exc, exc, em15[:, :], ALU.add))
            link(tt_(v3(t1), v3(q64), bc_e(exc), ALU.add))
            link(ts(t2, q64, 1.0, None, ALU.min))
            link(tt_(t1, t1, t2, ALU.mult))
            link(tt_(v3(t1), v3(t1), bc_e(e_id[:, :]), ALU.add))
            link(stt(t0, q64, -float(P), t0, ALU.mult, ALU.add))
            link(stt(t0, t1, float(P), t0, ALU.mult, ALU.add))
            for j, oh in enumerate((o1, o2)):
                link(tt_(t2, oh, t0, ALU.mult))
                link(v.tensor_reduce(dst[:, j, :], v3(t2), AX_X, ALU.add))
            link(v.tensor_copy(yrow[:, :, :], dst[:, :, :]))
            yr = yrow[:, :, :].rearrange("p a b -> p (a b)")
            link(ts(ytmp[:, 0, :], yr, 7, None, ALU.arith_shift_right))
            link(ts(ytmp[:, 1, :], yr, P - 1, None, ALU.bitwise_and))
            link(stt(trow[:, :, :].rearrange("p a b -> p (a b)"), ytmp[:, 1, :], float(NBLK), ytmp[:, 0, :], ALU.mult, ALU.add))
            cv = cond.rearrange("p (k e) -> p k e", e=NE)
            link(tt_(cv, inc.unsqueeze(1).to_broadcast([P, MAX_OVER, NE]), k_id[:, :].unsqueeze(2).to_broadcast([P, MAX_OVER, NE]), ALU.is_le))
            link(v.tensor_reduce(sel[:, 0:MAX_OVER], cv, AX_X, ALU.add))
            link(ts(sel[:, 0:MAX_OVER], sel[:, 0:MAX_OVER], float(NE - 1), None, ALU.min))
            link(v.tensor_copy(sel[:, MAX_OVER:8], inc[:, NE - 1:NE]))
            v.tensor_copy(info[:, :], sel).then_inc(route_ready, 1)
            v.wait_ge(route_ready, l + 1)

        def experts(l):
            s = 2 * l + 1
            e0 = l * NE
            for t in range(TT + 1):
                if t < TT:
                    residual(l, t)
                    if l == 0 and t == 0:
                        mod_take(MOD_SPLIT - 1)
                    scale_x(s, t)
                if t:
                    take_ht(s, t - 1)
            route(l)

            def xst(e, par, first=False):
                if not first:
                    v.wait_ge(up_done, e + (e0 - 1))
                v.wait_ge(xs_turned, e + (e0 + 1))
                for kt in range(4, KT):
                    ins = ts(xsT[par][:, kt, :], ps[:, 1, (kt - 4) * P:(kt - 3) * P], AB[:, s, 0, kt:kt + 1], AB[:, s, 1, kt:kt + 1], ALU.mult, ALU.add)
                ins.then_inc(xst_dve, 1)

            def scale_y(buf, done):
                for h in range(2):
                    ins = tt_(buf[:, h * HALF:h * HALF + HALF], ps[:, 5 + h, :], G[:, 2 * l + 1, h * HALF:h * HALF + HALF], ALU.mult)
                ins.then_inc(done, 1)

            def take_y(e, par, stored):
                v.wait_ge(down_done, e + (e0 + 1))
                if stored is not None:
                    v.wait_ge(yb_stored[par], stored * 16 + (NE // 2) * l * 16)
                scale_y(ybuf[par], yb_ready)

            def step(e, par, stored=None, first=False, last=False):
                if not first:
                    take_y(e - 1, 1 - par, stored)
                if not last:
                    xst(e + 1, 1 - par, first)
                v.wait_ge(silu_done, e + (e0 + 1))
                v.wait_ge(up_done, e + (e0 + 1))
                tt_(hid, ps[:, 3, :], sg, ALU.mult).then_inc(hid_ready, 1)

            xst(0, 0, True)
            step(0, 0, first=True)
            step(1, 1)
            step(2, 0)
            step(3, 1, 1)
            with v.Fori(2, NE // 2 - 1) as i:
                step(2 * i, 0, i - 1)
                step(2 * i + 1, 1, i)
            step(NE - 2, 0, NE // 2 - 2)
            step(NE - 1, 1, NE // 2 - 1, last=True)
            take_y(NE - 1, 1, NE // 2 - 1)

            o = over[l]
            v.wait_ge(yb_stored[0], 16 * (NE // 2) * (l + 1))
            n_over = v.value_load(info[0:1, 7:8], min_val=0, max_val=MAX_OVER)
            with v.Fori(0, MAX_OVER) as k:
                with v.If(k < n_over):
                    v.wait_ge(o["turned"], k + 1)
                    for kt in range(4, KT):
                        ins = ts(xsT[0][:, kt, :], ps[:, 1, (kt - 4) * P:(kt - 3) * P], AB[:, s, 0, kt:kt + 1], AB[:, s, 1, kt:kt + 1], ALU.mult, ALU.add)
                    ins.then_inc(o["xst"], 1)
                    v.wait_ge(o["silu"], k + 1)
                    v.wait_ge(o["gu"], k + 1)
                    tt_(hid, ps[:, 3, :], sg, ALU.mult).then_inc(o["hid"], 1)
                    v.wait_ge(o["down"], k + 1)
                    v.wait_ge(o["stored"], (k + 1) * 16)
                    scale_y(ybuf[0], o["yb"])

            def combine(t):
                v.wait_ge(comb_filled[t], 32 * (l + 1))
                link(stt(X[:, t, :], comb[0][t], comb_w[:, 0, t:t + 1], X[:, t, :], ALU.mult, ALU.add))
                stt(X[:, t, :], comb[1][t], comb_w[:, 1, t:t + 1], X[:, t, :], ALU.mult, ALU.add).then_inc(x_ready, 1)
                v.wait_ge(x_ready, TT * (2 * l + 1) + t + 1)

            combine(0)
            for t in range(TT):
                if t + 1 < TT:
                    combine(t + 1)
                scale_x(s + 1, t)

        experts(0)
        for t in range(TT):
            take_ht(2, t)

        def rotate(z, n):
            v.wait_ge(qkv_act, 4 * n)
            zv = z.rearrange("p t (h d) -> p t h d", d=HD)
            z1, z2 = zv[:, :, :, 0:ROT], zv[:, :, :, ROT:2 * ROT]
            bc = lambda x: x.rearrange("p (t r) -> p t r", r=ROT).unsqueeze(2).to_broadcast([P, TT, HEADS, ROT])
            sin, cos = bc(rope[:, 4, :]), bc(rope[:, 5, :])
            r4 = [x.rearrange("p (t h r) -> p t h r", h=HEADS, r=ROT) for x in rots]
            link(tt_(r4[0], z1, cos, ALU.mult))
            link(tt_(r4[1], z2, sin, ALU.mult))
            link(tt_(r4[2], z2, cos, ALU.mult))
            link(tt_(r4[3], z1, sin, ALU.mult))
            link(tt_(z1, r4[0], r4[1], ALU.subtract))
            link(tt_(z2, r4[2], r4[3], ALU.add))
            v.sem_inc(rot_ready, 1)

        v.wait_ge(rope_ready, 2)
        for w in range(6):
            dest = (Q, K, V)[w // 2]
            for t in (1, 3):
                v.wait_ge(qkv_ready, 4 * w + t + 1)
                v.tensor_copy(dest[:, t, (w % 2) * HALF:(w % 2) * HALF + HALF], ps[:, (4 * w + t) % 6, :]).then_inc(qkv_dve, 1)
                if t == 1 and w >= 3:
                    mod_take(MOD_SPLIT + w - 3)
                if 1 <= w < 5:
                    mod_acc(MOD_SPLIT + w - 1, 4 * (t // 2), 4)
            if w in (1, 3):
                v.wait_ge(qkv_dve, 2 * (w + 1))
                rotate(dest, (w + 1) // 2)
        mod_take(LAYERS * PARTS - 1)
        for hp in range(8):
            v.wait_ge(kt_turned, hp + 1)
            v.tensor_copy(KTR[:, hp, :], ps[:, (2 * hp + 1) % 8, :]).then_inc(kt_ready, 1)

        def score_step(n):
            it = (n // 2) % TT
            v.wait_ge(s_ready, n + 1)
            if n >= 4:
                v.wait_ge(p_turned, n - 3)
            lc = LC[:, (TT - 1 - it) * P:(TT - 1 - it) * P + S]
            link(v.tensor_tensor_reduce(prob[n % 4], ps[:, n % 3, :], lc, HD ** -0.5, -3.0e38, ALU.add, ALU.max, mx[:, n:n + 1]))
            ts(nmx[:, n:n + 1], mx[:, n:n + 1], -1.0, None, ALU.mult).then_inc(max_ready, 1)

        def head_out(hp):
            v.wait_ge(av_ready, 8 * hp + 8)
            link(v.reciprocal(rsum[:, 8 * hp:8 * hp + 8], ssum[:, 8 * hp:8 * hp + 8]))
            o4 = O[:, :, hp * P:(hp + 1) * P].rearrange("p t (h d) -> p t h d", d=HD)
            p4 = ps[:, 5 + hp % 2, :].rearrange("p (t h d) -> p t h d", h=2, d=HD)
            r4 = rsum[:, 8 * hp:8 * hp + 8].rearrange("p (t h) -> p t h", h=2).unsqueeze(3).to_broadcast([P, TT, 2, HD])
            tt_(o4, p4, r4, ALU.mult).then_inc(o_ready, 1)

        v.wait_ge(mask_ready, 1)
        v.wait_ge(kt_turned, 8)
        score_step(0)
        score_step(1)
        for u in range(64):
            if u + 2 < 64:
                score_step(u + 2)
            if u % 2 == 1:
                v.wait_ge(p_turned, u + 1)
                if u >= 4:
                    v.wait_ge(av_ready, u - 3)
                v.tensor_copy(probT[u % 4], ps[:, 3 + u % 2, :]).then_inc(pt_dve, 1)
            if u % 8 == 2 and u > 8:
                head_out(u // 8 - 1)
        head_out(7)
        for kt in range(1, KT, 2):
            v.wait_ge(o_turned, kt + 1)
            v.tensor_copy(OT[:, kt, :], ps[:, kt, :]).then_inc(ot_dve, 1)
        experts(1)

    @block.tensor
    def _(pe):
        def turn_x(s, t):
            pe.wait_ge(xn_ready, TT * s + t + 1)
            for kt in range(KT):
                ins = pe.transpose(ps[:, 2 * t + kt // 4, (kt % 4) * P:(kt % 4 + 1) * P], xnorm[s][:, t, kt:D:KT], ident[:, :])
            ins.then_inc(xn_turned, 1)

        def wait_ht(s, t=TT - 1):
            pe.wait_ge(ht_act, TT * s + t + 1)
            pe.wait_ge(ht_dve, TT * s + t + 1)

        def mod_reduce(n):
            l, q = part_of(n)
            if n:
                pe.wait_ge(mod_done, n)
            pe.wait_ge(acc_ready, n + 1)
            if q in (2, 5):
                for h in range(2):
                    ins = pe.matmul(ps[:, 6 + h, :], ones[:, :], acc[n % 2][:, h * HALF:h * HALF + HALF], start=True, stop=True)
            else:
                for kt in range(KT):
                    ins = pe.matmul(ps[:, 7, kt:kt + 1], acc[n % 2][:, kt:D:KT], ones[:, 0:1], start=True, stop=True)
            ins.then_inc(mod_reduced, 1)

        pe.wait_ge(consts_ready, 1)
        pe.wait_ge(params_loaded, 16 * 13)
        mod_reduce(0)
        for t in range(3):
            turn_x(0, t)
        mod_reduce(1)
        pe.wait_ge(mod_done, 2)
        turn_x(0, 3)
        wait_ht(0)
        pe.transpose(ps[:, 7, 64:120], rows[0:56, :], ident[0:56, 0:56]).then_inc(cols_turned, 1)

        def z_tile(t):
            g, j = t // 4, t % 4
            if j == 0:
                wait_slab(pe, ("in", g))
            if 6 <= t < 14:
                pe.wait_ge(z_act, t - 1)
            elif 14 <= t < 18:
                pe.wait_ge(gate_read, LRU_TILES)
            elif t >= 18:
                pe.wait_ge(z_dve, t - 17)
            for kt in range(KT):
                ins = pe.matmul(ps[:, z_bank(t), :], slab(("in", g))[:, kt, j * P:(j + 1) * P], HT[:, kt, :], start=(kt == 0), stop=(kt == KT - 1))
            ins.then_inc(z_ready, 1)

        def gate_products(j):
            pe.wait_ge(z_act, LRU_TILES)
            pe.wait_ge(xr_ready, j + 1)
            if j:
                pe.wait_ge(gate_read, j)
            for d in range(2):
                for w in range(2):
                    ins = pe.matmul(ps[:, 2 * d + w, :], BD[:, (d * 2 + w) * LRU_TILES + j, :], xr[j], start=True, stop=True)
            ins.then_inc(gate_ready, 1)

        pe.wait_ge(bd_loaded, 16 * 8)
        reduce_after = {5: 2, 8: 3, 11: 4, 14: 5, 17: 6}
        for t in range(20):
            z_tile(t)
            if t in (4, 6, 8, 10):
                gate_products((t - 4) // 2)
            if t in reduce_after:
                mod_reduce(reduce_after[t])

        def project(l, t):
            lhs, order = ((mixT, (4, 5, 6, 7, 0, 1, 2, 3)), (OT, range(KT)))[l]
            for half in range(2):
                name = (("out", "o")[l], half)
                wait_slab(pe, name)
                for i, kt in enumerate(order):
                    ins = pe.matmul(ps[:, 2 * t + half, :], lhs[:, kt, t * P:(t + 1) * P], slab(name)[:, kt, :], start=(i == 0), stop=(i == KT - 1))
                ins.then_inc(y_ready, 1)

        pe.wait_ge(mix_ready, LRU_TILES)
        pe.wait_ge(z_dve, 8)

        def experts(l):
            s = 2 * l + 1
            e0 = l * NE

            def logits(t):
                wait_ht(s, t)
                for kt in range(KT):
                    ins = pe.matmul(ps[:, 0, t * NE:(t + 1) * NE], HT[:, kt, t * P:(t + 1) * P], rw[:, kt, :], start=(kt == 0), stop=(kt == KT - 1))
                return ins

            for t in range(TT + 1):
                if t < TT:
                    if l == 0 and t == 3:
                        pe.wait_ge(mod_done, MOD_SPLIT)
                    project(l, t)
                    if l == 0 and t == 0:
                        mod_reduce(MOD_SPLIT - 1)
                if t:
                    turn_x(s, t - 1)
                if t >= 2:
                    logits(t - 2)
            logits(TT - 1).then_inc(logit_ready, 1)
            pe.wait_ge(hot_ready, l + 1)
            for t in range(TT):
                for t0 in range(t + 1):
                    pe.matmul(ps[:, 1, t * NE:(t + 1) * NE], before[:, :] if t0 == t else ones_b[:, :], hot[:, t0, :], start=(t0 == 0), stop=(t0 == t))
            for t in range(TT):
                ins = pe.matmul(ps[:, 1, TT * NE:(TT + 1) * NE], ones_b[:, :], hot[:, t, :], start=(t == 0), stop=(t == TT - 1))
            ins.then_inc(rank_ready, 1)
            pe.wait_ge(route_ready, l + 1)

            def turn_xs(buf, done):
                for kt in range(KT):
                    ins = pe.transpose(ps[:, kt // 4, (kt % 4) * P:(kt % 4 + 1) * P], xs[buf][:, kt:D:KT], ident[:, :])
                ins.then_inc(done, 1)

            def product(par, w, bank, kts):
                for kt in kts:
                    ins = pe.matmul(ps[:, bank, :], xsT[par][:, kt, :], w[:, kt, :], start=(kt == 0), stop=(kt == KT - 1))
                return ins

            def turn_hid(done):
                for f in range(FT):
                    ins = pe.transpose(ps[:, 4, f * P:(f + 1) * P], hid[:, f * P:(f + 1) * P], ident[:, :])
                ins.then_inc(done, 1)

            def down(w, done):
                for h in range(2):
                    for f in range(FT):
                        ins = pe.matmul(ps[:, 5 + h, :], hidT[:, f, :], w[:, 2 * f + h, :], start=(f == 0), stop=(f == FT - 1))
                ins.then_inc(done, 1)

            def turn_hidden(e):
                pe.wait_ge(hid_ready, e + (e0 + 1))
                turn_hid(hid_turned)

            def down_product(e, par, turn, first=False):
                pe.wait_ge(hidt_ready, e + (e0 + 1))
                if not first:
                    pe.wait_ge(yb_ready, e + e0)
                wait_slab(pe, ("exp", l, 2, par), turn)
                down(slab(("exp", l, 2, par)), down_done)

            def step(e, par, turn, first=0, last=False):
                prev_turn = turn if par else turn - 1
                pe.wait_ge(xst_act, e + (e0 + 1))
                pe.wait_ge(xst_dve, e + (e0 + 1))
                if first != 1:
                    pe.wait_ge(silu_done, e + e0)
                wait_slab(pe, ("exp", l, 0, par), turn)
                product(par, slab(("exp", l, 0, par)), 2, range(KT // 2))
                if first != 1:
                    turn_hidden(e - 1)
                product(par, slab(("exp", l, 0, par)), 2, range(KT // 2, KT)).then_inc(gate_done, 1)
                if first != 1:
                    down_product(e - 1, 1 - par, prev_turn, first == 2)
                if not last:
                    pe.wait_ge(xs_filled[1 - par], (turn + par) * 16 + (16 + (NE // 2) * l * 16))
                    turn_xs(1 - par, xs_turned)
                wait_slab(pe, ("exp", l, 1, par), turn)
                product(par, slab(("exp", l, 1, par)), 3, range(KT)).then_inc(up_done, 1)

            pe.wait_ge(xs_filled[0], (NE // 2) * l * 16 + 16)
            turn_xs(0, xs_turned)
            step(0, 0, 0, first=1)
            step(1, 1, 0, first=2)
            with pe.Fori(1, NE // 2 - 1) as i:
                for par in range(2):
                    step(2 * i + par, par, i)
            step(NE - 2, 0, NE // 2 - 1)
            step(NE - 1, 1, NE // 2 - 1, last=True)
            turn_hidden(NE - 1)
            down_product(NE - 1, 1, NE // 2 - 1)

            o = over[l]
            over_slab = [slab(("exp", l, c, 0)) for c in range(3)]
            pe.wait_ge(yb_ready, e0 + NE)
            n_over = pe.value_load(info[0:1, 7:8], min_val=0, max_val=MAX_OVER)
            with pe.Fori(0, MAX_OVER) as k:
                with pe.If(k < n_over):
                    pe.wait_ge(o["xs"], (k + 1) * 16)
                    turn_xs(0, o["turned"])
                    pe.wait_ge(o["xst"], (k + 1) * 2)
                    pe.wait_ge(o["wg"], (k + 1) * 16)
                    product(0, over_slab[0], 2, range(KT)).then_inc(o["gate"], 1)
                    pe.wait_ge(o["wu"], (k + 1) * 16)
                    product(0, over_slab[1], 3, range(KT)).then_inc(o["gu"], 1)
                    pe.wait_ge(o["hid"], k + 1)
                    turn_hid(o["hidt_in"])
                    pe.wait_ge(o["hidt"], k + 1)
                    pe.wait_ge(o["wd"], (k + 1) * 16)
                    pe.wait_ge(o["stored"], (k + 1) * 16)
                    down(over_slab[2], o["down"])

        experts(0)
        for t in range(TT):
            turn_x(2, t)
        for w in range(6):
            wait_slab(pe, ("qkv", w))
            for t in range(TT):
                i = 4 * w + t
                if w == 0:
                    wait_ht(2, t)
                if i >= 6:
                    pe.wait_ge(qkv_dve if t % 2 else qkv_act, (i - 6) // 2 + 1)
                for kt in range(KT):
                    ins = pe.matmul(ps[:, i % 6, :], HT[:, kt, t * P:(t + 1) * P], slab(("qkv", w))[:, kt, :], start=(kt == 0), stop=(kt == KT - 1))
                ins.then_inc(qkv_ready, 1)
            if w >= 2:
                mod_reduce(MOD_SPLIT + w - 2)
        pe.wait_ge(mod_done, LAYERS * PARTS)
        pe.wait_ge(qkv_act, 12)
        pe.wait_ge(qkv_dve, 12)
        pe.wait_ge(rot_ready, 2)
        for hp in range(8):
            if hp >= 4:
                pe.wait_ge(qt_ready, hp - 3)
            for t in range(TT):
                ins = pe.transpose(ps[:, (2 * hp) % 8, t * P:(t + 1) * P], Q[:, t, hp * P:(hp + 1) * P], ident[:, :])
            ins.then_inc(qt_turned, 1)
            if hp >= 4:
                pe.wait_ge(kt_ready, hp - 3)
            for t in range(TT):
                ins = pe.transpose(ps[:, (2 * hp + 1) % 8, t * P:(t + 1) * P], K[:, t, hp * P:(hp + 1) * P], ident[:, :])
            ins.then_inc(kt_turned, 1)

        def scores(n):
            hp, it, par = n // 8, (n // 2) % TT, n % 2
            if n >= 3:
                pe.wait_ge(max_ready, n - 2)
            r0 = HD * par
            pe.matmul(ps[:, n % 3, :], QT[r0:r0 + HD, hp, it * P:(it + 1) * P], KTR[r0:r0 + HD, hp, :], start=True, stop=True).then_inc(s_ready, 1)

        def weigh(n):
            hp, it, par = n // 8, (n // 2) % TT, n % 2
            pe.wait_ge(pt_act if n % 2 == 0 else pt_dve, n // 2 + 1)
            if n % 8 == 0 and hp >= 2:
                pe.wait_ge(o_ready, hp - 1)
            dest = ps[:, 5 + hp % 2, (n % 8) * HD:(n % 8 + 1) * HD]
            h = 2 * hp + par
            for jt in range(TT):
                ins = pe.matmul(dest, probT[n % 4][:, jt * P:(jt + 1) * P], V[:, jt, h * HD:(h + 1) * HD], start=(jt == 0), stop=(jt == TT - 1))
            ins.then_inc(av_ready, 1)

        pe.wait_ge(qt_ready, 8)
        pe.wait_ge(kt_ready, 8)
        scores(0)
        scores(1)
        for u in range(64):
            if u + 2 < 64:
                scores(u + 2)
            pe.wait_ge(p_ready, u + 1)
            if u >= 2:
                pe.wait_ge(pt_act if u % 2 == 0 else pt_dve, u // 2)
            for jt in range(TT):
                ins = pe.transpose(ps[:, 3 + u % 2, jt * P:(jt + 1) * P], prob[u % 4][:, jt * P:(jt + 1) * P], ident[:, :])
            ins.then_inc(p_turned, 1)
            if u >= 1:
                weigh(u - 1)
        weigh(63)
        pe.wait_ge(o_ready, 8)
        for kt in range(KT):
            for t in range(TT):
                ins = pe.transpose(ps[:, kt, t * P:(t + 1) * P], O[:, t, kt * P:(kt + 1) * P], ident[:, :])
            ins.then_inc(o_turned, 1)
        pe.wait_ge(ot_act, 4)
        pe.wait_ge(ot_dve, 4)
        experts(1)


_INS = ["x", "c", "positions", "mod_w", "mod_b", "norm_mix_g", "norm_ffn_g", "final_norm_g", "w_in_ab", "conv_a_w",
        "conv_b_w", "conv_b_b", "lru_wa", "lru_ba", "lru_wx", "lru_bx", "lru_lambda", "w_out_ab", "w_qkv", "w_o",
        "router_w", "router_bias", "expert_w_gate", "expert_w_up", "expert_w_down"]


def kernel(**inputs):
    import concourse.bacc as _bacc
    from concourse.bass_utils import run_bass_kernel_spmd as _run

    nc = _bacc.Bacc("TRN2", target_bir_lowering=False, num_devices=1, dynamic_dma_scratch_size=4096)
    arrays, args = {}, {}
    for name in _INS:
        arr = np.ascontiguousarray(inputs[name])
        arrays[f"in_{name}_dram"] = arr
        args[name] = nc.dram_tensor(f"in_{name}_dram", arr.shape, mybir.dt.from_np(arr.dtype), kind="ExternalInput").ap()
    out = nc.dram_tensor("out_dram", (1, S, D), F32, kind="ExternalOutput").ap()
    trunk(nc, args, out)
    r = _run(nc, [arrays], core_ids=[0])
    return r.results[0]["out_dram"]
```

```python
from contextlib import ExitStack

import numpy as np

import concourse.bass as bass
from concourse import mybir

ALU = mybir.AluOpType
ACT = mybir.ActivationFunctionType
AX_X = mybir.AxisListType.X
F32 = mybir.dt.float32
BF16 = mybir.dt.bfloat16
I32 = mybir.dt.int32
U32 = mybir.dt.uint32
F32R = mybir.dt.float32r

P = 128
D = 1024
S = 512
TT = S // P
KT = D // P
HALF = 512
LRU_TILES = 4
HEADS, HD = 16, 64
ROT = 8
NE, NG, EPG = 16, 4, 4
FF = 512
FT = FF // P
MAX_OVER = 2 * S // P - 1
NBLK = NE + MAX_OVER
WIDE = NBLK + NBLK % 2
RING = 6
MOD_RING = 4
MOD_SLICES = KT
LAYERS = 2
PARTS = 6
EPS = 1e-6
NEG = -1.0e30
NO_TOKEN = 1 << 20
ROPE_THETA = 500000.0
MAGIC = 12582912.0
LSPAN = (TT - 1) * P + S


class Link:

    def __init__(self, eng, sem):
        self.eng, self.sem, self.n, self.turn, self.per = eng, sem, 0, None, 0

    def __call__(self, ins):
        self.n += 1
        ins.then_inc(self.sem, 1)
        value = self.n if self.turn is None else self.turn * self.per + self.n
        self.eng.wait_ge(self.sem, value)

    def enter_loop(self, turn, first, per):
        self.turn, self.per, self.entry = turn, per, self.n
        self.n -= first * per

    def leave_loop(self, first, end):
        assert self.n + first * self.per == self.entry + self.per, (self.n + first * self.per - self.entry, self.per)
        self.turn = None
        self.n = self.entry + (end - first) * self.per


def part_of(n):
    return n // PARTS, n % PARTS


def trunk(nc, a, out):
    with ExitStack() as ctx:
        build(nc, ctx, a, out)


def build(nc, ctx, a, out):
    def small(name, shape, dt=F32):
        return ctx.enter_context(nc.sbuf_tensor(name, shape, dt))

    def twins(name, shape):
        with nc.sbuf_tensor(name, shape, F32) as plain:
            pass
        return plain, small(name + "_r", shape, F32R)

    sems = {}

    def sem(name):
        sems[name] = ctx.enter_context(nc.semaphore(name))
        return sems[name]

    UNIT = 512
    X = small("x_res", [P, TT, D])
    ring, ring_r = twins("slab_ring", [P, RING, KT, HALF])
    modr, modr_r = twins("mod_ring", [P, 8, UNIT])
    G, G_r = twins("gate_rows", [P, 4, D])
    LC = small("log_count", [P, LSPAN])
    HT, HT_r = twins("h_t", [P, KT, S])
    XN, XN_r = twins("x_norm", [P, TT, D])
    R, R_r = twins("scratch", [P, 16, UNIT])

    ps = ctx.enter_context(nc.psum_tensor("ps", [P, 8, HALF], F32))

    mod_slot = [modr[:, 2 * i:2 * i + 2, :].rearrange("p a n -> p (a n)") for i in range(MOD_RING)]
    u_in = R[:, 0, :]
    xr = [R[:, 1 + j, :] for j in range(LRU_TILES)]
    th = [R[:, 5, :], R[:, 8, :]]
    ti = [R[:, 6, :], R[:, 9, :]]
    av = [R[:, 7, :], R[:, 10, :]]
    tmp0 = R[:, 11, :]
    acc = [R[:, 12:14, :].rearrange("p a n -> p (a n)"), R[:, 14:16, :].rearrange("p a n -> p (a n)")]
    mixT = XN[:, :, :].rearrange("p t (h n) -> p (t h) n", h=2)
    BD = G[:, 2:4, :].rearrange("p g (x o) -> p (g x) o", o=P)
    mflt = R[:, 11, :].rearrange("p (i n) -> p i n", n=P)
    mlow = R[:, 10, 0:P].bitcast(I32)
    xs = [R[:, 0:2, :].rearrange("p a n -> p (a n)"), R[:, 2:4, :].rearrange("p a n -> p (a n)")]
    xsT = [R[:, i:i + 2, :].rearrange("p a (b n) -> p (a b) n", n=P) for i in (4, 13)]
    sg = R[:, 6, :]
    hid = R[:, 7, :]
    hidT = R[:, 8, :].rearrange("p (f n) -> p f n", n=P)
    ybuf = [R[:, 9:11, :].rearrange("p a n -> p (a n)"), R[:, 11:13, :].rearrange("p a n -> p (a n)")]
    xs_low = [R_r[:, i:i + 2, :].rearrange("p a (b n) -> p (a b) n", n=P) for i in (4, 13)]
    xs_high = [[G_r[:, g, :].rearrange("p (a n) -> p a n", n=P) for g in gs] for gs in ((0, 2), (1, 2))]
    w_high = [[HT_r, (XN_r[:, :, :].rearrange("p t (h n) -> p (t h) n", h=2), modr_r)[l]] for l in range(LAYERS)]
    rt = R[:, 13:16, :].rearrange("p a n -> p (a n)")
    place_hot = R_r[:, 9:11, :].rearrange("p a (t n) -> p (a t) n", n=P)
    block_tok = R_r[:, 11, 0:2 * TT * WIDE].rearrange("p (a b) -> p a b", b=WIDE)
    comb = [[XN[:, t, :] for t in range(TT)],
            [modr[:, 2 * t:2 * t + 2, :].rearrange("p a n -> p (a n)") for t in range(TT)]]
    Q = R[:, 0:8, :].rearrange("p (t h) n -> p t (h n)", h=2)
    O = Q
    QT = R[:, 8:16, :]
    K = modr[:, :, :].rearrange("p (t h) n -> p t (h n)", h=2)
    KTR = HT
    V = XN
    OT = modr
    xnorm = [modr[:, :, :].rearrange("p (t h) n -> p t (h n)", h=2) if s == 1 else XN for s in range(2 * LAYERS + 1)]
    prob = [modr[:, i, :] for i in range(4)]
    rots = [G[:, i // 2, (i % 2) * HALF:(i % 2) * HALF + HALF] for i in range(4)]
    probT = rots

    ident = small("ident", [P, P])
    ones = small("ones", [P, P])
    before = small("before", [P, P], BF16)
    ones_b = small("ones_b", [P, P], BF16)
    rows = small("param_rows", [56, P])
    cols = small("param_cols", [P, 56])
    cT = small("c_t", [P, KT])
    cs = small("c_silu", [P, KT])
    gcols = small("norm_gains", [P, LAYERS, 2, KT])
    mbc = small("mod_b_cols", [P, LAYERS * PARTS, KT])
    AB = small("mod_ab", [P, LAYERS * 2, 2, KT])
    rw = small("router_w", [P, KT, NE])
    rb = small("router_b", [P, NE])
    lru = small("lru_consts", [P, 6, 8])
    hbias = small("half_bias", [P, 16])
    dec = small("decay", [P, 2, 8])
    stats = small("stats", [P, 4, TT])
    eps = small("eps", [P, 1])
    posi = small("pos_i", [P, TT], I32)
    posf = small("pos_f", [P, TT])
    invf = small("inv_freq", [P, ROT])
    rope = small("rope", [P, 6, TT * ROT])
    mx = small("row_max", [P, 64])
    nmx = small("neg_max", [P, 64])
    ssum = small("row_sum", [P, 64])
    rsum = small("row_rcp", [P, 64])
    e_id = small("expert_id", [P, NE])
    g_id = small("group_id", [P, NE])
    em15 = small("over_base", [P, NE])
    k_id = small("over_id", [P, MAX_OVER])
    tok1 = small("token_id_plus_1", [P, TT])
    b_id = small("block_id", [P, WIDE])
    p_id = small("place_id", [P, P])
    slot_tok = small("slot_token", [P, WIDE], I32)
    gpad = small("group_pad", [P, TT, 8])
    mx8 = small("max8", [P, TT, 8])
    ix8 = small("index8", [P, TT, 8], U32)
    comb_w = small("combine_w", [P, 2, TT])
    yrow = small("y_row", [P, 2, TT], I32)
    ytmp = small("block_and_place_i", [P, 2, 2 * TT], I32)
    yplace = small("block_and_place", [P, 2, 2 * TT])
    empty = small("slot_empty", [P, WIDE])
    dst = small("dest", [P, 2, TT])
    info = small("over_info", [P, 8], I32)
    hot = small("hot_b", [P, TT, NE], BF16)
    idx = [small(f"gather_idx{i}", [P, 1], I32) for i in range(2)]

    xn_dram = nc.dram_tensor("xn_rows", [S, D], F32, kind="Internal").ap()
    y_dram = nc.dram_tensor("y_rows", [NBLK * P, D], F32, kind="Internal").ap()

    x_loaded = sem("x_loaded")
    params_loaded, c_loaded = sem("params_loaded"), sem("c_loaded")
    bd_loaded = sem("bd_loaded")
    g_bias_loaded = [sem(f"g_bias_loaded{i}") for i in range(4)]
    slab_filled = [sem(f"slab_filled{i}") for i in range(RING)]
    mod_filled = [sem(f"mod_filled{i}") for i in range(MOD_RING)]
    mod_used = sem("mod_used")
    dve_step, act_step, pool_step = sem("dve_step"), sem("act_step"), sem("pool_step")
    consts_ready = sem("consts_ready")
    bd_zeroed = sem("bd_zeroed")
    mask_base = sem("mask_base")
    mask_ready = sem("mask_ready")
    cs_ready = sem("cs_ready")
    cols_turned = sem("cols_turned")
    lam_abs, lam_exp = sem("lam_abs"), sem("lam_exp")
    angle_ready, rope_ready = sem("angle_ready"), sem("rope_ready")
    dec_ready = sem("dec_ready")
    x_ready = sem("x_ready")
    rms_ready = sem("rms_ready")
    xn_ready = sem("xn_ready")
    xn_turned = sem("xn_turned")
    ht_act, ht_dve = sem("ht_act"), sem("ht_dve")
    acc_ready, mod_reduced, mod_done = sem("acc_ready"), sem("mod_reduced"), sem("mod_done")
    z_ready, z_act, z_dve = sem("z_ready"), sem("z_act"), sem("z_dve")
    xr_ready, gate_ready, gate_read = sem("xr_ready"), sem("gate_ready"), sem("gate_read")
    m_ready, mult_ready, scan_done = sem("m_ready"), sem("mult_ready"), sem("scan_done")
    mix_ready = sem("mix_ready")
    y_ready = sem("y_ready")
    logit_ready, score_ready = sem("logit_ready"), sem("score_ready")
    hot_ready, rank_ready, route_ready = sem("hot_ready"), sem("rank_ready"), sem("route_ready")
    xn_stored, place_ready, slots_summed, slots_ready = sem("xn_stored"), sem("place_ready"), sem("slots_summed"), sem("slots_ready")
    xs_filled = [sem("xs_filled0"), sem("xs_filled1")]
    xs_turned, xst_act, xst_dve = sem("xs_turned"), sem("xst_act"), sem("xst_dve")
    high_ready, low_ready = [sem("gate_high"), sem("up_high")], [sem("gate_low"), sem("up_low")]
    xs_high_ready, xst_turned, xst_split = sem("xs_high_ready"), sem("xst_turned"), sem("xst_split")
    gate_done, up_done, silu_done = sem("gate_done"), sem("up_done"), sem("silu_done")
    hid_ready, hid_turned, hidt_ready = sem("hid_ready"), sem("hid_turned"), sem("hidt_ready")
    down_done, yb_ready = sem("down_done"), sem("yb_ready")
    yb_stored = [sem("yb_stored0"), sem("yb_stored1")]
    turn_seen, stores_seen = sem("turn_seen"), sem("stores_seen")
    y_zeroed = sem("y_zeroed")
    comb_filled = [sem(f"comb_filled{t}") for t in range(TT)]
    over = [{n: sem(f"over{l}_{n}") for n in ("wg", "wu", "wd", "xs", "turned", "xst", "gu", "silu", "hid", "hidt_in", "hidt", "down", "yb", "stored", "step", "gate")}
            for l in range(LAYERS)]
    qkv_high, qkv_low, qkv_chunk = sem("qkv_high"), sem("qkv_low"), sem("qkv_chunk")
    ht_full, ht_high_act, ht_high_dve = sem("ht_full"), sem("ht_high_act"), sem("ht_high_dve")
    qkv_ready, qkv_act, qkv_dve = sem("qkv_ready"), sem("qkv_act"), sem("qkv_dve")
    rot_ready, qt_turned, kt_turned, qt_ready, kt_ready = (sem(n) for n in ("rot_ready", "qt_turned", "kt_turned", "qt_ready", "kt_ready"))
    s_ready, max_ready, p_ready, p_turned = sem("s_ready"), sem("max_ready"), sem("p_ready"), sem("p_turned")
    pt_act, pt_dve, av_ready, o_ready = sem("pt_act"), sem("pt_dve"), sem("av_ready"), sem("o_ready")
    o_turned, ot_act, ot_dve = sem("o_turned"), sem("ot_act"), sem("ot_dve")
    fg_loaded = sem("fg_loaded")
    final_ready, out_stored = sem("final_ready"), sem("out_stored")

    fills = [0] * RING
    place = {}

    def plan(name, slot, times=1):
        fills[slot] += 1
        place[name] = (slot, fills[slot])
        fills[slot] += times - 1

    for g in range(5):
        plan(("in", g), g)
    plan(("out", 0), 5)
    plan(("out", 1), 0)
    EXP_SLOT = {(c, par): (1 + 3 * par + c) % RING for c in range(3) for par in range(2)}
    for l in range(LAYERS):
        if l == 1:
            for w in range(6):
                plan(("qkv", w), (4, 5, 0)[w % 3])
            plan(("o", 0), 5)
            plan(("o", 1), 0)
        for (c, par), slot in EXP_SLOT.items():
            plan(("exp", l, c, par), slot, NE // 2)
    HT_HIGH_SLOT, QKV_HIGH_SLOT, MOD1_SLOT = 1, 2, 3
    QKV_SLICES = (6, 6, 4, 6, 4, 6)

    def slab(name):
        return ring[:, place[name][0], :, :]

    def wait_slab(eng, name, turn=0):
        slot, times = place[name]
        eng.wait_ge(slab_filled[slot], turn * 16 + 16 * times)

    def split_of(l, c, par, chunk):
        kts = slice(chunk * KT // 2, (chunk + 1) * KT // 2)
        return slab(("exp", l, c, par))[:, kts, :], w_high[l][c][:, kts, :], w_low(l, c, par)[:, kts, :]

    def w_low(l, c, par):
        return ring_r[:, place["exp", l, c, par][0], :, :]

    ht_high = ring_r[:, HT_HIGH_SLOT, :, :]

    def qkv_split_of(w, chunk):
        kts = slice(chunk * KT // 2, (chunk + 1) * KT // 2)
        return slab(("qkv", w))[:, kts, :], ring_r[:, QKV_HIGH_SLOT, kts, :], ring_r[:, place["qkv", w][0], kts, :]

    IN_ORDER = [4, 3, 2, 0, 1]
    MOD_SPLIT = 8
    mod1_slot = [ring[:, MOD1_SLOT, 2 * i:2 * i + 2, :].rearrange("p a n -> p (a n)") for i in range(MOD_RING)]

    def mod_place(g):
        return (mod_slot if g < MOD_SPLIT * MOD_SLICES else mod1_slot)[g % MOD_RING]

    def z_bank(t):
        return t if t < 4 else t - 14 if 14 <= t < 18 else 4 + t % 2

    def pair(bank):
        return ps[:, bank:bank + 2, :].rearrange("p a n -> p (a n)")

    N_PARAMS = 12

    def pk(w):
        return w.rearrange("(p k) n -> p k n", p=P)

    def kp(w):
        return w.rearrange("(k p) n -> p k n", p=P)

    w_in, w_out = pk(a["w_in_ab"][0]), kp(a["w_out_ab"][0])
    w_qkv, w_o = pk(a["w_qkv"][0]), kp(a["w_o"][0])

    block = ctx.enter_context(nc.Block())

    @block.sync
    def _(sp):
        def load_slab(name, src):
            sp.dma_start(slab(name), src).then_inc(slab_filled[place[name][0]], 16)

        def load_mod(n, ms=range(MOD_SLICES)):
            l, q = part_of(n)
            for m in ms:
                g = n * MOD_SLICES + m
                if g >= MOD_RING:
                    sp.wait_ge(mod_used, g - MOD_RING + 1)
                src = pk(a["mod_w"][l])[:, m, q * D:(q + 1) * D]
                sp.dma_start(mod_place(g), src).then_inc(mod_filled[g % MOD_RING], 16)

        def load_gate_bias(n):
            l, q = part_of(n)
            g = 2 * l + q // 5
            sp.dma_start(G[:, g, :], a["mod_b"][l, q * D:(q + 1) * D].unsqueeze(0).to_broadcast([P, D])).then_inc(g_bias_loaded[g], 16)

        def part_src(l, c, e):
            if c < 2:
                return a[("expert_w_gate", "expert_w_up")[c]][l, bass.ds(e, 1)].rearrange("e (p k) n -> p (e k) n", p=P)
            return a["expert_w_down"][l, bass.ds(e, 1)].rearrange("e (k p) n -> p (e k) n", p=P)

        def part_dst(c, par):
            dst_ap = ring[:, EXP_SLOT[c, par], :, :]
            return dst_ap if c < 2 else dst_ap.rearrange("p (f h) n -> p f (h n)", h=2)

        def load_part(l, c, e, par):
            sp.dma_start(part_dst(c, par), part_src(l, c, e)).then_inc(slab_filled[EXP_SLOT[c, par]], 16)

        load_mod(0)
        sp.dma_start(X[:, :, :], a["x"][0].rearrange("(t p) d -> p t d", p=P)).then_inc(x_loaded, 16)
        load_mod(1)
        for g in range(5):
            load_slab(("in", g), w_in[:, :, IN_ORDER[g] * HALF:IN_ORDER[g] * HALF + HALF])
        load_slab(("out", 0), w_out[:, :, 0:HALF])
        load_gate_bias(2)
        load_gate_bias(5)
        for n in range(2, MOD_SPLIT):
            load_mod(n)
            if n == 4:
                sp.wait_ge(z_ready, 4)
                load_slab(("out", 1), w_out[:, :, HALF:D])

        def stream_experts(l):
            e0 = l * NE
            free = {0: [(z_ready, 8), (z_ready, 12), (z_ready, 16), (z_ready, 20), (y_ready, 8), (y_ready, 8)],
                    1: [(qkv_ready, 24), (qkv_ready, 24), (mod_used, LAYERS * PARTS * MOD_SLICES), (qkv_ready, 16), (y_ready, 16), (y_ready, 16)]}[l]
            for e in range(2):
                for c in range(3):
                    sp.wait_ge(*free[3 * e + c])
                    load_part(l, c, e, e)

            def refill(pair, par, more, first=False):
                e = 2 * pair + par
                if more:
                    sp.wait_ge(gate_done, e + (e0 + 1))
                    load_part(l, 0, e + 2, par)
                if not first:
                    sp.wait_ge(down_done, e + e0)
                    load_part(l, 2, e + 1, 1 - par)
                if more:
                    sp.wait_ge(up_done, e + (e0 + 1))
                    load_part(l, 1, e + 2, par)
                if not first:
                    store(e - 1, 1 - par)

            def store(e, par):
                sp.wait_ge(yb_ready, e + (e0 + 1))
                sp.dma_start(y_dram[bass.ds(e * P, P), :], ybuf[par]).then_inc(yb_stored[par], 16)

            refill(0, 0, True, first=True)
            refill(0, 1, True)
            with sp.Fori(1, NE // 2 - 1) as i:
                refill(i, 0, True)
                refill(i, 1, True)
            refill(NE // 2 - 1, 0, False)
            o = over[l]
            n_over = sp.value_load(info[0:1, 7:8], min_val=0, max_val=MAX_OVER)

            def load_over(k, name, c):
                ex = sp.value_load(info[0:1, bass.ds(k, 1)], min_val=0, max_val=NE - 1)
                sp.dma_start(part_dst(c, 0), part_src(l, c, ex)).then_inc(o[name], 16)

            sp.wait_ge(gate_done, e0 + NE - 1)
            sp.wait_ge(up_done, e0 + NE - 1)
            with sp.If(n_over > 0):
                load_over(0, "wg", 0)
                load_over(0, "wu", 1)
            sp.wait_ge(down_done, e0 + NE - 1)
            with sp.If(n_over > 0):
                load_over(0, "wd", 2)
                sp.sem_inc(o["stored"], 16)
            store(NE - 2, 0)
            if l == 0:
                for w, used in enumerate((gate_done, up_done, down_done)):
                    sp.wait_ge(used, e0 + NE)
                    load_slab(("qkv", w), w_qkv[:, :, w * HALF:(w + 1) * HALF])
            store(NE - 1, 1)
            with sp.Fori(0, MAX_OVER) as k:
                with sp.If(k + 1 < n_over):
                    ex = sp.value_load(info[0:1, bass.ds(k + 1, 1)], min_val=0, max_val=NE - 1)
                    for c, name, used in ((0, "wg", "gate"), (1, "wu", "gu"), (2, "wd", "down")):
                        sp.wait_ge(o[used], k + 1)
                        sp.dma_start(part_dst(c, 0), part_src(l, c, ex)).then_inc(o[name], 16)
                with sp.If(k < n_over):
                    sp.wait_ge(o["yb"], k + 1)
                    sp.dma_start(y_dram[bass.ds((k + NE) * P, P), :], ybuf[0]).then_inc(o["stored"], 16)
                    sp.wait_ge(o["stored"], (k + 2) * 16)
                    sp.sem_inc(stores_seen, 1)
            for par in range(2):
                sp.wait_ge(yb_stored[par], 16 * (NE // 2) * (l + 1))

        stream_experts(0)

        def load_qkv(w):
            sp.wait_ge(qkv_ready, 4 * (w - 2))
            load_slab(("qkv", w), w_qkv[:, :, w * HALF:(w + 1) * HALF])

        first, second = range(MOD_SLICES // 2), range(MOD_SLICES // 2, MOD_SLICES)
        sp.wait_ge(comb_filled[TT - 1], 32)
        load_mod(8)
        load_qkv(3)
        load_gate_bias(8)
        load_gate_bias(11)
        load_mod(9, first)
        load_qkv(4)
        load_mod(9, second)
        load_mod(10, first)
        load_qkv(5)
        load_mod(10, second)
        load_mod(11)
        sp.wait_ge(qkv_ready, 20)
        load_slab(("o", 0), w_o[:, :, 0:HALF])
        sp.wait_ge(qkv_ready, 24)
        load_slab(("o", 1), w_o[:, :, HALF:D])
        stream_experts(1)
        for t in range(TT):
            sp.wait_ge(final_ready, t + 1)
            sp.dma_start(out[0, t * P:(t + 1) * P, :], XN[:, t, :]).then_inc(out_stored, 16)
        sp.wait_ge(out_stored, 16 * TT)

    @block.gpsimd
    def _(gp):
        link = Link(gp, pool_step)
        link(gp.memset(ident[:, :], 0.0))
        link(gp.affine_select(out=ident[:, :], in_=ident[:, :], compare_op=ALU.not_equal, fill=1.0, base=0, pattern=[[-1, P]], channel_multiplier=1))
        link(gp.memset(ones[:, :], 1.0))
        link(gp.memset(BD, 0.0))
        gp.sem_inc(bd_zeroed, 1)
        link(gp.memset(ones_b[:, :], 1.0))
        link(gp.memset(eps[:, :], EPS))
        link(gp.affine_select(out=before[:, :], in_=ones_b[:, :], compare_op=ALU.is_gt, fill=0.0, base=0, pattern=[[1, P]], channel_multiplier=-1))
        for i in range(ROT):
            f = float(np.float32(ROPE_THETA) ** np.float32(-2.0 * i / (2 * ROT)))
            link(gp.memset(invf[:, i:i + 1], f))
        link(gp.iota(mlow, [[1, P]], base=P, channel_multiplier=-1))
        link(gp.iota(e_id[:, :], [[1, NE]], base=0, channel_multiplier=0, allow_small_or_imprecise_dtypes=True))
        link(gp.iota(g_id[:, :], [[1, NG], [0, EPG]], base=0, channel_multiplier=0, allow_small_or_imprecise_dtypes=True))
        link(gp.iota(em15[:, :], [[-1, NE]], base=NE - 1, channel_multiplier=0, allow_small_or_imprecise_dtypes=True))
        link(gp.iota(k_id[:, :], [[1, MAX_OVER]], base=0, channel_multiplier=0, allow_small_or_imprecise_dtypes=True))
        link(gp.iota(tok1[:, :], [[P, TT]], base=1, channel_multiplier=1, allow_small_or_imprecise_dtypes=True))
        link(gp.iota(b_id[:, :], [[1, WIDE]], base=0, channel_multiplier=0, allow_small_or_imprecise_dtypes=True))
        link(gp.iota(p_id[:, :], [[1, P]], base=0, channel_multiplier=0, allow_small_or_imprecise_dtypes=True))
        link(gp.memset(gpad[:, :, :], NEG))
        gp.sem_inc(consts_ready, 1)

        gp.wait_ge(mask_base, 1)
        rep = LSPAN // P
        wide = lambda i: mflt[:, i, :].unsqueeze(1).to_broadcast([P, rep, P])
        part = R[:, 8:10, :].rearrange("p a n -> p (a n)")[:, 0:LSPAN]
        lcv = LC[:, :].rearrange("p (r n) -> p r n", n=P)
        link(gp.tensor_copy(lcv, wide(0)))
        for i, radius in ((1, 256), (2, 64)):
            link(gp.tensor_copy(part.rearrange("p (r n) -> p r n", n=P), wide(i)))
            link(gp.affine_select(out=part, in_=part, compare_op=ALU.is_ge, fill=0.0, base=radius + (TT - 1) * P, pattern=[[-1, LSPAN]], channel_multiplier=1))
            link(gp.affine_select(out=part, in_=part, compare_op=ALU.is_ge, fill=0.0, base=radius - (TT - 1) * P, pattern=[[1, LSPAN]], channel_multiplier=-1))
            link(gp.tensor_tensor(LC[:, :], LC[:, :], part, ALU.add))
        gp.sem_inc(mask_ready, 1)

        zeros = R[:, 8:10, :].rearrange("p a n -> p (a n)")
        gp.wait_ge(scan_done, LRU_TILES)
        link(gp.memset(zeros, 0.0))
        gp.wait_ge(y_ready, 1)
        for b in range(NE, NBLK):
            gp.dma_start(y_dram[b * P:(b + 1) * P, :], zeros).then_inc(y_zeroed, 16)
        gp.wait_ge(y_zeroed, 16 * MAX_OVER)

        def gathers(l):
            e0 = l * NE
            gp.wait_ge(xn_ready, 4 * (2 * l + 2))
            link(gp.memset(R[:, 0:4, :], 0.0))
            gp.wait_ge(slots_ready, l + 1)
            gp.wait_ge(xn_stored, 16 * TT * (l + 1))

            def gather(col, buf, done):
                link(gp.tensor_copy(idx[buf][:, :], slot_tok[:, bass.ds(col, 1)]))
                gp.sem_inc(turn_seen, 1)
                gp.indirect_dma_start(out=xs[buf], out_offset=None, in_=xn_dram,
                                      in_offset=bass.IndirectOffsetOnAxis(ap=idx[buf][:, 0:1], axis=0),
                                      bounds_check=S - 1, oob_is_err=False).then_inc(done, 16)

            gather(0, 0, xs_filled[0])
            gather(1, 1, xs_filled[1])
            with gp.Fori(0, NE // 2 - 1) as i:
                link.enter_loop(i, 0, 2)
                for par in range(2):
                    gp.wait_ge(xs_turned, 2 * i + (par + e0 + 1))
                    gp.sem_inc(turn_seen, 1)
                    gather(2 * i + (par + 2), par, xs_filled[par])
                link.leave_loop(0, NE // 2 - 1)

            o = over[l]
            gp.wait_ge(route_ready, l + 1)
            n_over = gp.value_load(info[0:1, 7:8], min_val=0, max_val=MAX_OVER)
            gp.wait_ge(xs_turned, e0 + NE - 1)

            def gather_over(k):
                gp.tensor_copy(idx[0][:, :], slot_tok[:, bass.ds(k + NE, 1)]).then_inc(o["step"], 1)
                gp.wait_ge(o["step"], k + 1)
                gp.sem_inc(turn_seen, 1)
                gp.indirect_dma_start(out=xs[0], out_offset=None, in_=xn_dram,
                                      in_offset=bass.IndirectOffsetOnAxis(ap=idx[0][:, 0:1], axis=0),
                                      bounds_check=S - 1, oob_is_err=False).then_inc(o["xs"], 16)

            with gp.If(n_over > 0):
                gather_over(0)
            with gp.Fori(0, MAX_OVER - 1) as k:
                with gp.If(k + 1 < n_over):
                    gp.wait_ge(o["turned"], k + 1)
                    gp.sem_inc(turn_seen, 1)
                    gather_over(k + 1)
            for par in range(2):
                gp.wait_ge(yb_stored[par], 16 * (NE // 2) * (l + 1))
            gp.sem_inc(turn_seen, 1)
            with gp.If(n_over > 0):
                gp.wait_ge(o["stored"], n_over * 16 + 16)
                gp.sem_inc(turn_seen, 1)
            for t in range(TT):
                for j in range(2):
                    gp.indirect_dma_start(out=comb[j][t], out_offset=None, in_=y_dram,
                                          in_offset=bass.IndirectOffsetOnAxis(ap=yrow[:, j, t:t + 1], axis=0),
                                          bounds_check=NBLK * P - 1, oob_is_err=False).then_inc(comb_filled[t], 16)

        gathers(0)
        gathers(1)

    @block.scalar
    def _(act):
        link = Link(act, act_step)
        def load(dst_ap, src):
            act.dma_start(dst_ap, src).then_inc(params_loaded, 16)

        with nc.allow_non_contiguous_dma(reason="512 positions, once"):
            act.dma_start(cT[:, :], a["c"][0].rearrange("(p k) -> p k", k=KT)).then_inc(c_loaded, 16)
            act.wait_ge(c_loaded, 16)
            act.activation(cs[:, :], cT[:, :], ACT.Silu).then_inc(cs_ready, 1)
            load(mbc[:, :, :], a["mod_b"].rearrange("l (q p k) -> p (l q) k", p=P, k=KT))
            load(gcols[:, :, 0, :], a["norm_mix_g"].rearrange("l (p k) -> p l k", k=KT))
            load(gcols[:, :, 1, :], a["norm_ffn_g"].rearrange("l (p k) -> p l k", k=KT))
            load(rows[0:12, :], a["conv_a_w"][0].rearrange("k (j n) -> (k j) n", n=P))
            load(rows[12:28, :], a["conv_b_w"][0].rearrange("k (j n) -> (k j) n", n=P))
            load(rows[28:32, :], a["conv_b_b"][0].rearrange("(j n) -> j n", n=P))
            load(rows[32:40, :], a["lru_ba"][0].rearrange("d (j n) -> (d j) n", n=P))
            load(rows[40:48, :], a["lru_bx"][0].rearrange("d (j n) -> (d j) n", n=P))
            load(rows[48:56, :], a["lru_lambda"][0].rearrange("d (j n) -> (d j) n", n=P))
            load(posi[:, :], a["positions"][0].rearrange("(t p) -> p t", p=P))
            load(rw[:, :, :], a["router_w"].rearrange("(p k) e -> p k e", k=KT))
            load(rb[:, :], a["router_bias"].unsqueeze(0).to_broadcast([P, NE]))
            act.wait_ge(bd_zeroed, 1)
            for d in range(2):
                for w, name in enumerate(("lru_wa", "lru_wx")):
                    src = a[name][0, d].rearrange("(j two) i o -> two i j o", two=2)
                    b0 = (d * 2 + w) * LRU_TILES
                    for two in range(2):
                        act.dma_start(BD[two * 64:(two + 1) * 64, b0:b0 + LRU_TILES, two * 64:(two + 1) * 64], src[two]).then_inc(bd_loaded, 16)

        def rms(s, t):
            if s == 0:
                act.wait_ge(x_loaded, 16)
            else:
                act.wait_ge(x_ready, TT * (s - 1) + t + 1)
            if s == 1 and t == 0:
                act.wait_ge(mod_used, MOD_SPLIT * MOD_SLICES)
            link(act.activation(xnorm[s][:, t, :], X[:, t, :], ACT.Square, accum_out=stats[:, 0, t:t + 1]))
            act.activation(stats[:, 1, t:t + 1], stats[:, 0, t:t + 1], ACT.Sqrt, scale=1.0 / D, bias=eps[:, 0:1]).then_inc(rms_ready, 1)

        def take_ht(s, t):
            act.wait_ge(xn_turned, TT * s + t + 1)
            for kt in range(4):
                ins = act.activation(HT[:, kt, t * P:(t + 1) * P], ps[:, 2 * t, kt * P:(kt + 1) * P], ACT.Identity, bias=AB[:, s, 1, kt:kt + 1], scale=AB[:, s, 0, kt:kt + 1])
            ins.then_inc(ht_act, 1)
            if s == 2:
                act.wait_ge(ht_act, TT * s + t + 1)
                act.activation(ht_high[:, 0:4, t * P:(t + 1) * P], HT[:, 0:4, t * P:(t + 1) * P], ACT.Copy).then_inc(ht_high_act, 1)

        act.wait_ge(consts_ready, 1)
        for t in range(TT):
            rms(0, t)
        act.wait_ge(mod_done, 2)
        for t in range(TT):
            take_ht(0, t)
        act.wait_ge(angle_ready, 1)
        act.activation(rope[:, 4, :], rope[:, 2, :], ACT.Sin).then_inc(rope_ready, 1)
        act.activation(rope[:, 5, :], rope[:, 3, :], ACT.Sin).then_inc(rope_ready, 1)
        act.wait_ge(lam_abs, 1)
        act.activation(lru[:, 1, :], lru[:, 0, :], ACT.Exp, scale=-1.0).then_inc(lam_exp, 1)
        for j in range(LRU_TILES):
            act.wait_ge(z_ready, j + 1)
            if j:
                act.wait_ge(xr_ready, j)
            act.activation(u_in, ps[:, j, :], ACT.Copy).then_inc(z_act, 1)
        act.wait_ge(mask_ready, 1)
        act.wait_ge(dec_ready, 1)

        def take_z(t):
            j = t % 4
            act.wait_ge(z_ready, t + 1)
            act.activation(mixT[:, LRU_TILES + j if t < 8 else j, :], ps[:, z_bank(t), :], ACT.Gelu_apprx_tanh if t < 8 else ACT.Copy).then_inc(z_act, 1)

        for j in range(LRU_TILES):
            take_z(4 + 2 * j)
            act.wait_ge(gate_ready, j + 1)
            if j:
                act.wait_ge(scan_done, j)
            for d in range(2):
                c = d * LRU_TILES + j
                link(act.activation(th[d], ps[:, 2 * d, :], ACT.Tanh, bias=hbias[:, c:c + 1], scale=0.5))
                link(act.activation(ti[d], ps[:, 2 * d + 1, :], ACT.Tanh, bias=hbias[:, 8 + c:9 + c], scale=0.5))
                if d == 1:
                    act.sem_inc(gate_read, 1)
                link(act.activation(av[d], th[d], ACT.Exp, bias=dec[:, 0, c:c + 1], scale=dec[:, 0, c:c + 1]))
                act.activation(th[d], th[d], ACT.Tanh, bias=dec[:, 1, c:c + 1], scale=dec[:, 1, c:c + 1]).then_inc(m_ready, 1)
            take_z(5 + 2 * j)
            for d in range(2):
                act.wait_ge(mult_ready, 4 * j + d + 1)
                act.activation(th[d], th[d], ACT.Sqrt, scale=0.25).then_inc(m_ready, 1)

        def experts(l):
            s = 2 * l + 1
            e0 = l * NE
            for t in range(TT + 1):
                if t < TT:
                    rms(s, t)
                if t:
                    act.wait_ge(logit_ready, TT * l + t)
                    act.activation(rt[:, (t - 1) * NE:t * NE], ps[:, 0, (t - 1) * NE:t * NE], ACT.Sigmoid).then_inc(score_ready, 1)
                if t < TT:
                    take_ht(s, t)
                    act.dma_start(xn_dram[t * P:(t + 1) * P, :], xnorm[s][:, t, :]).then_inc(xn_stored, 16)
            if l == 1:
                act.dma_start(G[:, 0, :], a["final_norm_g"].unsqueeze(0).to_broadcast([P, D])).then_inc(fg_loaded, 16)
            def xst(e, par, first=False):
                if not first:
                    act.wait_ge(up_done, e + (e0 - 1))
                act.wait_ge(xs_turned, e + (e0 + 1))
                for kt in range(4):
                    ins = act.activation(xsT[par][:, kt, :], ps[:, 0, kt * P:(kt + 1) * P], ACT.Identity, bias=AB[:, s, 1, kt:kt + 1], scale=AB[:, s, 0, kt:kt + 1])
                ins.then_inc(xst_act, 1)
                act.wait_ge(xst_act, e + (e0 + 1))
                act.activation(xs_high[l][par][:, 0:4, :], xsT[par][:, 0:4, :], ACT.Copy).then_inc(xs_high_ready, 1)

            def high(c, e, par, turn, chunk, first=False):
                wait_slab(act, ("exp", l, c, par), turn)
                if not first:
                    act.wait_ge((gate_done, up_done)[c], e + e0)
                w, top, _ = split_of(l, c, par, chunk)
                act.activation(top, w, ACT.Copy).then_inc(high_ready[c], 1)

            def take_hid(e, first=False):
                act.wait_ge(hid_turned, e + (e0 + 1))
                if not first:
                    act.wait_ge(down_done, e + e0)
                act.activation(hidT, ps[:, 4, :].rearrange("p (f n) -> p f n", n=P), ACT.Copy).then_inc(hidt_ready, 1)

            def step(e, par, turn, first=0, last=False):
                high(1, e, par, turn, 0, first == 1)
                if first != 1:
                    take_hid(e - 1, first == 2)
                high(1, e, par, turn, 1, first == 1)
                act.wait_ge(gate_done, e + (e0 + 1))
                if first != 1:
                    act.wait_ge(hid_ready, e + e0)
                act.activation(sg, ps[:, 2, :], ACT.Silu).then_inc(silu_done, 1)
                if not last:
                    for chunk in range(2):
                        high(0, e + 1, 1 - par, turn + par, chunk)
                    xst(e + 1, 1 - par, first == 1)

            for chunk in range(2):
                high(0, 0, 0, 0, chunk, True)
            xst(0, 0, True)
            step(0, 0, 0, first=1)
            step(1, 1, 0, first=2)
            with act.Fori(1, NE // 2 - 1) as i:
                for par in range(2):
                    step(2 * i + par, par, i)
            step(NE - 2, 0, NE // 2 - 1)
            step(NE - 1, 1, NE // 2 - 1, last=True)
            take_hid(NE - 1)

            o = over[l]
            act.wait_ge(route_ready, l + 1)
            n_over = act.value_load(info[0:1, 7:8], min_val=0, max_val=MAX_OVER)
            with act.Fori(0, MAX_OVER) as k:
                with act.If(k < n_over):
                    act.wait_ge(o["turned"], k + 1)
                    for kt in range(4):
                        ins = act.activation(xsT[0][:, kt, :], ps[:, 0, kt * P:(kt + 1) * P], ACT.Identity, bias=AB[:, s, 1, kt:kt + 1], scale=AB[:, s, 0, kt:kt + 1])
                    ins.then_inc(o["xst"], 1)
                    act.wait_ge(o["gate"], k + 1)
                    act.activation(sg, ps[:, 2, :], ACT.Silu).then_inc(o["silu"], 1)
                    act.wait_ge(o["hidt_in"], k + 1)
                    act.activation(hidT, ps[:, 4, :].rearrange("p (f n) -> p f n", n=P), ACT.Copy).then_inc(o["hidt"], 1)

        experts(0)
        def high_qkv(w, chunk):
            wait_slab(act, ("qkv", w))
            if w:
                act.wait_ge(*((qkv_chunk, w) if chunk == 0 else (qkv_ready, 4 * w)))
            plain, top, _ = qkv_split_of(w, chunk)
            act.activation(top, plain, ACT.Copy).then_inc(qkv_high, 1)

        high_qkv(0, 0)
        high_qkv(0, 1)
        rms(2, 0)
        for t in range(1, TT):
            rms(2, t)
            take_ht(2, t - 1)
        take_ht(2, TT - 1)
        for w in range(6):
            if w:
                high_qkv(w, 1)
            if w + 1 < 6:
                high_qkv(w + 1, 0)
            dest = (Q, K, V)[w // 2]
            for t in (0, 2):
                act.wait_ge(qkv_ready, 4 * w + t + 1)
                act.activation(dest[:, t, (w % 2) * HALF:(w % 2) * HALF + HALF], ps[:, (4 * w + t) % 6, :], ACT.Copy).then_inc(qkv_act, 1)
        for hp in range(8):
            act.wait_ge(qt_turned, hp + 1)
            act.activation(QT[:, hp, :], ps[:, (2 * hp) % 8, :], ACT.Copy).then_inc(qt_ready, 1)

        def exp_step(v):
            act.wait_ge(max_ready, v + 1)
            act.activation(prob[v % 4], prob[v % 4], ACT.Exp, bias=nmx[:, v:v + 1], accum_out=ssum[:, v:v + 1]).then_inc(p_ready, 1)

        exp_step(0)
        exp_step(1)
        for u in range(64):
            if u + 2 < 64:
                exp_step(u + 2)
            if u % 2 == 0:
                act.wait_ge(p_turned, u + 1)
                if u >= 4:
                    act.wait_ge(av_ready, u - 3)
                act.activation(probT[u % 4], ps[:, 3 + u % 2, :], ACT.Copy).then_inc(pt_act, 1)
        for kt in range(0, KT, 2):
            act.wait_ge(o_turned, kt + 1)
            act.activation(OT[:, kt, :], ps[:, kt, :], ACT.Copy).then_inc(ot_act, 1)
        experts(1)
        for t in range(TT):
            rms(4, t)

    @block.vector
    def _(v):
        link = Link(v, dve_step)
        ts, tt_, stt = v.tensor_scalar, v.tensor_tensor, v.scalar_tensor_tensor

        def mod_acc(n, m0, count):
            for m in range(m0, m0 + count):
                g = n * MOD_SLICES + m
                dest, w = acc[n % 2], mod_place(g)
                v.wait_ge(mod_filled[g % MOD_RING], 16 * (g // MOD_RING + 1))
                if m == 0:
                    ins = ts(dest, w, cs[:, 0:1], None, ALU.mult)
                else:
                    ins = stt(dest, w, cs[:, m:m + 1], dest, ALU.mult, ALU.add)
                ins.then_inc(mod_used, 1)
                v.wait_ge(mod_used, g + 1)
            if m0 + count == MOD_SLICES:
                v.sem_inc(acc_ready, 1)

        def mod_take(n):
            l, q = part_of(n)
            v.wait_ge(mod_reduced, n + 1)
            if q in (2, 5):
                g = 2 * l + q // 5
                v.wait_ge(g_bias_loaded[g], 16)
                link(tt_(G[:, g, 0:HALF], ps[:, 6, :], G[:, g, 0:HALF], ALU.add))
                tt_(G[:, g, HALF:D], ps[:, 7, :], G[:, g, HALF:D], ALU.add).then_inc(mod_done, 1)
            else:
                w = 2 * l + q // 3
                if q % 3 == 0:
                    tt_(AB[:, w, 1, :], ps[:, 7, 0:KT], mbc[:, n, :], ALU.add).then_inc(mod_done, 1)
                else:
                    link(tt_(AB[:, w, 0, :], ps[:, 7, 0:KT], mbc[:, n, :], ALU.add))
                    stt(AB[:, w, 0, :], AB[:, w, 0, :], 1.0, gcols[:, l, q // 3, :], ALU.add, ALU.mult).then_inc(mod_done, 1)
            v.wait_ge(mod_done, n + 1)

        def scale_x(s, t):
            v.wait_ge(rms_ready, TT * s + t + 1)
            r = stats[:, 2, t:t + 1]
            link(v.reciprocal(r, stats[:, 1, t:t + 1]))
            if s < 4:
                ts(xnorm[s][:, t, :], X[:, t, :], r, None, ALU.mult).then_inc(xn_ready, 1)
            else:
                if t == 0:
                    v.wait_ge(fg_loaded, 16)
                stt(XN[:, t, :], X[:, t, :], r, G[:, 0, :], ALU.mult, ALU.mult).then_inc(final_ready, 1)

        def take_ht(s, t):
            v.wait_ge(xn_turned, TT * s + t + 1)
            for kt in range(4, KT):
                ins = ts(HT[:, kt, t * P:(t + 1) * P], ps[:, 2 * t + 1, (kt - 4) * P:(kt - 3) * P], AB[:, s, 0, kt:kt + 1], AB[:, s, 1, kt:kt + 1], ALU.mult, ALU.add)
            if s != 2:
                ins.then_inc(ht_dve, 1)
                return
            cut = slice(t * P, (t + 1) * P)
            ins.then_inc(ht_full, 1)
            v.wait_ge(ht_full, t + 1)
            v.tensor_copy(ht_high[:, 4:8, cut], HT[:, 4:8, cut]).then_inc(ht_high_dve, 1)
            v.wait_ge(ht_high_dve, t + 1)
            v.wait_ge(ht_high_act, t + 1)
            tt_(HT_r[:, :, cut], HT[:, :, cut], ht_high[:, :, cut].bitcast(F32), ALU.subtract).then_inc(ht_dve, 1)

        v.wait_ge(cs_ready, 1)
        mod_acc(0, 0, 8)

        v.wait_ge(consts_ready, 1)
        mi = mlow
        mtmp = mflt[:, 3, :].bitcast(I32)
        m16, m4 = mflt[:, 0, :], mflt[:, 1, :]
        link(ts(mtmp, mi, 15, None, ALU.bitwise_and))
        link(ts(m16, mtmp, 0, None, ALU.is_equal))
        link(ts(mtmp, mi, 3, None, ALU.bitwise_and))
        link(ts(m4, mtmp, 0, None, ALU.is_equal))
        L2, L3 = 8.0 * float(np.log(2.0)), 8.0 * float(np.log(3.0))
        f2 = mflt[:, 2, :]
        t3 = mflt[:, 3, :]
        link(ts(f2, m16, L3 - L2, None, ALU.mult))
        link(stt(f2, m4, L2, f2, ALU.mult, ALU.add))
        link(ts(t3, m4, -NEG, NEG, ALU.mult, ALU.add))
        link(stt(t3, m16, L2, t3, ALU.mult, ALU.add))
        link(tt_(f2, f2, t3, ALU.subtract))
        link(ts(m16, m16, -NEG, NEG, ALU.mult, ALU.add))
        link(tt_(m4, t3, m16, ALU.subtract))
        v.sem_inc(mask_base, 1)

        for t in range(TT):
            scale_x(0, t)
            mod_acc(1, 2 * t, 2)
        v.wait_ge(params_loaded, 16 * N_PARAMS)
        mod_take(0)
        mod_take(1)
        for t in range(TT):
            take_ht(0, t)

        link(v.tensor_copy(posf[:, :], posi[:, :]))
        ang, nn, red, co = (rope[:, i, :] for i in range(4))
        as3 = lambda x: x.rearrange("p (t r) -> p t r", r=ROT)
        link(tt_(as3(ang), posf[:, :].unsqueeze(2).to_broadcast([P, TT, ROT]), invf[:, :].unsqueeze(1).to_broadcast([P, TT, ROT]), ALU.mult))
        link(ts(nn, ang, float(1.0 / (2.0 * np.pi)), MAGIC, ALU.mult, ALU.add))
        link(ts(nn, nn, -MAGIC, None, ALU.add))
        two_pi = 2.0 * np.pi
        c1 = 6.28125
        c2 = float(np.float32(int((two_pi - c1) * 2 ** 20) / 2 ** 20))
        c3 = float(two_pi - c1 - c2)
        link(stt(red, nn, -c1, ang, ALU.mult, ALU.add))
        link(stt(red, nn, -c2, red, ALU.mult, ALU.add))
        link(stt(red, nn, -c3, red, ALU.mult, ALU.add))
        link(ts(red, red, 3.1415925, -3.1415925, ALU.min, ALU.max))
        link(ts(co, red, -1.0, None, ALU.mult))
        link(tt_(co, co, red, ALU.max))
        link(ts(co, co, -1.0, float(np.pi / 2), ALU.mult, ALU.add))
        v.sem_inc(angle_ready, 1)

        v.wait_ge(cols_turned, 1)
        link(v.tensor_copy(cols[:, :], ps[:, 7, 64:120]))
        link(ts(hbias[:, :], cols[:, 32:48], 0.5, None, ALU.mult))
        lam = cols[:, 48:56]
        link(ts(lru[:, 0, :], lam, -1.0, None, ALU.mult))
        link(tt_(lru[:, 0, :], lru[:, 0, :], lam, ALU.max))
        v.sem_inc(lam_abs, 1)
        v.wait_ge(lam_exp, 1)
        e_, s_, t_, y_ = lru[:, 1, :], lru[:, 2, :], lru[:, 3, :], lru[:, 4, :]
        link(ts(s_, e_, 2.0, None, ALU.add))
        link(v.reciprocal(s_, s_))
        link(tt_(s_, s_, e_, ALU.mult))
        link(tt_(t_, s_, s_, ALU.mult))
        link(ts(y_, t_, 1.0 / 17.0, None, ALU.mult))
        for k in range(15, 1, -2):
            link(stt(y_, y_, 1.0 / k, t_, ALU.add, ALU.mult))
        link(stt(y_, y_, 1.0, s_, ALU.add, ALU.mult))
        link(ts(t_, lam, -1.0, 0.0, ALU.mult, ALU.max))
        link(stt(t_, y_, 2.0, t_, ALU.mult, ALU.add))
        link(ts(dec[:, 0, :], t_, -4.0, None, ALU.mult))
        ts(dec[:, 1, :], t_, 4.0, None, ALU.mult).then_inc(dec_ready, 1)

        def col(i):
            return cols[:, i:i + 1]

        def conv_b(j):
            v.wait_ge(z_act, j + 1)
            u, x = u_in, xr[j]
            w = lambda k: col(12 + 4 * k + j)
            link(ts(x, u, w(1), col(28 + j), ALU.mult, ALU.add))
            link(stt(x[:, 1:S], u[:, 0:S - 1], w(0), x[:, 1:S], ALU.mult, ALU.add))
            link(stt(x[:, 0:S - 1], u[:, 1:S], w(2), x[:, 0:S - 1], ALU.mult, ALU.add))
            stt(x[:, 0:S - 2], u[:, 2:S], w(3), x[:, 0:S - 2], ALU.mult, ALU.add).then_inc(xr_ready, 1)
            v.wait_ge(xr_ready, j + 1)

        def gates_in(j):
            for d in range(2):
                v.wait_ge(m_ready, 4 * j + d + 1)
                link(tt_(tmp0, av[d], av[d], ALU.mult))
                stt(th[d], tmp0, 1.0, th[d], ALU.add, ALU.mult).then_inc(mult_ready, 1)
                v.wait_ge(mult_ready, 4 * j + d + 1)
                link(stt(ti[d], ti[d], 1.0, xr[j], ALU.add, ALU.mult))

        def gates_out(j):
            for d in range(2):
                v.wait_ge(m_ready, 4 * j + 2 + d + 1)
                link(tt_(ti[d], ti[d], th[d], ALU.mult))
                if d == 0:
                    x0, x1, o_ = av[0], ti[0], th[0]
                else:
                    x0, x1, o_ = av[1][:, ::-1], ti[1][:, ::-1], th[1][:, ::-1]
                v.tensor_tensor_scan(o_, x0, x1, 0.0, ALU.mult, ALU.add).then_inc(mult_ready, 1)
                v.wait_ge(mult_ready, 4 * j + 2 + d + 1)
            link(tt_(tmp0, th[0], th[1], ALU.add))
            v.sem_inc(scan_done, 1)
            tt_(mixT[:, LRU_TILES + j, :], mixT[:, LRU_TILES + j, :], tmp0, ALU.mult).then_inc(mix_ready, 1)
            v.wait_ge(mix_ready, j + 1)

        def val(j):
            t = 12 + j
            v.wait_ge(z_ready, t + 1)
            v.wait_ge(z_act, 8 + j + 1)
            m = mixT[:, j, :]
            tt_(m, ps[:, z_bank(t), :], m, ALU.mult).then_inc(z_dve, 1)
            v.wait_ge(z_dve, j + 1)
            c_ = xr[j]
            w = lambda k: col(4 * k + j)
            link(ts(c_, m, w(1), None, ALU.mult))
            link(stt(c_[:, 1:S], m[:, 0:S - 1], w(0), c_[:, 1:S], ALU.mult, ALU.add))
            link(stt(c_[:, 0:S - 1], m[:, 1:S], w(2), c_[:, 0:S - 1], ALU.mult, ALU.add))

        def gb(j):
            t = 16 + j
            v.wait_ge(z_ready, t + 1)
            tt_(mixT[:, j, :], ps[:, z_bank(t), :], xr[j], ALU.mult).then_inc(z_dve, 1)

        conv_b(0)
        conv_b(1)
        conv_b(2)
        mod_acc(2, 0, 2)
        conv_b(3)
        mod_acc(2, 2, 6)
        gates_in(0)
        mod_acc(3, 0, 3)
        gates_out(0)
        mod_acc(3, 3, 2)
        mod_take(2)
        gates_in(1)
        mod_acc(3, 5, 3)
        gates_out(1)
        mod_acc(4, 0, 2)
        gates_in(2)
        mod_acc(4, 2, 4)
        gates_out(2)
        mod_acc(4, 6, 2)
        mod_take(3)
        gates_in(3)
        mod_acc(5, 0, 3)
        gates_out(3)
        mod_acc(5, 3, 2)
        mod_take(4)
        val(0)
        mod_acc(5, 5, 3)
        val(1)
        mod_acc(6, 0, 2)
        mod_take(5)
        val(2)
        mod_acc(6, 2, 3)
        val(3)
        mod_acc(6, 5, 3)
        gb(0)
        mod_acc(7, 0, 2)
        gb(1)
        mod_acc(7, 2, 2)
        mod_take(6)
        gb(2)
        mod_acc(7, 4, 2)
        gb(3)
        mod_acc(7, 6, 2)

        def residual(l, t):
            v.wait_ge(y_ready, 8 * l + 2 * t + 2)
            link(tt_(pair(2 * t), pair(2 * t), G[:, 2 * l, :], ALU.mult))
            tt_(X[:, t, :], pair(2 * t), X[:, t, :], ALU.add).then_inc(x_ready, 1)
            v.wait_ge(x_ready, TT * 2 * l + t + 1)

        def low_qkv(w, chunk):
            v.wait_ge(qkv_high, 2 * w + chunk + 1)
            plain, top, rest = qkv_split_of(w, chunk)
            tt_(rest, plain, top.bitcast(F32), ALU.subtract).then_inc(qkv_low, 1)

        n = TT * NE
        sc, bia, o1, o2, t0, t1, t2, t3 = (rt[:, i * n:(i + 1) * n] for i in range(8))
        b0 = 8 * n
        grp = lambda t, i: rt[:, b0 + t * 40 + 4 * i:b0 + t * 40 + 4 * i + 4]
        b1 = b0 + TT * 40
        cmp_, inc, exc = (rt[:, b1 + 16 * i:b1 + 16 + 16 * i] for i in range(3))
        s12 = rt[:, b1 + 48:b1 + 64]
        sel = rt[:, b1 + 64:b1 + 72]
        cond = rt[:, b1 + 80:b1 + 80 + MAX_OVER * NE]
        v3 = lambda x: x.rearrange("p (t e) -> p t e", t=TT)
        bc_e = lambda x: x.unsqueeze(1).to_broadcast([P, TT, NE])

        def choose(l, t):
            v.wait_ge(score_ready, TT * l + t + 1)
            cut = slice(t * NE, (t + 1) * NE)
            b, m = bia[:, cut], t1[:, cut]
            hi, lo = rt[:, b0 + t * 40:b0 + t * 40 + 8], rt[:, b0 + t * 40 + 8:b0 + t * 40 + 16]
            hm, lm, h1, gi = (grp(t, i) for i in range(4, 8))
            ef = rt[:, b0 + t * 40 + 32:b0 + t * 40 + 40]
            link(tt_(b, sc[:, cut], rb[:, :], ALU.add))
            link(tt_(hi, b[:, 0:NE:2], b[:, 1:NE:2], ALU.max))
            link(tt_(lo, b[:, 0:NE:2], b[:, 1:NE:2], ALU.min))
            link(tt_(hm, hi[:, 0:8:2], hi[:, 1:8:2], ALU.min))
            link(tt_(lm, lo[:, 0:8:2], lo[:, 1:8:2], ALU.max))
            link(tt_(h1, hi[:, 0:8:2], hi[:, 1:8:2], ALU.max))
            link(tt_(hm, hm, lm, ALU.max))
            link(tt_(gpad[:, t, 0:NG], h1, hm, ALU.add))
            link(v.max(mx8[:, t, :], gpad[:, t, :]))
            link(v.max_index(ix8[:, t, :], mx8[:, t, :], gpad[:, t, :]))
            link(v.tensor_copy(gi[:, 0:1], ix8[:, t, 0:1]))
            link(ts(m, g_id[:, :], gi[:, 0:1], NEG, ALU.not_equal, ALU.mult))
            link(tt_(m, m, b, ALU.add))
            link(v.max(mx8[:, t, :], m))
            link(v.max_index(ix8[:, t, :], mx8[:, t, :], m))
            link(v.tensor_copy(ef, ix8[:, t, :]))
            link(ts(o1[:, cut], e_id[:, :], ef[:, 0:1], None, ALU.is_equal))
            link(ts(o2[:, cut], e_id[:, :], ef[:, 1:2], None, ALU.is_equal))
            tt_(hot[:, t, :], o1[:, cut], o2[:, cut], ALU.add).then_inc(hot_ready, 1)

        def route(l):
            v.wait_ge(rank_ready, l + 1)
            rank, cnt = ps[:, 1, 0:n], ps[:, 1, n:n + NE]
            link(ts(cmp_, cnt, float(P), None, ALU.is_gt))
            for i in range(2, TT):
                link(stt(cmp_, cnt, float(i * P), cmp_, ALU.is_gt, ALU.add))
            link(v.tensor_tensor_scan(inc, ones[:, 0:NE], cmp_, 0.0, ALU.mult, ALU.add))
            link(tt_(exc, inc, cmp_, ALU.subtract))
            link(tt_(exc, exc, em15[:, :], ALU.add))
            link(stt(v3(t1), v3(rank), float(P), bc_e(exc), ALU.is_ge, ALU.mult))
            link(tt_(v3(t1), v3(t1), bc_e(e_id[:, :]), ALU.add))
            link(stt(t0, t1, float(P), rank, ALU.mult, ALU.add))
            both = rt[:, 2 * n:4 * n]
            pair_t = rt[:, 6 * n:8 * n]
            link(tt_(pair_t.rearrange("p (j x) -> p j x", j=2), both.rearrange("p (j x) -> p j x", j=2), t0.unsqueeze(1).to_broadcast([P, 2, n]), ALU.mult))
            link(v.tensor_reduce(dst[:, :, :].rearrange("p j t -> p (j t)"), pair_t.rearrange("p (x e) -> p x e", e=NE), AX_X, ALU.add))
            link(v.tensor_copy(yrow[:, :, :], dst[:, :, :]))
            yr = yrow[:, :, :].rearrange("p a b -> p (a b)")
            link(ts(ytmp[:, 0, :], yr, 7, None, ALU.arith_shift_right))
            link(ts(ytmp[:, 1, :], yr, P - 1, None, ALU.bitwise_and))
            link(v.tensor_copy(yplace[:, :, :], ytmp[:, :, :]))
            if l == 0:
                v.wait_ge(y_zeroed, 16 * MAX_OVER)
            nx = 2 * TT
            link(tt_(place_hot, p_id[:, :].unsqueeze(1).to_broadcast([P, nx, P]), yplace[:, 1, :].unsqueeze(2).to_broadcast([P, nx, P]), ALU.is_equal))
            at = rt[:, b1 + 80:b1 + 80 + nx * WIDE].rearrange("p (a b) -> p a b", b=WIDE)
            link(tt_(at, b_id[:, :].unsqueeze(1).to_broadcast([P, nx, WIDE]), yplace[:, 0, :].unsqueeze(2).to_broadcast([P, nx, WIDE]), ALU.is_equal))
            for j in range(2):
                ins = tt_(block_tok[:, j * TT:(j + 1) * TT, :], at[:, j * TT:(j + 1) * TT, :], tok1[:, :].unsqueeze(2).to_broadcast([P, TT, WIDE]), ALU.mult)
            ins.then_inc(place_ready, 1)
            v.wait_ge(place_ready, l + 1)
            v.wait_ge(slots_summed, l + 1)
            slots = ps[:, 2, 0:WIDE]
            link(ts(empty[:, :], slots, 0.0, float(NO_TOKEN), ALU.is_equal, ALU.mult))
            stt(slot_tok[:, :], slots, -1.0, empty[:, :], ALU.add, ALU.add).then_inc(slots_ready, 1)
            v.wait_ge(slots_ready, l + 1)
            cv = cond.rearrange("p (k e) -> p k e", e=NE)
            link(tt_(cv, inc.unsqueeze(1).to_broadcast([P, MAX_OVER, NE]), k_id[:, :].unsqueeze(2).to_broadcast([P, MAX_OVER, NE]), ALU.is_le))
            link(v.tensor_reduce(sel[:, 0:MAX_OVER], cv, AX_X, ALU.add))
            link(ts(sel[:, 0:MAX_OVER], sel[:, 0:MAX_OVER], float(NE - 1), None, ALU.min))
            link(v.tensor_copy(sel[:, MAX_OVER:8], inc[:, NE - 1:NE]))
            v.tensor_copy(info[:, :], sel).then_inc(route_ready, 1)
            v.wait_ge(route_ready, l + 1)
            link(tt_(pair_t.rearrange("p (j x) -> p j x", j=2), both.rearrange("p (j x) -> p j x", j=2), sc.unsqueeze(1).to_broadcast([P, 2, n]), ALU.mult))
            link(v.tensor_reduce(s12[:, 0:8], pair_t.rearrange("p (x e) -> p x e", e=NE), AX_X, ALU.add))
            link(tt_(s12[:, 8:12], s12[:, 0:4], s12[:, 4:8], ALU.add))
            link(v.reciprocal(s12[:, 12:16], s12[:, 8:12]))
            link(tt_(comb_w[:, 0, :], s12[:, 0:4], s12[:, 12:16], ALU.mult))
            link(tt_(comb_w[:, 1, :], s12[:, 4:8], s12[:, 12:16], ALU.mult))

        def experts(l):
            s = 2 * l + 1
            e0 = l * NE
            for t in range(TT + 1):
                if t < TT:
                    residual(l, t)
                    if l == 0 and t == 0:
                        mod_take(MOD_SPLIT - 1)
                    scale_x(s, t)
                if t:
                    choose(l, t - 1)
                if t < TT:
                    take_ht(s, t)
            route(l)

            def xst(e, par, first=False):
                if not first:
                    v.wait_ge(up_done, e + (e0 - 1))
                v.wait_ge(xs_turned, e + (e0 + 1))
                for kt in range(4, KT):
                    ins = ts(xsT[par][:, kt, :], ps[:, 1, (kt - 4) * P:(kt - 3) * P], AB[:, s, 0, kt:kt + 1], AB[:, s, 1, kt:kt + 1], ALU.mult, ALU.add)
                ins.then_inc(xst_turned, 1)
                v.wait_ge(xst_turned, e + (e0 + 1))
                v.tensor_copy(xs_high[l][par][:, 4:8, :], xsT[par][:, 4:8, :]).then_inc(xst_split, 1)
                v.wait_ge(xst_split, e + (e0 + 1))
                v.wait_ge(xs_high_ready, e + (e0 + 1))
                tt_(xs_low[par], xsT[par], xs_high[l][par].bitcast(F32), ALU.subtract).then_inc(xst_dve, 1)

            def low(c, e, par, chunk):
                v.wait_ge(high_ready[c], 2 * e + (2 * e0 + chunk + 1))
                w, top, rest = split_of(l, c, par, chunk)
                tt_(rest, w, top.bitcast(F32), ALU.subtract).then_inc(low_ready[c], 1)

            def scale_y(buf, done):
                for h in range(2):
                    ins = tt_(buf[:, h * HALF:h * HALF + HALF], ps[:, 5 + h, :], G[:, 2 * l + 1, h * HALF:h * HALF + HALF], ALU.mult)
                ins.then_inc(done, 1)

            def take_y(e, par, stored):
                v.wait_ge(down_done, e + (e0 + 1))
                if stored is not None:
                    v.wait_ge(yb_stored[par], stored * 16 + (NE // 2) * l * 16)
                scale_y(ybuf[par], yb_ready)

            def step(e, par, stored=None, first=False, last=False):
                for chunk in range(2):
                    low(1, e, par, chunk)
                if not last:
                    for chunk in range(2):
                        low(0, e + 1, 1 - par, chunk)
                if not first:
                    take_y(e - 1, 1 - par, stored)
                if not last:
                    xst(e + 1, 1 - par, first)
                v.wait_ge(silu_done, e + (e0 + 1))
                v.wait_ge(up_done, e + (e0 + 1))
                tt_(hid, ps[:, 3, :], sg, ALU.mult).then_inc(hid_ready, 1)

            for chunk in range(2):
                low(0, 0, 0, chunk)
            xst(0, 0, True)
            step(0, 0, first=True)
            step(1, 1)
            step(2, 0)
            step(3, 1, 1)
            with v.Fori(2, NE // 2 - 1) as i:
                step(2 * i, 0, i - 1)
                step(2 * i + 1, 1, i)
            step(NE - 2, 0, NE // 2 - 2)
            step(NE - 1, 1, NE // 2 - 1, last=True)
            take_y(NE - 1, 1, NE // 2 - 1)

            o = over[l]
            v.wait_ge(yb_stored[0], 16 * (NE // 2) * (l + 1))
            n_over = v.value_load(info[0:1, 7:8], min_val=0, max_val=MAX_OVER)
            with v.Fori(0, MAX_OVER) as k:
                with v.If(k < n_over):
                    v.wait_ge(o["turned"], k + 1)
                    for kt in range(4, KT):
                        ins = ts(xsT[0][:, kt, :], ps[:, 1, (kt - 4) * P:(kt - 3) * P], AB[:, s, 0, kt:kt + 1], AB[:, s, 1, kt:kt + 1], ALU.mult, ALU.add)
                    ins.then_inc(o["xst"], 1)
                    v.wait_ge(o["silu"], k + 1)
                    v.wait_ge(o["gu"], k + 1)
                    tt_(hid, ps[:, 3, :], sg, ALU.mult).then_inc(o["hid"], 1)
                    v.wait_ge(o["down"], k + 1)
                    v.wait_ge(o["stored"], (k + 1) * 16)
                    scale_y(ybuf[0], o["yb"])

            def combine(t):
                v.wait_ge(comb_filled[t], 32 * (l + 1))
                link(stt(X[:, t, :], comb[0][t], comb_w[:, 0, t:t + 1], X[:, t, :], ALU.mult, ALU.add))
                stt(X[:, t, :], comb[1][t], comb_w[:, 1, t:t + 1], X[:, t, :], ALU.mult, ALU.add).then_inc(x_ready, 1)
                v.wait_ge(x_ready, TT * (2 * l + 1) + t + 1)

            if l == 0:
                low_qkv(0, 0)
                low_qkv(0, 1)
            combine(0)
            for t in range(TT):
                if t + 1 < TT:
                    combine(t + 1)
                scale_x(s + 1, t)
                if l == 0 and t:
                    take_ht(2, t - 1)
            if l == 0:
                take_ht(2, TT - 1)

        experts(0)
        def rotate(z, n):
            v.wait_ge(qkv_act, 4 * n)
            zv = z.rearrange("p t (h d) -> p t h d", d=HD)
            z1, z2 = zv[:, :, :, 0:ROT], zv[:, :, :, ROT:2 * ROT]
            bc = lambda x: x.rearrange("p (t r) -> p t r", r=ROT).unsqueeze(2).to_broadcast([P, TT, HEADS, ROT])
            sin, cos = bc(rope[:, 4, :]), bc(rope[:, 5, :])
            r4 = [x.rearrange("p (t h r) -> p t h r", h=HEADS, r=ROT) for x in rots]
            link(tt_(r4[0], z1, cos, ALU.mult))
            link(tt_(r4[1], z2, sin, ALU.mult))
            link(tt_(r4[2], z2, cos, ALU.mult))
            link(tt_(r4[3], z1, sin, ALU.mult))
            link(tt_(z1, r4[0], r4[1], ALU.subtract))
            link(tt_(z2, r4[2], r4[3], ALU.add))
            v.sem_inc(rot_ready, 1)

        v.wait_ge(rope_ready, 2)
        summed = 0

        def sum_slices(count):
            for i in range(summed, summed + count):
                if i % MOD_SLICES == 0 and i >= 2 * MOD_SLICES:
                    mod_take(MOD_SPLIT + i // MOD_SLICES - 2)
                mod_acc(MOD_SPLIT + i // MOD_SLICES, i % MOD_SLICES, 1)
            return summed + count

        for w in range(6):
            if w:
                low_qkv(w, 1)
            if w in (2, 4):
                v.wait_ge(qkv_dve, 2 * w)
                rotate((Q, K)[w // 2 - 1], w // 2)
            summed = sum_slices(QKV_SLICES[w] // 2)
            if w + 1 < 6:
                low_qkv(w + 1, 0)
            dest = (Q, K, V)[w // 2]
            for t in (1, 3):
                v.wait_ge(qkv_ready, 4 * w + t + 1)
                v.tensor_copy(dest[:, t, (w % 2) * HALF:(w % 2) * HALF + HALF], ps[:, (4 * w + t) % 6, :]).then_inc(qkv_dve, 1)
                if t == 1:
                    summed = sum_slices(QKV_SLICES[w] - QKV_SLICES[w] // 2)
        mod_take(LAYERS * PARTS - 2)
        mod_take(LAYERS * PARTS - 1)
        for hp in range(8):
            v.wait_ge(kt_turned, hp + 1)
            v.tensor_copy(KTR[:, hp, :], ps[:, (2 * hp + 1) % 8, :]).then_inc(kt_ready, 1)

        def score_step(n):
            it = (n // 2) % TT
            v.wait_ge(s_ready, n + 1)
            if n >= 4:
                v.wait_ge(p_turned, n - 3)
            lc = LC[:, (TT - 1 - it) * P:(TT - 1 - it) * P + S]
            link(v.tensor_tensor_reduce(prob[n % 4], ps[:, n % 3, :], lc, HD ** -0.5, -3.0e38, ALU.add, ALU.max, mx[:, n:n + 1]))
            ts(nmx[:, n:n + 1], mx[:, n:n + 1], -1.0, None, ALU.mult).then_inc(max_ready, 1)

        def head_out(hp):
            v.wait_ge(av_ready, 8 * hp + 8)
            link(v.reciprocal(rsum[:, 8 * hp:8 * hp + 8], ssum[:, 8 * hp:8 * hp + 8]))
            o4 = O[:, :, hp * P:(hp + 1) * P].rearrange("p t (h d) -> p t h d", d=HD)
            p4 = ps[:, 5 + hp % 2, :].rearrange("p (t h d) -> p t h d", h=2, d=HD)
            r4 = rsum[:, 8 * hp:8 * hp + 8].rearrange("p (t h) -> p t h", h=2).unsqueeze(3).to_broadcast([P, TT, 2, HD])
            tt_(o4, p4, r4, ALU.mult).then_inc(o_ready, 1)

        v.wait_ge(mask_ready, 1)
        v.wait_ge(kt_turned, 8)
        score_step(0)
        score_step(1)
        for u in range(64):
            if u + 2 < 64:
                score_step(u + 2)
            if u % 2 == 1:
                v.wait_ge(p_turned, u + 1)
                if u >= 4:
                    v.wait_ge(av_ready, u - 3)
                v.tensor_copy(probT[u % 4], ps[:, 3 + u % 2, :]).then_inc(pt_dve, 1)
            if u % 8 == 2 and u > 8:
                head_out(u // 8 - 1)
        head_out(7)
        for kt in range(1, KT, 2):
            v.wait_ge(o_turned, kt + 1)
            v.tensor_copy(OT[:, kt, :], ps[:, kt, :]).then_inc(ot_dve, 1)
        experts(1)

    @block.tensor
    def _(pe):
        def turn_x(s, t):
            pe.wait_ge(xn_ready, TT * s + t + 1)
            for kt in range(KT):
                ins = pe.transpose(ps[:, 2 * t + kt // 4, (kt % 4) * P:(kt % 4 + 1) * P], xnorm[s][:, t, kt:D:KT], ident[:, :])
            ins.then_inc(xn_turned, 1)

        def wait_ht(s, t=TT - 1):
            pe.wait_ge(ht_act, TT * s + t + 1)
            pe.wait_ge(ht_dve, TT * s + t + 1)

        def mod_reduce(n):
            l, q = part_of(n)
            if n:
                pe.wait_ge(mod_done, n)
            pe.wait_ge(acc_ready, n + 1)
            if q in (2, 5):
                for h in range(2):
                    ins = pe.matmul(ps[:, 6 + h, :], ones[:, :], acc[n % 2][:, h * HALF:h * HALF + HALF], start=True, stop=True)
            else:
                for kt in range(KT):
                    ins = pe.matmul(ps[:, 7, kt:kt + 1], acc[n % 2][:, kt:D:KT], ones[:, 0:1], start=True, stop=True)
            ins.then_inc(mod_reduced, 1)

        pe.wait_ge(consts_ready, 1)
        mod_reduce(0)
        for t in range(3):
            turn_x(0, t)
        mod_reduce(1)
        pe.wait_ge(mod_done, 2)
        turn_x(0, 3)
        wait_ht(0)
        pe.wait_ge(params_loaded, 16 * N_PARAMS)
        pe.transpose(ps[:, 7, 64:120], rows[0:56, :], ident[0:56, 0:56]).then_inc(cols_turned, 1)

        def z_tile(t):
            g, j = t // 4, t % 4
            if j == 0:
                wait_slab(pe, ("in", g))
            if 6 <= t < 14:
                pe.wait_ge(z_act, t - 1)
            elif 14 <= t < 18:
                pe.wait_ge(gate_read, LRU_TILES)
            elif t >= 18:
                pe.wait_ge(z_dve, t - 17)
            for kt in range(KT):
                ins = pe.matmul(ps[:, z_bank(t), :], slab(("in", g))[:, kt, j * P:(j + 1) * P], HT[:, kt, :], start=(kt == 0), stop=(kt == KT - 1))
            ins.then_inc(z_ready, 1)

        def gate_products(j):
            pe.wait_ge(z_act, LRU_TILES)
            pe.wait_ge(xr_ready, j + 1)
            if j:
                pe.wait_ge(gate_read, j)
            for d in range(2):
                for w in range(2):
                    ins = pe.matmul(ps[:, 2 * d + w, :], BD[:, (d * 2 + w) * LRU_TILES + j, :], xr[j], start=True, stop=True)
            ins.then_inc(gate_ready, 1)

        pe.wait_ge(bd_loaded, 16 * 8)
        reduce_after = {5: 2, 8: 3, 11: 4, 14: 5, 17: 6}
        for t in range(20):
            z_tile(t)
            if t in (4, 6, 8, 10):
                gate_products((t - 4) // 2)
            if t in reduce_after:
                mod_reduce(reduce_after[t])

        def project(l, t, half):
            lhs, order = ((mixT, (4, 5, 6, 7, 0, 1, 2, 3)), (OT, range(KT)))[l]
            name = (("out", "o")[l], half)
            wait_slab(pe, name)
            for i, kt in enumerate(order):
                ins = pe.matmul(ps[:, 2 * t + half, :], lhs[:, kt, t * P:(t + 1) * P], slab(name)[:, kt, :], start=(i == 0), stop=(i == KT - 1))
            ins.then_inc(y_ready, 1)

        pe.wait_ge(mix_ready, LRU_TILES)
        pe.wait_ge(z_dve, 8)

        def experts(l):
            s = 2 * l + 1
            e0 = l * NE

            def logits(t):
                wait_ht(s, t)
                for kt in range(KT):
                    ins = pe.matmul(ps[:, 0, t * NE:(t + 1) * NE], HT[:, kt, t * P:(t + 1) * P], rw[:, kt, :], start=(kt == 0), stop=(kt == KT - 1))
                ins.then_inc(logit_ready, 1)

            for t in range(TT):
                if l == 0 and t == 3:
                    pe.wait_ge(mod_done, MOD_SPLIT)
                project(l, t, 0)
                if t:
                    turn_x(s, t - 1)
                project(l, t, 1)
                if l == 0 and t == 0:
                    mod_reduce(MOD_SPLIT - 1)
                if t:
                    logits(t - 1)
            turn_x(s, TT - 1)
            logits(TT - 1)
            pe.wait_ge(hot_ready, TT * (l + 1))
            for t in range(TT):
                for t0 in range(t + 1):
                    pe.matmul(ps[:, 1, t * NE:(t + 1) * NE], before[:, :] if t0 == t else ones_b[:, :], hot[:, t0, :], start=(t0 == 0), stop=(t0 == t))
            for t in range(TT):
                ins = pe.matmul(ps[:, 1, TT * NE:(TT + 1) * NE], ones_b[:, :], hot[:, t, :], start=(t == 0), stop=(t == TT - 1))
            ins.then_inc(rank_ready, 1)
            pe.wait_ge(place_ready, l + 1)
            for i in range(2 * TT):
                ins = pe.matmul(ps[:, 2, 0:WIDE], place_hot[:, i, :], block_tok[:, i, :], start=(i == 0), stop=(i == 2 * TT - 1))
            ins.then_inc(slots_summed, 1)

            def turn_xs(buf, done):
                for kt in range(KT):
                    ins = pe.transpose(ps[:, kt // 4, (kt % 4) * P:(kt % 4 + 1) * P], xs[buf][:, kt:D:KT], ident[:, :])
                ins.then_inc(done, 1)

            def product(w, bank, done):
                for kt in range(KT):
                    ins = pe.matmul(ps[:, bank, :], xsT[0][:, kt, :], w[:, kt, :], start=(kt == 0), stop=(kt == KT - 1))
                ins.then_inc(done, 1)

            def split_product(par, c, bank, kts):
                for kt in kts:
                    high, low = xs_high[l][par][:, kt, :], xs_low[par][:, kt, :]
                    w_top, w_rest = w_high[l][c][:, kt, :], w_low(l, c, par)[:, kt, :]
                    for i, (x, w) in enumerate(((high, w_top), (high, w_rest), (low, w_top))):
                        ins = pe.matmul(ps[:, bank, :], x, w, start=(kt == 0 and i == 0), stop=(kt == KT - 1 and i == 2))
                return ins

            def turn_hid(done):
                for f in range(FT):
                    ins = pe.transpose(ps[:, 4, f * P:(f + 1) * P], hid[:, f * P:(f + 1) * P], ident[:, :])
                ins.then_inc(done, 1)

            def down(w, done):
                for h in range(2):
                    for f in range(FT):
                        ins = pe.matmul(ps[:, 5 + h, :], hidT[:, f, :], w[:, 2 * f + h, :], start=(f == 0), stop=(f == FT - 1))
                ins.then_inc(done, 1)

            def turn_hidden(e):
                pe.wait_ge(hid_ready, e + (e0 + 1))
                turn_hid(hid_turned)

            def down_product(e, par, turn, first=False):
                pe.wait_ge(hidt_ready, e + (e0 + 1))
                if not first:
                    pe.wait_ge(yb_ready, e + e0)
                wait_slab(pe, ("exp", l, 2, par), turn)
                down(slab(("exp", l, 2, par)), down_done)

            def step(e, par, turn, first=0, last=False):
                prev_turn = turn if par else turn - 1
                pe.wait_ge(xst_act, e + (e0 + 1))
                pe.wait_ge(xst_dve, e + (e0 + 1))
                if first != 1:
                    pe.wait_ge(silu_done, e + e0)
                pe.wait_ge(low_ready[0], 2 * e + (2 * e0 + 2))
                split_product(par, 0, 2, range(KT // 2))
                if first != 1:
                    turn_hidden(e - 1)
                split_product(par, 0, 2, range(KT // 2, KT)).then_inc(gate_done, 1)
                if first != 1:
                    down_product(e - 1, 1 - par, prev_turn, first == 2)
                if not last:
                    pe.wait_ge(xs_filled[1 - par], (turn + par) * 16 + (16 + (NE // 2) * l * 16))
                    turn_xs(1 - par, xs_turned)
                pe.wait_ge(low_ready[1], 2 * e + (2 * e0 + 2))
                split_product(par, 1, 3, range(KT)).then_inc(up_done, 1)

            pe.wait_ge(xs_filled[0], (NE // 2) * l * 16 + 16)
            turn_xs(0, xs_turned)
            step(0, 0, 0, first=1)
            step(1, 1, 0, first=2)
            with pe.Fori(1, NE // 2 - 1) as i:
                for par in range(2):
                    step(2 * i + par, par, i)
            step(NE - 2, 0, NE // 2 - 1)
            step(NE - 1, 1, NE // 2 - 1, last=True)
            turn_hidden(NE - 1)
            down_product(NE - 1, 1, NE // 2 - 1)

            o = over[l]
            over_slab = [slab(("exp", l, c, 0)) for c in range(3)]
            pe.wait_ge(yb_ready, e0 + NE)
            pe.wait_ge(route_ready, l + 1)
            n_over = pe.value_load(info[0:1, 7:8], min_val=0, max_val=MAX_OVER)
            with pe.Fori(0, MAX_OVER) as k:
                with pe.If(k < n_over):
                    pe.wait_ge(o["xs"], (k + 1) * 16)
                    turn_xs(0, o["turned"])
                    pe.wait_ge(o["xst"], (k + 1) * 2)
                    pe.wait_ge(o["wg"], (k + 1) * 16)
                    product(over_slab[0], 2, o["gate"])
                    pe.wait_ge(o["wu"], (k + 1) * 16)
                    product(over_slab[1], 3, o["gu"])
                    pe.wait_ge(o["hid"], k + 1)
                    turn_hid(o["hidt_in"])
                    pe.wait_ge(o["hidt"], k + 1)
                    pe.wait_ge(o["wd"], (k + 1) * 16)
                    pe.wait_ge(o["stored"], (k + 1) * 16)
                    down(over_slab[2], o["down"])

        experts(0)
        turn_x(2, 0)
        turn_x(2, 1)
        reduce_after_slab = {1: 8, 3: 9, 4: 10, 5: 11}
        for w in range(6):
            for chunk in range(2):
                pe.wait_ge(qkv_low, 2 * w + chunk + 1)
                _, top, rest = qkv_split_of(w, chunk)
                for t in range(TT):
                    i = 4 * w + t
                    cut = slice(t * P, (t + 1) * P)
                    if w == 0 and chunk == 0:
                        pe.wait_ge(ht_dve, TT * 2 + t + 1)
                    if i >= 6 and chunk == 0:
                        pe.wait_ge(qkv_dve if t % 2 else qkv_act, (i - 6) // 2 + 1)
                    for k in range(KT // 2):
                        kt = chunk * KT // 2 + k
                        for n, (x, y) in enumerate(((ht_high, top), (ht_high, rest), (HT_r, top))):
                            ins = pe.matmul(ps[:, i % 6, :], x[:, kt, cut], y[:, k, :], start=(kt == 0 and n == 0), stop=(kt == KT - 1 and n == 2))
                    if chunk == 1:
                        ins.then_inc(qkv_ready, 1)
                    elif t == TT - 1:
                        ins.then_inc(qkv_chunk, 1)
                    if w == 0 and chunk == 0 and t + 2 < TT:
                        turn_x(2, t + 2)
            if w in reduce_after_slab:
                mod_reduce(reduce_after_slab[w])
        pe.wait_ge(mod_done, LAYERS * PARTS)
        pe.wait_ge(qkv_act, 12)
        pe.wait_ge(qkv_dve, 12)
        pe.wait_ge(rot_ready, 2)
        for hp in range(8):
            if hp >= 4:
                pe.wait_ge(qt_ready, hp - 3)
            for t in range(TT):
                ins = pe.transpose(ps[:, (2 * hp) % 8, t * P:(t + 1) * P], Q[:, t, hp * P:(hp + 1) * P], ident[:, :])
            ins.then_inc(qt_turned, 1)
            if hp >= 4:
                pe.wait_ge(kt_ready, hp - 3)
            for t in range(TT):
                ins = pe.transpose(ps[:, (2 * hp + 1) % 8, t * P:(t + 1) * P], K[:, t, hp * P:(hp + 1) * P], ident[:, :])
            ins.then_inc(kt_turned, 1)

        def scores(n):
            hp, it, par = n // 8, (n // 2) % TT, n % 2
            if n >= 3:
                pe.wait_ge(max_ready, n - 2)
            r0 = HD * par
            pe.matmul(ps[:, n % 3, :], QT[r0:r0 + HD, hp, it * P:(it + 1) * P], KTR[r0:r0 + HD, hp, :], start=True, stop=True).then_inc(s_ready, 1)

        def weigh(n):
            hp, it, par = n // 8, (n // 2) % TT, n % 2
            pe.wait_ge(pt_act if n % 2 == 0 else pt_dve, n // 2 + 1)
            if n % 8 == 0 and hp >= 2:
                pe.wait_ge(o_ready, hp - 1)
            dest = ps[:, 5 + hp % 2, (n % 8) * HD:(n % 8 + 1) * HD]
            h = 2 * hp + par
            for jt in range(TT):
                ins = pe.matmul(dest, probT[n % 4][:, jt * P:(jt + 1) * P], V[:, jt, h * HD:(h + 1) * HD], start=(jt == 0), stop=(jt == TT - 1))
            ins.then_inc(av_ready, 1)

        pe.wait_ge(qt_ready, 8)
        pe.wait_ge(kt_ready, 8)
        scores(0)
        scores(1)
        for u in range(64):
            if u + 2 < 64:
                scores(u + 2)
            pe.wait_ge(p_ready, u + 1)
            if u >= 2:
                pe.wait_ge(pt_act if u % 2 == 0 else pt_dve, u // 2)
            for jt in range(TT):
                ins = pe.transpose(ps[:, 3 + u % 2, jt * P:(jt + 1) * P], prob[u % 4][:, jt * P:(jt + 1) * P], ident[:, :])
            ins.then_inc(p_turned, 1)
            if u >= 1:
                weigh(u - 1)
        weigh(63)
        pe.wait_ge(o_ready, 8)
        for kt in range(KT):
            for t in range(TT):
                ins = pe.transpose(ps[:, kt, t * P:(t + 1) * P], O[:, t, kt * P:(kt + 1) * P], ident[:, :])
            ins.then_inc(o_turned, 1)
        pe.wait_ge(ot_act, 4)
        pe.wait_ge(ot_dve, 4)
        experts(1)


_INS = ["x", "c", "positions", "mod_w", "mod_b", "norm_mix_g", "norm_ffn_g", "final_norm_g", "w_in_ab", "conv_a_w",
        "conv_b_w", "conv_b_b", "lru_wa", "lru_ba", "lru_wx", "lru_bx", "lru_lambda", "w_out_ab", "w_qkv", "w_o",
        "router_w", "router_bias", "expert_w_gate", "expert_w_up", "expert_w_down"]


def kernel(**inputs):
    import concourse.bacc as _bacc
    from concourse.bass_utils import run_bass_kernel_spmd as _run

    nc = _bacc.Bacc("TRN2", target_bir_lowering=False, num_devices=1, dynamic_dma_scratch_size=4096)
    arrays, args = {}, {}
    for name in _INS:
        arr = np.ascontiguousarray(inputs[name])
        arrays[f"in_{name}_dram"] = arr
        args[name] = nc.dram_tensor(f"in_{name}_dram", arr.shape, mybir.dt.from_np(arr.dtype), kind="ExternalInput").ap()
    out = nc.dram_tensor("out_dram", (1, S, D), F32, kind="ExternalOutput").ap()
    trunk(nc, args, out)
    r = _run(nc, [arrays], core_ids=[0])
    return r.results[0]["out_dram"]
```
